# Optimizing a Trainium2 kernel written in Bass

```python
import math
import jax, jax.numpy as jnp
from jax import lax
import numpy as np

D_MODEL = 1024
BATCH = 1
SEQ = 256
DEPTH = 1

GRID_W = 64
SSM_HEADS = 16
SSM_HEAD_DIM = 64
SSM_INNER = SSM_HEADS * SSM_HEAD_DIM
SSM_GROUPS = 2
SSM_STATE = 128
SSM_CONV = 5
SSM_CHUNK = 128
CONV_CH = SSM_INNER + 2 * SSM_GROUPS * SSM_STATE
ATTN_HEADS = 8
ATTN_KV_HEADS = 2
ATTN_HEAD_DIM = 128
ATTN_Q_WIDTH = ATTN_HEADS * ATTN_HEAD_DIM
ATTN_KV_WIDTH = ATTN_KV_HEADS * ATTN_HEAD_DIM
ATTN_Q_BLOCK = 128
ROPE_THETA = 10000.0
ROPE_AXIS_DIM = ATTN_HEAD_DIM // 2
N_BRANCHES = 2
Z_END = SSM_INNER
XBC_END = Z_END + CONV_CH
DTF_END = XBC_END + SSM_HEADS
DTB_END = DTF_END + SSM_HEADS
Q_END = DTB_END + ATTN_Q_WIDTH
K_END = Q_END + ATTN_KV_WIDTH
V_END = K_END + ATTN_KV_WIDTH
IN_COLS = V_END + N_BRANCHES * D_MODEL
SPLITS = [Z_END, XBC_END, DTF_END, DTB_END, Q_END, K_END, V_END]
N_EXPERTS = 32
TOP_K = 4
D_EXPERT = D_MODEL
SWIGLU_LIMIT = 7.0
SWIGLU_ALPHA = 1.702
MOE_BLOCK = 128
NORM_EPS = 1e-6

kernel_name = "hybrid_ssd_axial_gqa_moe_encoder"

def rmsnorm(x, g):
    xf = x.astype(jnp.float32)
    y = xf * lax.rsqrt(jnp.mean(xf * xf, axis=-1, keepdims=True) + NORM_EPS)
    return y.astype(x.dtype) * g

def depthwise_conv(u, w, b):
    pad = (SSM_CONV - 1) // 2
    y = lax.conv_general_dilated(u, w[:, None, :], window_strides=(1,),
                                 padding=[(pad, SSM_CONV - 1 - pad)],
                                 dimension_numbers=('NWC', 'WIO', 'NWC'),
                                 feature_group_count=u.shape[-1])
    return y + b

def ssd_scan(x, dt, A, Bm, Cm):
    b, l, h, p = x.shape
    g, n = Bm.shape[-2:]
    hg = h // g
    c = l // SSM_CHUNK
    L = SSM_CHUNK
    xr = (x * dt[..., None].astype(x.dtype)).reshape(b, c, L, g, hg, p)
    a = (dt * A.astype(jnp.float32)).reshape(b, c, L, g, hg)
    a_cs = jnp.cumsum(a, axis=2)
    Br = Bm.reshape(b, c, L, g, n)
    Cr = Cm.reshape(b, c, L, g, n)
    seg = a_cs[:, :, :, None] - a_cs[:, :, None, :]
    mask = jnp.tril(jnp.ones((L, L), dtype=bool))[:, :, None, None]
    lmat = jnp.exp(jnp.where(mask, seg, -jnp.inf))
    cb = jnp.einsum('bclgn,bcsgn->bclsg', Cr, Br)
    y_diag = jnp.einsum('bclsgh,bcsghp->bclghp', cb[..., None] * lmat, xr)
    decay_to_end = jnp.exp(a_cs[:, :, -1:] - a_cs)
    states = jnp.einsum('bclgn,bclghp->bcghpn', Br, xr * decay_to_end[..., None])
    chunk_decay = jnp.exp(a_cs[:, :, -1])

    def step(carry, inp):
        st, dec = inp
        return carry * dec[..., None, None] + st, carry

    init = jnp.zeros((b, g, hg, p, n), states.dtype)
    _, prev = lax.scan(step, init, (jnp.moveaxis(states, 1, 0), jnp.moveaxis(chunk_decay, 1, 0)))
    prev = jnp.moveaxis(prev, 0, 1)
    y_off = jnp.einsum('bclgn,bcghpn->bclghp', Cr, prev) * jnp.exp(a_cs)[..., None]
    return (y_diag + y_off).reshape(b, l, h, p).astype(x.dtype)

def rope_axis(part, ang):
    m = ang.shape[-1]
    cos = jnp.cos(ang)[None, :, None, :].astype(part.dtype)
    sin = jnp.sin(ang)[None, :, None, :].astype(part.dtype)
    p1, p2 = part[..., :m], part[..., m:]
    return jnp.concatenate([p1 * cos - p2 * sin, p2 * cos + p1 * sin], axis=-1)

def axial_rope(t, row, col):
    inv_freq = ROPE_THETA ** (-jnp.arange(0, ROPE_AXIS_DIM, 2, dtype=jnp.float32) / ROPE_AXIS_DIM)
    ang_r = row.astype(jnp.float32)[:, None] * inv_freq
    ang_c = col.astype(jnp.float32)[:, None] * inv_freq
    return jnp.concatenate([rope_axis(t[..., :ROPE_AXIS_DIM], ang_r),
                            rope_axis(t[..., ROPE_AXIS_DIM:], ang_c)], axis=-1)

def blocked_attention(q, k, v):
    b, s, hq, d = q.shape
    hkv = k.shape[2]
    grp = hq // hkv
    nb = s // ATTN_Q_BLOCK
    qb = q.reshape(b, nb, ATTN_Q_BLOCK, hkv, grp, d).transpose(1, 0, 2, 3, 4, 5)
    scale = d ** -0.5

    def one_block(qblk):
        sc = jnp.einsum('bqkgd,bskd->bkgqs', qblk, k).astype(jnp.float32) * scale
        pr = jax.nn.softmax(sc, axis=-1).astype(v.dtype)
        return jnp.einsum('bkgqs,bskd->bqkgd', pr, v)

    o = lax.map(one_block, qb)
    return o.transpose(1, 0, 2, 3, 4, 5).reshape(b, s, hq * d)

def token_mixer(h, w_in, conv_w, conv_b, dt_bias_f, dt_bias_b, a_log_f, a_log_b, d_skip,
                g_ssm, q_norm_g, k_norm_g, w_br_ssm, w_br_attn, w_out):
    b, s, _ = h.shape
    proj = h @ w_in
    z, xbc, dt_f, dt_b, q, k, v, gates = jnp.split(proj, SPLITS, axis=-1)

    xbc = jax.nn.silu(depthwise_conv(xbc, conv_w, conv_b))
    xs, Bm, Cm = jnp.split(xbc, [SSM_INNER, SSM_INNER + SSM_GROUPS * SSM_STATE], axis=-1)
    xs = xs.reshape(b, s, SSM_HEADS, SSM_HEAD_DIM)
    Bm = Bm.reshape(b, s, SSM_GROUPS, SSM_STATE)
    Cm = Cm.reshape(b, s, SSM_GROUPS, SSM_STATE)
    dtf = jax.nn.softplus((dt_f + dt_bias_f).astype(jnp.float32))
    dtb = jax.nn.softplus((dt_b + dt_bias_b).astype(jnp.float32))
    flip = lambda t: jnp.flip(t, axis=1)
    y_f = ssd_scan(xs, dtf, -jnp.exp(a_log_f.astype(jnp.float32)), Bm, Cm)
    y_b = flip(ssd_scan(flip(xs), flip(dtb), -jnp.exp(a_log_b.astype(jnp.float32)), flip(Bm), flip(Cm)))
    y = (y_f + y_b + xs * d_skip[:, None]).reshape(b, s, SSM_INNER)
    y = rmsnorm(y * jax.nn.silu(z), g_ssm)
    br_ssm = y @ w_br_ssm

    q = rmsnorm(q.reshape(b, s, ATTN_HEADS, ATTN_HEAD_DIM), q_norm_g)
    k = rmsnorm(k.reshape(b, s, ATTN_KV_HEADS, ATTN_HEAD_DIM), k_norm_g)
    v = v.reshape(b, s, ATTN_KV_HEADS, ATTN_HEAD_DIM)
    rows = s // GRID_W
    row = jnp.repeat(jnp.arange(rows, dtype=jnp.int32), GRID_W)
    col = jnp.tile(jnp.arange(GRID_W, dtype=jnp.int32), rows)
    q = axial_rope(q, row, col)
    k = axial_rope(k, row, col)
    br_attn = blocked_attention(q, k, v) @ w_br_attn

    g_s, g_a = jnp.split(jax.nn.sigmoid(gates), N_BRANCHES, axis=-1)
    return (g_s * br_ssm + g_a * br_attn) @ w_out

def moe_ffn(h, w_router, b_router, w_mlp1, b_mlp1, w_mlp2, b_mlp2):
    b, s, d = h.shape
    n = b * s
    hf = h.reshape(n, d)
    logits = (hf @ w_router + b_router).astype(jnp.float32)
    top_val, top_idx = lax.top_k(logits, TOP_K)
    top_w = jax.nn.softmax(top_val, axis=-1).astype(h.dtype)
    n_assign = n * TOP_K
    flat_e = top_idx.reshape(-1).astype(jnp.int32)
    flat_tok = jnp.arange(n_assign, dtype=jnp.int32) // TOP_K
    flat_w = top_w.reshape(-1)
    order = jnp.argsort(flat_e)
    sorted_e = flat_e[order]
    counts = jnp.bincount(flat_e, length=N_EXPERTS).astype(jnp.int32)
    padded = (counts + MOE_BLOCK - 1) // MOE_BLOCK * MOE_BLOCK
    start = jnp.cumsum(counts) - counts
    pad_end = jnp.cumsum(padded)
    pad_start = pad_end - padded
    dest = pad_start[sorted_e] + jnp.arange(n_assign, dtype=jnp.int32) - start[sorted_e]
    n_blocks = -(-n_assign // MOE_BLOCK) + N_EXPERTS
    n_rows = n_blocks * MOE_BLOCK
    row_tok = jnp.zeros((n_rows,), jnp.int32).at[dest].set(flat_tok[order])
    row_w = jnp.zeros((n_rows,), h.dtype).at[dest].set(flat_w[order])
    block_e = jnp.minimum(jnp.searchsorted(pad_end, jnp.arange(n_blocks, dtype=jnp.int32) * MOE_BLOCK,
                                           side='right'), N_EXPERTS - 1)
    xb = hf[row_tok].reshape(n_blocks, MOE_BLOCK, d)

    def expert_block(args):
        xblk, e = args
        hm = xblk @ w_mlp1[e] + b_mlp1[e]
        gate, up = hm[:, :D_EXPERT], hm[:, D_EXPERT:]
        gate = jnp.minimum(gate, SWIGLU_LIMIT)
        up = jnp.clip(up, -SWIGLU_LIMIT, SWIGLU_LIMIT)
        act = gate * jax.nn.sigmoid(SWIGLU_ALPHA * gate) * (up + 1)
        return act @ w_mlp2[e] + b_mlp2[e]

    yb = lax.map(expert_block, (xb, block_e)).reshape(n_rows, d)
    y = jax.ops.segment_sum(yb * row_w[:, None], row_tok, num_segments=n)
    return y.reshape(b, s, d)

def setup_inputs(seed: int = 0) -> dict:
    key = jax.random.key(seed)
    ks = jax.random.split(key, 26)
    nrm = lambda k, shape, sc: jax.random.normal(k, shape, jnp.float32) * sc
    lo, hi = math.log(0.001), math.log(0.1)
    dt_f = jnp.exp(jax.random.uniform(ks[5], (DEPTH, SSM_HEADS)) * (hi - lo) + lo)
    dt_b = jnp.exp(jax.random.uniform(ks[6], (DEPTH, SSM_HEADS)) * (hi - lo) + lo)
    return {
        "x": nrm(ks[0], (BATCH, SEQ, D_MODEL), 1.0),
        "g_mix": 1.0 + nrm(ks[1], (DEPTH, D_MODEL), 0.02),
        "w_in": nrm(ks[2], (DEPTH, D_MODEL, IN_COLS), D_MODEL ** -0.5),
        "conv_w": nrm(ks[3], (DEPTH, SSM_CONV, CONV_CH), SSM_CONV ** -0.5),
        "conv_b": nrm(ks[4], (DEPTH, CONV_CH), 0.02),
        "dt_bias_f": dt_f + jnp.log(-jnp.expm1(-dt_f)),
        "dt_bias_b": dt_b + jnp.log(-jnp.expm1(-dt_b)),
        "a_log_f": jnp.log(jax.random.uniform(ks[7], (DEPTH, SSM_HEADS), minval=1.0, maxval=16.0)),
        "a_log_b": jnp.log(jax.random.uniform(ks[8], (DEPTH, SSM_HEADS), minval=1.0, maxval=16.0)),
        "d_skip": 1.0 + nrm(ks[9], (DEPTH, SSM_HEADS), 0.02),
        "g_ssm": 1.0 + nrm(ks[10], (DEPTH, SSM_INNER), 0.02),
        "q_norm_g": 1.0 + nrm(ks[11], (DEPTH, ATTN_HEAD_DIM), 0.02),
        "k_norm_g": 1.0 + nrm(ks[12], (DEPTH, ATTN_HEAD_DIM), 0.02),
        "w_br_ssm": nrm(ks[13], (DEPTH, SSM_INNER, D_MODEL), SSM_INNER ** -0.5),
        "w_br_attn": nrm(ks[14], (DEPTH, ATTN_Q_WIDTH, D_MODEL), ATTN_Q_WIDTH ** -0.5),
        "w_out": nrm(ks[15], (DEPTH, D_MODEL, D_MODEL), D_MODEL ** -0.5),
        "g_ffn": 1.0 + nrm(ks[16], (DEPTH, D_MODEL), 0.02),
        "w_router": nrm(ks[17], (DEPTH, D_MODEL, N_EXPERTS), D_MODEL ** -0.5),
        "b_router": nrm(ks[18], (DEPTH, N_EXPERTS), 0.01),
        "w_mlp1": nrm(ks[19], (DEPTH, N_EXPERTS, D_MODEL, 2 * D_EXPERT), D_MODEL ** -0.5),
        "b_mlp1": nrm(ks[20], (DEPTH, N_EXPERTS, 2 * D_EXPERT), 0.02),
        "w_mlp2": nrm(ks[21], (DEPTH, N_EXPERTS, D_EXPERT, D_MODEL), D_EXPERT ** -0.5),
        "b_mlp2": nrm(ks[22], (DEPTH, N_EXPERTS, D_MODEL), 0.02),
        "g_final": 1.0 + nrm(ks[23], (D_MODEL,), 0.02),
    }

def reference(x, g_mix, w_in, conv_w, conv_b, dt_bias_f, dt_bias_b, a_log_f, a_log_b, d_skip,
              g_ssm, q_norm_g, k_norm_g, w_br_ssm, w_br_attn, w_out, g_ffn, w_router, b_router,
              w_mlp1, b_mlp1, w_mlp2, b_mlp2, g_final):
    for l in range(DEPTH):
        x = x + token_mixer(rmsnorm(x, g_mix[l]), w_in[l], conv_w[l], conv_b[l],
                            dt_bias_f[l], dt_bias_b[l], a_log_f[l], a_log_b[l], d_skip[l],
                            g_ssm[l], q_norm_g[l], k_norm_g[l], w_br_ssm[l], w_br_attn[l], w_out[l])
        x = x + moe_ffn(rmsnorm(x, g_ffn[l]), w_router[l], b_router[l],
                        w_mlp1[l], b_mlp1[l], w_mlp2[l], b_mlp2[l])
    return rmsnorm(x, g_final)


_drawn_inputs = setup_inputs


def setup_inputs(seed=0):
    import zlib

    import numpy as np

    out = dict(_drawn_inputs(seed))
    spreads = {}
    factors = {'d_skip': 12.164,
     'q_norm_g': 8.0,
     'k_norm_g': 5.779,
     'b_mlp1': 5.627,
     'b_mlp2': 6.452,
     'g_final': 8.465,
     'b_router': 2.703}
    for name, (base, spread) in spreads.items():
        noise = np.random.default_rng([zlib.crc32(name.encode()), seed]).standard_normal(out[name].shape)
        drawn = base * np.exp(spread * noise) if base else spread * noise
        out[name] = __import__('jax').numpy.asarray(drawn.astype(out[name].dtype))
    for name, factor in factors.items():
        out[name] = (out[name] * factor).astype(out[name].dtype)
    return out
```

```python
import concourse.bass as bass
from concourse import mybir
from contextlib import ExitStack

F32 = mybir.dt.float32
I32 = mybir.dt.int32
ALU = mybir.AluOpType
ACT = mybir.ActivationFunctionType
AXX = mybir.AxisListType.X

P = 128
D = 1024
SEQ = 256
TT = SEQ // P
KD = D // P
NH = 16
HD = 64
NST = 128
CONV = 5
PAD = (CONV - 1) // 2
XBC_TILES = (D + 2 * 2 * NST) // P
AH = 8
KVH = 2
AD = 128
XBC0 = D
DT0 = XBC0 + XBC_TILES * P
Q0 = DT0 + 2 * NH
G0 = Q0 + AH * AD + 2 * KVH * AD
NE = 32
TOPK = 4
DE = D
LIMIT = 7.0
ALPHA = 1.702
EPS = 1e-6
CAP = 64
NPASS = SEQ // CAP
NEG = -1e30

UW = 256
UNIT = KD * UW
RING_MIX = 10
RING = 16
EXP_UNITS = 12
BODY = 4

U_XBC, U_Z, U_K, U_Q, U_V, U_G, U_BA, U_BS, U_O = 0, 6, 10, 11, 15, 16, 24, 28, 32
N_MIX = 36

R_GMIX, R_GSSM, R_GFFN, R_CB, R_CW = 0, 8, 16, 24, 36
N_ROWS = R_CW + CONV * XBC_TILES
C_ID, C_LE, C_GE, C_ONE, C_NEGF, C_ZERO, C_NEGB = (P * i for i in range(7))
C_IOTA = 7 * P
C_COS = C_IOTA + CAP
C_SIN = C_COS + TT * AD
N_CONST = C_SIN + TT * AD


def shape_constants():
    import numpy as np
    r = np.arange(P)
    c = np.zeros((P, N_CONST), np.float32)
    c[:, C_ID:C_ID + P] = r[:, None] == r[None, :]
    c[:, C_LE:C_LE + P] = r[:, None] <= r[None, :]
    c[:, C_GE:C_GE + P] = r[:, None] >= r[None, :]
    c[:, C_ONE:C_ONE + P] = 1.0
    c[:, C_NEGF:C_NEGF + P] = np.where(r[:, None] > r[None, :], NEG, 0.0)
    c[:, C_NEGB:C_NEGB + P] = np.where(r[:, None] < r[None, :], NEG, 0.0)
    c[:, C_IOTA:C_IOTA + CAP] = np.arange(CAP)[None, :]
    half = AD // 4
    inv = np.float32(10000.0) ** (-np.arange(0, AD // 2, 2, dtype=np.float32) / np.float32(AD // 2))
    tok = np.arange(SEQ)
    for axis, pos in enumerate((tok // 64, tok % 64)):
        ang = (pos.astype(np.float32)[:, None] * inv).astype(np.float32)
        cos, sin = np.cos(ang).astype(np.float32), np.sin(ang).astype(np.float32)
        for t in range(TT):
            for h, sign in ((0, -1.0), (1, 1.0)):
                o = t * AD + axis * 2 * half + h * half
                c[:, C_COS + o:C_COS + o + half] = cos[t * P:(t + 1) * P]
                c[:, C_SIN + o:C_SIN + o + half] = sign * sin[t * P:(t + 1) * P]
    return c


def encoder_layer(nc, x, g_mix, w_in, conv_w, conv_b, dt_bias_f, dt_bias_b, a_log_f, a_log_b, d_skip,
                  g_ssm, q_norm_g, k_norm_g, w_br_ssm, w_br_attn, w_out, g_ffn, w_router, b_router,
                  w_mlp1, b_mlp1, w_mlp2, b_mlp2, g_final, consts, out):
    with ExitStack() as ctx:
        def sb(name, shape, dt=F32):
            return ctx.enter_context(nc.sbuf_tensor(name, shape, dt))

        def sem(name):
            return ctx.enter_context(nc.semaphore(name))

        bank = [ctx.enter_context(nc.psum_tensor(f"bank{i}", [P, 512], F32)) for i in range(8)]

        ring = sb("ring", [P, RING, UNIT])
        over = ring[:, RING_MIX:RING, :].rearrange("p a b -> p (a b)")
        sig = over[:, 0:4096].rearrange("p (m l) -> p m l", m=16)
        roped = over[:, 0:2560].rearrange("p (t n) -> p t n", t=TT)
        xbcT = over[:, 4096:7168].rearrange("p (m l) -> p m l", m=XBC_TILES)
        siluz = over[:, 7168:9216].rearrange("p (m l) -> p m l", m=KD)
        b1raw = over[0:NE, 7168:9216]
        qk = over[:, 9216:11776].rearrange("p (t n) -> p t n", t=TT)
        kT = over[:, 11776:12288].rearrange("p (h l) -> p h l", h=KVH)

        xres = sb("xres", [P, TT, D])
        hN = sb("hN", [P, TT, D])
        hT = sb("hT", [P, KD, SEQ])
        cst = sb("cst", [P, N_CONST])
        prm = sb("prm", [P, P])
        prmT = sb("prmT", [P, N_ROWS + 8])
        dskr = sb("dskr", [8, 2])
        dske = sb("dske", [8, P])
        b1T = sb("b1T", [P, NE, 16])
        wr = sb("wr", [P, KD, NE])
        wdt = sb("wdt", [P, KD, 2 * NH])
        vec = sb("vec", [P, 2 * NH + 2 * NH + NE + 2 * AD])
        dtb_b, alog_b, brt_b = vec[:, 0:32], vec[:, 32:64], vec[:, 64:96]
        kg_b, qg_b = vec[:, 96:224], vec[:, 224:352]
        stat = sb("stat", [P, 64])
        dtv = sb("dtv", [P, TT, 32])
        dta = sb("dta", [P, TT, 32])
        dtu = sb("dtu", [P, TT, 32])
        acsN = sb("acsN", [P, TT, 32])
        nacs = sb("nacs", [P, TT, 32])
        acsT = sb("acsT", [32, SEQ])

        arena = sb("arena", [P, 10000])
        vN = arena[:, 0:512].rearrange("p (t n) -> p t n", t=TT)
        qT = arena[:, 512:2560].rearrange("p (h l) -> p h l", h=AH)
        cb = arena[:, 2560:3584].rearrange("p (g i l) -> p g i l", g=2, i=TT)
        ebuf = arena[:, 3584:5120].rearrange("p (h l) -> p h l", h=2)
        gbuf = arena[:, 5120:7168].rearrange("p (b h i l) -> p b h i l", b=2, h=2, i=TT)
        prob = arena[:, 7168:7680].rearrange("p (t s) -> p t s", t=TT)
        probT = arena[:, 7680:8192].rearrange("p (i q) -> p i q", i=TT)
        ropeb = arena[:, 3584:4096].rearrange("p (t n) -> p t n", t=TT)
        xp = arena[:, 8192:9232].rearrange("p (b m l) -> p b m l", b=2, m=2)
        sqacc = arena[:, 9232:9488]
        sqb = arena[:, 9488:9744]
        rB = arena[:, 9744:10000]
        slotP = arena[:, 0:256].rearrange("p (b t s) -> p b t s", b=2, t=TT)
        slotW = arena[:, 256:768].rearrange("p (b t e s) -> p b t e s", b=2, t=TT, e=2)
        xT = arena[:, 768:1792].rearrange("p (b k s) -> p b k s", b=2, k=KD)
        ga = arena[:, 1792:2304]
        ub = arena[:, 2304:2816]
        sg = arena[:, 2816:3328]
        actT = arena[:, 3328:4352].rearrange("p (b k s) -> p b k s", b=2, k=KD)
        yTs = arena[:, 4352:5376].rearrange("p (k e s) -> p k e s", k=KD, e=2)
        ys = arena[:, 5376:6400]
        slotWT = arena[:, 7696:7952]
        gfin = arena[:, 6400:7424]
        b2s = arena[0:NE, 5376:6400]
        wT = arena[0:NE, 7952:8208]
        msk = arena[:, 7424:7488].rearrange("p (t e) -> p t e", t=TT)
        lgt = arena[:, 7488:7552].rearrange("p (t e) -> p t e", t=TT)
        top8 = arena[:, 7552:7568].rearrange("p (t e) -> p t e", t=TT)
        eqm = arena[:, 7568:7632].rearrange("p (t e) -> p t e", t=TT)
        eqc = arena[:, 7632:7696].rearrange("p (t e) -> p t e", t=TT)
        rankm = sb("rankm", [P, TT, NE + 1])
        wtok = sb("wtok", [P, TT, NE + 1])
        cnt = sb("cnt", [P, 2])
        over_i = sb("over_i", [P, 1], I32)

        ident = cst[:, C_ID:C_ID + P]
        m_le = cst[:, C_LE:C_LE + P]
        m_ge = cst[:, C_GE:C_GE + P]
        ones = cst[:, C_ONE:C_ONE + P]
        iota = cst[:, C_IOTA:C_IOTA + CAP]

        slot_full = [sem(f"slot_full{i}") for i in range(RING)]
        unit_done = sem("unit_done")
        c_in = sem("c_in"); x_in = sem("x_in"); row_in = sem("row_in"); b1_in = sem("b1_in")
        vec_in = sem("vec_in"); dsk_in = sem("dsk_in"); wdt_in = sem("wdt_in"); late_in = sem("late_in")
        gfin_in = sem("gfin_in"); out_done = sem("out_done")
        act_step = sem("act_step"); dve_step = sem("dve_step"); pool_step = sem("pool_step")
        moe_dve_step = sem("moe_dve_step")
        dsk_ready = sem("dsk_ready"); prm_ready = sem("prm_ready"); prm_taken = sem("prm_taken")
        xsq_ready = sem("xsq_ready"); xr_ready = sem("xr_ready"); h_ready = sem("h_ready")
        hT_psum = sem("hT_psum"); hT_ready = sem("hT_ready")
        unit_taken = sem("unit_taken")
        xp_ready = sem("xp_ready"); conv_done = sem("conv_done"); silu_done = sem("silu_done")
        dt_psum = sem("dt_psum"); dt_in = sem("dt_in"); dt_exp = sem("dt_exp"); a_ready = sem("a_ready")
        acs_psum = sem("acs_psum"); acsN_ready = sem("acsN_ready"); acsT_psum = sem("acsT_psum")
        acsT_ready = sem("acsT_ready")
        xN_psum = sem("xN_psum"); xN_ready = sem("xN_ready"); cb_psum = sem("cb_psum"); cb_ready = sem("cb_ready")
        qsq_ready = sem("qsq_ready"); qr_ready = sem("qr_ready"); roped_ready = sem("roped_ready")
        qT_psum = sem("qT_psum"); qT_ready = sem("qT_ready")
        seg_psum = sem("seg_psum"); seg_masked = sem("seg_masked"); seg_exp = sem("seg_exp"); g_ready = sem("g_ready")
        sc_psum = sem("sc_psum"); sc_max = sem("sc_max"); sc_exp = sem("sc_exp"); prob_ready = sem("prob_ready")
        probT_psum = sem("probT_psum"); probT_ready = sem("probT_ready")
        o_psum = sem("o_psum"); o_ready = sem("o_ready")
        y_psum = sem("y_psum"); yz_ready = sem("yz_ready"); ysq_ready = sem("ysq_ready"); ysq_added = sem("ysq_added")
        yg_ready = sem("yg_ready")
        gate_ready = sem("gate_ready")
        ssq_psum = sem("ssq_psum"); ssq_ready = sem("ssq_ready"); rB_ready = sem("rB_ready")
        mix_ready = sem("mix_ready"); x1sq_ready = sem("x1sq_ready")
        x1r_ready = sem("x1r_ready"); h2_ready = sem("h2_ready"); h2T_psum = sem("h2T_psum"); h2T_ready = sem("h2T_ready")
        lg_psum = sem("lg_psum"); lmax_ready = sem("lmax_ready"); lexp_ready = sem("lexp_ready")
        w_ready = sem("w_ready"); wT_psum = sem("wT_psum"); wT_ready = sem("wT_ready")
        b2_psum = sem("b2_psum"); route_ready = sem("route_ready")
        p_ready = sem("p_ready"); x_psum = sem("x_psum"); xT_ready = sem("xT_ready")
        ga_ready = sem("ga_ready"); sg_ready = sem("sg_ready"); actT_ready = sem("actT_ready")
        yTs_ready = sem("yTs_ready"); pw_psum = sem("pw_psum"); pw_ready = sem("pw_ready")
        yt_psum = sem("yt_psum"); ys_ready = sem("ys_ready"); c_psum = sem("c_psum"); c_added = sem("c_added")
        fsq_ready = sem("fsq_ready"); fr_ready = sem("fr_ready"); fin_ready = sem("fin_ready")

        def mix_slot(n):
            return n % RING_MIX

        def moe_slot(j):
            return (j + N_MIX) % RING_MIX if j < RING_MIX else j

        def mix_full(eng, n):
            eng.wait_ge(slot_full[mix_slot(n)], 16 * (n // RING_MIX + 1))

        def mix_loads(s):
            return len([n for n in range(N_MIX) if mix_slot(n) == s])

        def moe_full(eng, i, u):
            s = moe_slot(u % RING)
            eng.wait_ge(slot_full[s], 16 * (mix_loads(s) + u // RING + 1) + i * (16 * BODY * EXP_UNITS // RING))

        def cols(w, c0):
            return w.rearrange("(k p) n -> p k n", p=P)[:, :, c0:c0 + UW]

        def mix_src(n):
            if n < U_Z:
                return cols(w_in[0], XBC0 + n * UW)
            if n < U_K:
                return cols(w_in[0], (n - U_Z) * UW)
            if n == U_K:
                return cols(w_in[0], Q0 + AH * AD)
            if n < U_V:
                return cols(w_in[0], Q0 + (n - U_Q) * UW)
            if n == U_V:
                return cols(w_in[0], Q0 + AH * AD + KVH * AD)
            if n < U_BA:
                return cols(w_in[0], G0 + (n - U_G) * UW)
            if n < U_BS:
                return cols(w_br_attn[0], (n - U_BA) * UW)
            if n < U_O:
                return cols(w_br_ssm[0], (n - U_BS) * UW)
            return cols(w_out[0], (n - U_O) * UW)

        w1v = w_mlp1[0].rearrange("e (k p) n -> e p k n", p=P)
        w2v = w_mlp2[0].rearrange("e (k p) n -> e p k n", p=P)

        def k_view(s):
            return ring[:, s, :].rearrange("p (k n) -> p k n", k=KD)

        def chain(eng, semaphore, base=0):
            n = [0]

            def link(ins):
                n[0] += 1
                ins.then_inc(semaphore, 1)
                eng.wait_ge(semaphore, base + n[0])
            link.count = n
            return link

        block = ctx.enter_context(nc.Block())

        @block.sync
        def _(sp):
            def load_moe(i, u):
                e = i * BODY + u // EXP_UNITS
                q = u % EXP_UNITS
                s = moe_slot(u % RING)
                if q < KD:
                    src = w1v[bass.ds(e, 1), :, q, :].rearrange("a p n -> (a p) n")
                else:
                    k = 2 * (q - KD)
                    src = w2v[bass.ds(e, 1), :, k:k + 2, :].rearrange("a p k n -> (a p) k n")
                dst = ring[:, s, :] if q < KD else ring[:, s, :].rearrange("p (k n) -> p k n", k=2)
                sp.dma_start(dst, src).then_inc(slot_full[s], 16)

            for n in range(N_MIX):
                if n >= RING_MIX:
                    sp.wait_ge(unit_done, n - RING_MIX + 1)
                sp.dma_start(k_view(mix_slot(n)), mix_src(n)).then_inc(slot_full[mix_slot(n)], 16)
            for u in range(BODY * EXP_UNITS):
                if u < RING_MIX:
                    sp.wait_ge(unit_done, N_MIX - RING_MIX + u + 1)
                elif u == RING_MIX:
                    sp.wait_ge(mix_ready, 4)
                elif u >= RING:
                    sp.wait_ge(unit_done, N_MIX + u - RING + 1)
                load_moe(0, u)
            with sp.Fori(1, NE // BODY) as i:
                for u in range(BODY * EXP_UNITS):
                    sp.wait_ge(unit_done, i * (BODY * EXP_UNITS) + (N_MIX + u - RING + 1))
                    load_moe(i, u)
            sp.wait_ge(fin_ready, 1)
            sp.dma_start(out[0, 0:P, :], hN[:, 0, :]).then_inc(out_done, 16)
            sp.wait_ge(fin_ready, 2)
            sp.dma_start(out[0, P:SEQ, :], hN[:, 1, :]).then_inc(out_done, 16)
            sp.wait_ge(out_done, 32)

        @block.tensor
        def _(pe):
            pe.wait_ge(c_in, 16)
            pe.wait_ge(row_in, 16 * 5)
            pe.wait_ge(dsk_ready, 1)
            nc.tensor.transpose(bank[6][:, 0:N_ROWS], prm[0:N_ROWS, :], ident[0:N_ROWS, 0:N_ROWS])
            nc.tensor.transpose(bank[6][:, N_ROWS:N_ROWS + 8], dske[:, :], ident[0:8, 0:8]).then_inc(prm_ready, 1)
            pe.wait_ge(b1_in, 16)
            for m in range(16):
                last = nc.tensor.transpose(bank[7][:, m * NE:(m + 1) * NE], b1raw[:, m * P:(m + 1) * P],
                                           ident[0:NE, 0:NE])
            last.then_inc(prm_ready, 1)

            def to_T(ready, psum_sem):
                pe.wait_ge(ready, 2)
                for b in range(4):
                    for kk in range(2):
                        for t in range(TT):
                            k = 2 * b + kk
                            last = nc.tensor.transpose(bank[2 + b][:, kk * 256 + t * P:kk * 256 + (t + 1) * P],
                                                       hN[:, t, k * P:(k + 1) * P], ident)
                    last.then_inc(psum_sem, 1)

            to_T(h_ready, hT_psum)

            def unit(n, rhs=None, tokens=None):
                mix_full(pe, n)
                if n >= 2:
                    pe.wait_ge(unit_taken, n - 1)
                w = k_view(mix_slot(n))
                for a in range(2):
                    for k in range(KD):
                        o = bank[n % 2][:, a * 256:(a + 1) * 256]
                        if tokens is None:
                            last = nc.tensor.matmul(o, w[:, k, a * P:(a + 1) * P], rhs[:, k, :],
                                                    start=(k == 0), stop=(k == KD - 1))
                        else:
                            last = nc.tensor.matmul(o, tokens[:, k, a * P:(a + 1) * P], w[:, k, :],
                                                    start=(k == 0), stop=(k == KD - 1))
                last.then_inc(unit_done, 1)

            pe.wait_ge(hT_ready, 4)
            for n in range(U_XBC, U_Z):
                unit(n, rhs=hT)
            pe.wait_ge(wdt_in, 16)
            pe.wait_ge(prm_taken, 2)
            for t in range(TT):
                for k in range(KD):
                    last = nc.tensor.matmul(bank[6][:, t * 32:(t + 1) * 32], hT[:, k, t * P:(t + 1) * P], wdt[:, k, :],
                                            start=(k == 0), stop=(k == KD - 1))
            last.then_inc(dt_psum, 1)
            for n in range(U_Z, U_K):
                unit(n, rhs=hT)
            pe.wait_ge(silu_done, 4)
            for b in range(4):
                t = b // 2
                for jj in range(4):
                    j = (b % 2) * 4 + jj
                    last = nc.tensor.transpose(bank[2 + b][:, jj * P:(jj + 1) * P], xbcT[:, j, t * P:(t + 1) * P], ident)
                last.then_inc(xN_psum, 1)
            pe.wait_ge(silu_done, 6)
            pe.wait_ge(dt_in, 1)
            for g in range(2):
                for i in range(TT):
                    last = nc.tensor.matmul(bank[6 + g][:, i * 256:(i + 1) * 256], xbcT[:, 8 + g, i * P:(i + 1) * P],
                                            xbcT[:, 10 + g, :], start=True, stop=True)
                last.then_inc(cb_psum, 1)

            unit(U_K, tokens=hT)
            pe.wait_ge(a_ready, 1)
            pe.wait_ge(cb_ready, 2)
            f, b_ = slice(0, NH), slice(NH, 2 * NH)
            nc.tensor.matmul(bank[7][:, 0:16], m_le, dta[:, 0, f], start=True, stop=True)
            nc.tensor.matmul(bank[7][:, 16:32], ones, dta[:, 1, b_], start=True, stop=False)
            nc.tensor.matmul(bank[7][:, 16:32], m_ge, dta[:, 0, b_], start=False, stop=True)
            nc.tensor.matmul(bank[7][:, 32:48], ones, dta[:, 0, f], start=True, stop=False)
            nc.tensor.matmul(bank[7][:, 32:48], m_le, dta[:, 1, f], start=False, stop=True)
            nc.tensor.matmul(bank[7][:, 48:64], m_ge, dta[:, 1, b_], start=True, stop=True).then_inc(acs_psum, 1)
            unit(U_Q, tokens=hT)
            pe.wait_ge(acsN_ready, 2)
            for t in range(TT):
                last = nc.tensor.transpose(bank[7][0:32, 256 + t * P:256 + (t + 1) * P], acsN[:, t, :], ident)
            last.then_inc(acsT_psum, 1)

            def qk_transposes(v):
                pe.wait_ge(roped_ready, v + 1)
                if v == 4:
                    pe.wait_ge(qT_ready, 1)
                for hh in range(2):
                    for t in range(TT):
                        last = nc.tensor.transpose(bank[2 + v % 4][:, hh * 256 + t * P:hh * 256 + (t + 1) * P],
                                                   roped[:, t, v * 256 + hh * P:v * 256 + (hh + 1) * P], ident)
                last.then_inc(qT_psum, 1)

            pe.wait_ge(xN_ready, 4)
            qk_transposes(0)
            for v in range(1, 4):
                unit(U_Q + v, tokens=hT)
                qk_transposes(v)
            unit(U_V, tokens=hT)
            qk_transposes(4)

            def seg(g):
                for hh in range(2):
                    h = 2 * g + hh
                    if h >= 2:
                        pe.wait_ge(seg_masked, h - 1)
                    for d in range(2):
                        r = d * NH + h
                        last = nc.tensor.matmul(bank[2 + hh][:, d * 256:(d + 1) * 256],
                                                ident[0:32, r:r + 1].to_broadcast([32, P]), acsT[:, :],
                                                start=True, stop=True)
                    last.then_inc(seg_psum, 1)

            def scores(h):
                if h >= 1:
                    pe.wait_ge(sc_exp, h)
                for t in range(TT):
                    last = nc.tensor.matmul(bank[4][:, t * 256:(t + 1) * 256], qT[:, h, t * P:(t + 1) * P],
                                            kT[:, h // (AH // KVH), :], start=True, stop=True)
                last.then_inc(sc_psum, 1)

            pe.wait_ge(qT_ready, 5)
            pe.wait_ge(acsT_ready, 1)
            seg(0)
            scores(0)
            for g in range(8):
                unit(U_G + g, rhs=hT)
                pe.wait_ge(prob_ready, g + 1)
                if g >= 1:
                    pe.wait_ge(probT_ready, g)
                for i in range(TT):
                    for t in range(TT):
                        last = nc.tensor.transpose(bank[5][:, i * 256 + t * P:i * 256 + (t + 1) * P],
                                                   prob[:, t, i * P:(i + 1) * P], ident)
                last.then_inc(probT_psum, 1)
                if g < 7:
                    seg(g + 1)
                    scores(g + 1)
                if g >= 1:
                    pe.wait_ge(yz_ready, 2 * g - 1)
                for hh in range(2):
                    pe.wait_ge(g_ready, 2 * g + hh + 1)
                    for i in range(TT):
                        last = nc.tensor.matmul(bank[7][hh * HD:(hh + 1) * HD, 0:256],
                                                hN[:, i, (2 * g + hh) * HD:(2 * g + hh + 1) * HD],
                                                gbuf[:, g % 2, hh, i, :], start=(i == 0), stop=(i == TT - 1))
                last.then_inc(y_psum, 1)
                pe.wait_ge(probT_ready, g + 1)
                if g >= 1:
                    pe.wait_ge(o_ready, g)
                for i in range(TT):
                    kv = g // (AH // KVH)
                    last = nc.tensor.matmul(bank[6][:, 0:256], vN[:, i, kv * AD:(kv + 1) * AD], probT[:, i, :],
                                            start=(i == 0), stop=(i == TT - 1))
                last.then_inc(o_psum, 1)

            pe.wait_ge(o_ready, 8)
            for n in range(U_BA, U_BS):
                unit(n, rhs=qT)
            pe.wait_ge(ysq_added, 8)
            nc.tensor.matmul(bank[7][:, 256:512], ones, sqacc, start=True, stop=True).then_inc(ssq_psum, 1)
            pe.wait_ge(yg_ready, 8)
            for n in range(U_BS, U_O):
                unit(n, rhs=xbcT)
            pe.wait_ge(mix_ready, 4)
            for n in range(U_O, N_MIX):
                unit(n, tokens=hT)

            to_T(h2_ready, h2T_psum)
            pe.wait_ge(h2T_ready, 4)
            pe.wait_ge(late_in, 16 * 2)
            for t in range(TT):
                for k in range(KD):
                    last = nc.tensor.matmul(bank[6][:, t * NE:(t + 1) * NE], hT[:, k, t * P:(t + 1) * P], wr[:, k, :],
                                            start=(k == 0), stop=(k == KD - 1))
            last.then_inc(lg_psum, 1)
            pe.wait_ge(w_ready, 1)
            nc.tensor.matmul(bank[7][:, 0:NE], m_le, msk[:, 0, :], start=True, stop=True)
            nc.tensor.matmul(bank[7][:, NE:2 * NE], ones, msk[:, 0, :], start=True, stop=False)
            nc.tensor.matmul(bank[7][:, NE:2 * NE], m_le, msk[:, 1, :], start=False, stop=True)
            nc.tensor.matmul(bank[7][:, 2 * NE:3 * NE], ones, msk[:, 0, :], start=True, stop=False)
            nc.tensor.matmul(bank[7][:, 2 * NE:3 * NE], ones, msk[:, 1, :], start=False, stop=True)
            pe.wait_ge(w_ready, 2)
            for t in range(TT):
                last = nc.tensor.transpose(bank[0][0:NE, t * P:(t + 1) * P], wtok[:, t, 0:NE], ident)
            last.then_inc(wT_psum, 1)
            pe.wait_ge(wT_ready, 1)
            for t in range(TT):
                for hf in range(2):
                    nc.tensor.matmul(bank[2 + 2 * t + hf][:, :], wT[:, t * P:(t + 1) * P], b2s[:, hf * 512:(hf + 1) * 512],
                                     start=True, stop=True).then_inc(b2_psum, 1)

            def gather(par):
                for k in range(KD):
                    for t in range(TT):
                        last = nc.tensor.matmul(bank[2][:, k * CAP:(k + 1) * CAP], hN[:, t, k * P:(k + 1) * P],
                                                slotP[:, par, t, :], start=(k == 0 and t == 0),
                                                stop=(k == KD - 1 and t == TT - 1), skip_group_check=True)
                last.then_inc(x_psum, 1)

            def mlp1(par, k, w):
                for m in range(16):
                    last = nc.tensor.matmul(bank[m // 8][:, (m % 8) * CAP:(m % 8 + 1) * CAP], w[:, m * P:(m + 1) * P],
                                            xT[:, par, k, :], start=(k == 0 and m % 8 == 0),
                                            stop=(k == KD - 1 and m % 8 == 7), skip_group_check=True)
                return last

            def mlp2(par, k, w):
                for m in range(KD):
                    last = nc.tensor.matmul(bank[3][:, m * CAP:(m + 1) * CAP], w[:, m * P:(m + 1) * P],
                                            actT[:, par, k, :], start=(k == 0 and m == 0),
                                            stop=(k == KD - 1 and m == KD - 1), skip_group_check=True)
                return last

            def slot_transposes(pb):
                for t in range(TT):
                    last = nc.tensor.transpose(bank[7][:, t * P:(t + 1) * P],
                                               slotW[:, pb, t, :, :].rearrange("p e s -> p (e s)"), ident)
                last.then_inc(pw_psum, 1)

            def y_transposes():
                for k in range(KD):
                    last = nc.tensor.transpose(bank[4 + k // 4][:, (k % 4) * P:(k % 4 + 1) * P],
                                               yTs[:, k, :, :].rearrange("p e s -> p (e s)"), ident)
                last.then_inc(yt_psum, 1)

            def combine(q):
                nc.tensor.matmul(bank[6 + q % 2][:, :], slotWT[:, (q // 2) * P:(q // 2 + 1) * P],
                                 ys[:, (q % 2) * 512:(q % 2 + 1) * 512], start=True, stop=True).then_inc(c_psum, 1)

            pe.wait_ge(p_ready, 1)
            pe.wait_ge(route_ready, 1)
            gather(0)
            with pe.Fori(0, NE // BODY) as i:
                for c in range(BODY):
                    e = i * BODY + c
                    par = c % 2
                    pe.wait_ge(xT_ready, e + 1)
                    for k in range(KD):
                        u = c * EXP_UNITS + k
                        moe_full(pe, i, u)
                        last = mlp1(par, k, ring[:, moe_slot(u % RING), :])
                        last.then_inc(unit_done, 1)
                    pe.wait_ge(p_ready, e + 2)
                    gather((c + 1) % 2)
                    pe.wait_ge(actT_ready, e + 1)
                    if par == 1:
                        pe.wait_ge(yTs_ready, e)
                    for kk in range(4):
                        u = c * EXP_UNITS + KD + kk
                        moe_full(pe, i, u)
                        w = ring[:, moe_slot(u % RING), :].rearrange("p (k n) -> p k n", k=2)
                        mlp2(par, 2 * kk, w[:, 0, :])
                        last = mlp2(par, 2 * kk + 1, w[:, 1, :])
                        last.then_inc(unit_done, 1)
                    if par == 1:
                        pair = i * 2 + c // 2
                        slot_transposes(c // 2)
                        pe.wait_ge(yTs_ready, e + 1)
                        y_transposes()
                        pe.wait_ge(pw_ready, pair + 1)
                        pe.wait_ge(ys_ready, pair + 1)
                        for q in range(4):
                            if q >= 2:
                                pe.wait_ge(c_added, pair * 4 + q - 1)
                            combine(q)

        @block.scalar
        def _(act):
            link = chain(act, act_step)
            act.dma_start(xres[:, :, :], x[0].rearrange("(t p) d -> p t d", p=P)).then_inc(x_in, 16)
            act.dma_start(cst[:, :], consts).then_inc(c_in, 16)
            for r, src in ((R_GMIX, g_mix[0].rearrange("(k p) -> k p", p=P)), (R_GSSM, g_ssm[0].rearrange("(k p) -> k p", p=P)),
                           (R_GFFN, g_ffn[0].rearrange("(k p) -> k p", p=P)), (R_CB, conv_b[0].rearrange("(k p) -> k p", p=P)),
                           (R_CW, conv_w[0].rearrange("j (k p) -> (j k) p", p=P))):
                act.dma_start(prm[r:r + src.shape[0], :], src).then_inc(row_in, 16)
            act.dma_start(dskr[:, :], d_skip[0].rearrange("(j h) -> j h", h=2)).then_inc(dsk_in, 16)
            act.dma_start(b1raw, b_mlp1[0]).then_inc(b1_in, 16)
            act.dma_start(wdt[:, :, :], w_in[0].rearrange("(k p) n -> p k n", p=P)[:, :, DT0:DT0 + 2 * NH]).then_inc(wdt_in, 16)
            at = 0
            for v in (dt_bias_f, dt_bias_b, a_log_f, a_log_b, b_router, k_norm_g, q_norm_g):
                act.dma_start(vec[:, at:at + v.shape[1]], v[0].partition_broadcast(P)).then_inc(vec_in, 16)
                at += v.shape[1]
            act.dma_start(wr[:, :, :], w_router[0].rearrange("(k p) n -> p k n", p=P)).then_inc(late_in, 16)

            act.wait_ge(x_in, 16)
            for t in range(TT):
                nc.scalar.activation(hN[:, t, :], xres[:, t, :], ACT.Square, accum_out=stat[:, t:t + 1]).then_inc(xsq_ready, 1)
            act.wait_ge(prm_ready, 1)
            nc.scalar.activation(prmT[:, :], bank[6][:, 0:N_ROWS + 8], ACT.Copy).then_inc(prm_taken, 1)
            act.wait_ge(prm_ready, 2)
            nc.scalar.activation(b1T[:, :, :], bank[7][:, :].rearrange("p (m e) -> p e m", m=16), ACT.Copy).then_inc(prm_taken, 1)

            def silu(u):
                act.wait_ge(conv_done, u + 1)
                nc.scalar.activation(xbcT[:, 2 * u:2 * u + 2, :], xbcT[:, 2 * u:2 * u + 2, :], ACT.Silu).then_inc(silu_done, 1)

            for u in range(6):
                act.wait_ge(unit_done, U_XBC + u + 1)
                if u >= 2:
                    act.wait_ge(conv_done, u - 1)
                else:
                    act.wait_ge(pool_step, 1)
                nc.scalar.activation(xp[:, u % 2, :, PAD:PAD + SEQ], bank[(U_XBC + u) % 2][:, :].rearrange("p (m l) -> p m l", m=2),
                                     ACT.Copy).then_inc(unit_taken, 1)
                if u >= 1:
                    silu(u - 1)
            silu(5)
            for u in range(4):
                act.wait_ge(unit_done, U_Z + u + 1)
                nc.scalar.activation(siluz[:, 2 * u:2 * u + 2, :], bank[(U_Z + u) % 2][:, :].rearrange("p (m l) -> p m l", m=2),
                                     ACT.Silu).then_inc(unit_taken, 1)
            for b in range(4):
                act.wait_ge(xN_psum, b + 1)
                t = b // 2
                nc.scalar.activation(hN[:, t, (b % 2) * 512:(b % 2 + 1) * 512], bank[2 + b][:, :], ACT.Copy).then_inc(xN_ready, 1)
            for g in range(2):
                act.wait_ge(cb_psum, g + 1)
                nc.scalar.activation(cb[:, g, :, :], bank[6 + g][:, :].rearrange("p (i l) -> p i l", i=TT), ACT.Copy).then_inc(cb_ready, 1)
            act.wait_ge(dt_in, 1)
            act.wait_ge(vec_in, 16 * 7)
            nc.scalar.activation(dtu[:, :, :], dta[:, :, :], ACT.Exp, scale=-1.0).then_inc(dt_exp, 1)
            nc.scalar.activation(alog_b, alog_b, ACT.Exp).then_inc(dt_exp, 1)

            def qk_square(v, n):
                act.wait_ge(unit_done, n + 1)
                nc.scalar.activation(qk[:, :, v * 256:(v + 1) * 256], bank[n % 2][:, :].rearrange("p (t c) -> p t c", t=TT),
                                     ACT.Copy).then_inc(unit_taken, 1)
                act.wait_ge(unit_taken, n + 1)
                nc.scalar.activation(roped[:, :, v * 256:(v + 1) * 256], qk[:, :, v * 256:(v + 1) * 256], ACT.Square).then_inc(qsq_ready, 1)

            def qT_copy(v):
                act.wait_ge(qT_psum, v + 1)
                dst = kT if v == 0 else qT[:, 2 * v - 2:2 * v, :]
                nc.scalar.activation(dst, bank[2 + v % 4][:, :].rearrange("p (h l) -> p h l", h=2), ACT.Copy).then_inc(qT_ready, 1)

            qk_square(0, U_K)
            qk_square(1, U_Q)
            act.wait_ge(acsT_psum, 1)
            nc.scalar.activation(acsT[:, :], bank[7][0:32, 256:512], ACT.Copy).then_inc(acsT_ready, 1)
            for v in range(2, 5):
                qk_square(v, U_Q + v - 1)
                qT_copy(v - 2)
            qT_copy(3)
            act.wait_ge(unit_done, U_V + 1)
            nc.scalar.activation(vN[:, :, :], bank[U_V % 2][:, :].rearrange("p (t c) -> p t c", t=TT), ACT.Copy).then_inc(unit_taken, 1)
            qT_copy(4)

            def seg_exps(g):
                for hh in range(2):
                    act.wait_ge(seg_masked, 2 * g + hh + 1)
                    nc.scalar.activation(ebuf[:, hh, :], ebuf[:, hh, :], ACT.Exp).then_inc(seg_exp, 1)

            def score_exps(h):
                act.wait_ge(sc_max, h + 1)
                if h >= 1:
                    act.wait_ge(probT_psum, h)
                for t in range(TT):
                    last = nc.scalar.activation(prob[:, t, :], bank[4][:, t * 256:(t + 1) * 256], ACT.Exp,
                                                bias=stat[:, 12 + t:13 + t], scale=float(AD) ** -0.5,
                                                accum_out=stat[:, 14 + t:15 + t])
                last.then_inc(sc_exp, 1)

            score_exps(0)
            seg_exps(0)
            for g in range(8):
                act.wait_ge(unit_done, U_G + g + 1)
                nc.scalar.activation(sig[:, 2 * g:2 * g + 2, :], bank[(U_G + g) % 2][:, :].rearrange("p (m l) -> p m l", m=2),
                                     ACT.Exp, scale=-1.0).then_inc(unit_taken, 1)
                act.wait_ge(probT_psum, g + 1)
                if g >= 1:
                    act.wait_ge(o_psum, g)
                nc.scalar.activation(probT[:, :, :], bank[5][:, :].rearrange("p (i q) -> p i q", i=TT), ACT.Copy).then_inc(probT_ready, 1)
                if g < 7:
                    score_exps(g + 1)
                    seg_exps(g + 1)
                act.wait_ge(o_psum, g + 1)
                nc.scalar.activation(qT[:, g, :], bank[6][:, 0:256], ACT.Copy).then_inc(o_ready, 1)
                act.wait_ge(yz_ready, 2 * g + 2)
                if g >= 1:
                    act.wait_ge(ysq_added, g)
                nc.scalar.activation(sqb, xbcT[:, g, :], ACT.Square).then_inc(ysq_ready, 1)
                nc.scalar.activation(xbcT[:, g, :], xbcT[:, g, :], ACT.Copy, scale=prmT[:, R_GSSM + g:R_GSSM + g + 1]).then_inc(yg_ready, 1)
            act.dma_start(b2s, b_mlp2[0]).then_inc(late_in, 16)
            act.wait_ge(ssq_psum, 1)
            nc.scalar.activation(rB, bank[7][:, 256:512], ACT.Copy, bias=EPS, scale=1.0 / D).then_inc(ssq_ready, 1)
            act.wait_ge(unit_taken, N_MIX)
            for t in range(TT):
                nc.scalar.activation(hN[:, t, :], xres[:, t, :], ACT.Square, accum_out=stat[:, 20 + t:21 + t]).then_inc(x1sq_ready, 1)
            act.wait_ge(lmax_ready, 1)
            for t in range(TT):
                last = nc.scalar.activation(lgt[:, t, :], lgt[:, t, :], ACT.Exp, bias=stat[:, 26 + t:27 + t])
            last.then_inc(lexp_ready, 1)
            act.wait_ge(wT_psum, 1)
            nc.scalar.activation(wT[:, :], bank[0][0:NE, 0:SEQ], ACT.Copy).then_inc(wT_ready, 1)
            act.wait_ge(wT_ready, 1)
            act.dma_start(gfin, g_final.partition_broadcast(P)).then_inc(gfin_in, 16)

            with act.Fori(0, NE // BODY) as i:
                for c in range(BODY):
                    e = i * BODY + c
                    act.wait_ge(ga_ready, e + 1)
                    nc.scalar.activation(sg, ga, ACT.Sigmoid, scale=ALPHA).then_inc(sg_ready, 1)
                    act.wait_ge(unit_done, e * EXP_UNITS + (N_MIX + EXP_UNITS))
                    nc.scalar.activation(yTs[:, :, c % 2, :], bank[3][:, :].rearrange("p (k s) -> p k s", k=KD), ACT.Copy).then_inc(yTs_ready, 1)
                    if c % 2 == 1:
                        pair = i * 2 + c // 2
                        act.wait_ge(pw_psum, pair + 1)
                        nc.scalar.activation(slotWT, bank[7][:, 0:256], ACT.Copy).then_inc(pw_ready, 1)
                        act.wait_ge(yt_psum, pair + 1)
                        nc.scalar.activation(ys[:, 0:512], bank[4][:, :], ACT.Copy)
                        nc.scalar.activation(ys[:, 512:1024], bank[5][:, :], ACT.Copy).then_inc(ys_ready, 1)

            act.wait_ge(c_added, 2 * NE)
            for t in range(TT):
                nc.scalar.activation(hN[:, t, :], xres[:, t, :], ACT.Square, accum_out=stat[:, 30 + t:31 + t]).then_inc(fsq_ready, 1)

        @block.gpsimd
        def _(pool):
            link = chain(pool, pool_step)
            link(nc.gpsimd.memset(xp, 0.0))
            nc.gpsimd.memset(stat[:, 40:64], -0.5).then_inc(pool_step, 1)
            nc.gpsimd.memset(sqacc, 0.0).then_inc(pool_step, 1)
            pool.wait_ge(pool_step, 3)
            link.count[0] = 3

            def rsqrt_mean(o, n, count):
                link(nc.gpsimd.tensor_scalar(stat[:, o:o + n], stat[:, o:o + n], 1.0 / count, EPS, ALU.mult, ALU.add))
                return nc.gpsimd.tensor_tensor(stat[:, o:o + n], stat[:, o:o + n], stat[:, 40:40 + n], ALU.pow)

            pool.wait_ge(xsq_ready, 2)
            rsqrt_mean(0, TT, D).then_inc(xr_ready, 1)
            for v in range(5):
                pool.wait_ge(qr_ready, 2 * v + 1)
                rsqrt_mean(4, 4, AD).then_inc(qr_ready, 1)
            for g in range(8):
                pool.wait_ge(ysq_ready, g + 1)
                nc.gpsimd.tensor_tensor(sqacc, sqacc, sqb, ALU.add).then_inc(ysq_added, 1)
                pool.wait_ge(ysq_added, g + 1)
            pool.wait_ge(ssq_ready, 1)
            nc.gpsimd.tensor_tensor(rB, rB, stat[:, 40:41].to_broadcast([P, 256]), ALU.pow).then_inc(rB_ready, 1)
            pool.wait_ge(x1sq_ready, 2)
            rsqrt_mean(20, TT, D).then_inc(x1r_ready, 1)
            pool.wait_ge(fsq_ready, 2)
            rsqrt_mean(30, TT, D).then_inc(fr_ready, 1)

        @block.vector
        def _(dve):
            link = chain(dve, dve_step)
            V = nc.vector
            dve.wait_ge(dsk_in, 16)
            V.tensor_copy(dske[:, :].rearrange("j (h p) -> j h p", h=2),
                          dskr[:, :].unsqueeze(2).to_broadcast([8, 2, HD])).then_inc(dsk_ready, 1)
            dve.wait_ge(xr_ready, 1)
            for t in range(TT):
                V.tensor_scalar(hN[:, t, :], xres[:, t, :], stat[:, t:t + 1], None, ALU.mult).then_inc(h_ready, 1)
            dve.wait_ge(prm_taken, 1)

            def scaled_T(psum_sem, ready, row):
                for b in range(4):
                    dve.wait_ge(psum_sem, b + 1)
                    V.tensor_tensor(hT[:, 2 * b:2 * b + 2, :], bank[2 + b][:, :].rearrange("p (k l) -> p k l", k=2),
                                    prmT[:, row + 2 * b:row + 2 * b + 2].unsqueeze(2).to_broadcast([P, 2, SEQ]), ALU.mult).then_inc(ready, 1)

            scaled_T(hT_psum, hT_ready, R_GMIX)
            for u in range(6):
                dve.wait_ge(unit_taken, U_XBC + u + 1)
                for j in range(CONV):
                    for mm in range(2):
                        m = 2 * u + mm
                        wcol = prmT[:, R_CW + j * XBC_TILES + m:R_CW + j * XBC_TILES + m + 1]
                        src = xp[:, u % 2, mm, j:j + SEQ]
                        if j == 0:
                            last = V.tensor_scalar(xbcT[:, m, :], src, wcol, prmT[:, R_CB + m:R_CB + m + 1], ALU.mult, ALU.add)
                        else:
                            last = V.scalar_tensor_tensor(xbcT[:, m, :], src, wcol, xbcT[:, m, :], ALU.mult, ALU.add)
                    if j < CONV - 1:
                        link(last)
                last.then_inc(conv_done, 1)
            dve.wait_ge(dt_psum, 1)
            dve.wait_ge(vec_in, 16 * 7)
            link(V.tensor_tensor(dtv[:, :, :], bank[6][:, 0:64].rearrange("p (t c) -> p t c", t=TT),
                                 dtb_b.unsqueeze(1).to_broadcast([P, TT, 32]), ALU.add))
            V.scalar_tensor_tensor(dta[:, :, :], dtv[:, :, :], -1.0, dtv[:, :, :], ALU.mult, ALU.max).then_inc(dt_in, 1)
            dve.wait_ge(dt_exp, 2)
            link(V.tensor_scalar(dta[:, :, :], dtu[:, :, :], 2.0, None, ALU.add))
            link(V.reciprocal(dta[:, :, :], dta[:, :, :]))
            link(V.tensor_tensor(dtu[:, :, :], dtu[:, :, :], dta[:, :, :], ALU.mult))
            link(V.tensor_tensor(acsN[:, :, :], dtu[:, :, :], dtu[:, :, :], ALU.mult))
            link(V.tensor_scalar(dta[:, :, :], acsN[:, :, :], 1.0 / 19, None, ALU.mult))
            for k in range(17, 1, -2):
                link(V.scalar_tensor_tensor(dta[:, :, :], dta[:, :, :], 1.0 / k, acsN[:, :, :], ALU.add, ALU.mult))
            link(V.scalar_tensor_tensor(dta[:, :, :], dta[:, :, :], 1.0, dtu[:, :, :], ALU.add, ALU.mult))
            link(V.tensor_scalar(dtv[:, :, :], dtv[:, :, :], 0.0, None, ALU.max))
            link(V.scalar_tensor_tensor(dtv[:, :, :], dta[:, :, :], 2.0, dtv[:, :, :], ALU.mult, ALU.add))
            V.scalar_tensor_tensor(dta[:, :, :], dtv[:, :, :], -1.0, alog_b.unsqueeze(1).to_broadcast([P, TT, 32]),
                                   ALU.mult, ALU.mult).then_inc(a_ready, 1)

            def rope(v):
                raw = qk[:, :, v * 256:(v + 1) * 256].rearrange("p t (h d) -> p t h d", h=2)
                new = roped[:, :, v * 256:(v + 1) * 256].rearrange("p t (h d) -> p t h d", h=2)
                tmp = ropeb[:, :, :].rearrange("p t (h d) -> p t h d", h=2)
                ss = stat[:, 4:8].rearrange("p (t h) -> p t h", t=TT)
                dve.wait_ge(qsq_ready, v + 1)
                V.tensor_reduce(ss, new, AXX, ALU.add).then_inc(qr_ready, 1)
                dve.wait_ge(qr_ready, 2 * v + 2)
                link(V.tensor_tensor(raw, raw, ss.unsqueeze(3).to_broadcast([P, TT, 2, AD]), ALU.mult))
                gb = (kg_b if v == 0 else qg_b).unsqueeze(1).unsqueeze(1).to_broadcast([P, TT, 2, AD])
                link(V.tensor_tensor(raw, raw, gb, ALU.mult))
                for t in range(TT):
                    cosv = cst[:, C_COS + t * AD:C_COS + (t + 1) * AD].unsqueeze(1).to_broadcast([P, 2, AD])
                    V.tensor_tensor(new[:, t], raw[:, t], cosv, ALU.mult)
                    for hf in range(2):
                        o = hf * 32
                        sn = cst[:, C_SIN + t * AD:C_SIN + (t + 1) * AD].rearrange("p (a c) -> p a c", a=2)[:, :, o:o + 32]
                        last = V.tensor_tensor(tmp[:, t].rearrange("p h (a c) -> p h a c", a=2)[:, :, :, o:o + 32],
                                               raw[:, t].rearrange("p h (a c) -> p h a c", a=2)[:, :, :, 32 - o:64 - o],
                                               sn.unsqueeze(1).to_broadcast([P, 2, 2, 32]), ALU.mult)
                link(last)
                V.tensor_tensor(new, new, tmp, ALU.add).then_inc(roped_ready, 1)

            rope(0)
            dve.wait_ge(acs_psum, 1)
            V.tensor_copy(acsN[:, :, :], bank[7][:, 0:64].rearrange("p (t c) -> p t c", t=TT)).then_inc(acsN_ready, 1)
            V.tensor_scalar(nacs[:, :, :], bank[7][:, 0:64].rearrange("p (t c) -> p t c", t=TT), -1.0, None, ALU.mult).then_inc(acsN_ready, 1)
            for v in range(1, 5):
                rope(v)

            def seg_mask(g):
                for hh in range(2):
                    h = 2 * g + hh
                    dve.wait_ge(seg_psum, h + 1)
                    e, b = ebuf[:, hh, :], bank[2 + hh]
                    f0, b0 = nacs[:, 0, h:h + 1], nacs[:, 0, NH + h:NH + h + 1]
                    f1, b1 = nacs[:, 1, h:h + 1], nacs[:, 1, NH + h:NH + h + 1]
                    V.scalar_tensor_tensor(e[:, 0:256], b[:, 0:256], f0, cst[:, C_NEGF:C_NEGF + 256], ALU.add, ALU.add)
                    V.scalar_tensor_tensor(e[:, 256:384], b[:, 256:384], b0, cst[:, C_NEGB:C_NEGB + P], ALU.add, ALU.add)
                    V.scalar_tensor_tensor(e[:, 384:512], b[:, 128:256], f1, cst[:, C_NEGF:C_NEGF + P], ALU.add, ALU.add)
                    V.scalar_tensor_tensor(e[:, 512:768], b[:, 256:512], b1, cst[:, C_ZERO:C_ZERO + 256], ALU.add, ALU.add).then_inc(seg_masked, 1)

            def seg_weight(g):
                if g >= 2:
                    dve.wait_ge(y_psum, g - 1)
                for hh in range(2):
                    h = 2 * g + hh
                    dve.wait_ge(seg_exp, h + 1)
                    e, o = ebuf[:, hh, :], gbuf[:, g % 2, hh, :, :]
                    f0, b0 = dtv[:, 0, h:h + 1], dtv[:, 0, NH + h:NH + h + 1]
                    f1, b1 = dtv[:, 1, h:h + 1], dtv[:, 1, NH + h:NH + h + 1]
                    V.tensor_scalar(o[:, 0, :], e[:, 0:256], f0, None, ALU.mult)
                    link(V.tensor_scalar(o[:, 1, :], e[:, 512:768], b1, None, ALU.mult))
                    V.scalar_tensor_tensor(o[:, 0, 0:P], e[:, 256:384], b0, o[:, 0, 0:P], ALU.mult, ALU.add)
                    link(V.scalar_tensor_tensor(o[:, 1, P:256], e[:, 384:512], f1, o[:, 1, P:256], ALU.mult, ALU.add))
                    V.tensor_tensor(o, o, cb[:, h // 8, :, :], ALU.mult).then_inc(g_ready, 1)

            def score_max(h):
                dve.wait_ge(sc_psum, h + 1)
                link(V.tensor_reduce(stat[:, 12:14], bank[4][:, :].rearrange("p (t s) -> p t s", t=TT), AXX, ALU.max))
                V.tensor_scalar(stat[:, 12:14], stat[:, 12:14], -(float(AD) ** -0.5), None, ALU.mult).then_inc(sc_max, 1)

            def prob_norm(h):
                dve.wait_ge(sc_exp, h + 1)
                link(V.reciprocal(stat[:, 16:18], stat[:, 14:16]))
                for t in range(TT):
                    last = V.tensor_scalar(prob[:, t, :], prob[:, t, :], stat[:, 16 + t:17 + t], None, ALU.mult)
                last.then_inc(prob_ready, 1)

            dve.wait_ge(qT_psum, 5)
            dve.wait_ge(acsN_ready, 2)
            dve.wait_ge(cb_ready, 2)
            score_max(0)
            seg_mask(0)
            prob_norm(0)
            seg_weight(0)
            for g in range(8):
                dve.wait_ge(unit_taken, U_G + g + 1)
                link(V.tensor_scalar(sig[:, 2 * g:2 * g + 2, :], sig[:, 2 * g:2 * g + 2, :], 1.0, None, ALU.add))
                V.reciprocal(sig[:, 2 * g:2 * g + 2, :], sig[:, 2 * g:2 * g + 2, :]).then_inc(gate_ready, 1)
                if g < 7:
                    seg_mask(g + 1)
                    score_max(g + 1)
                dve.wait_ge(y_psum, g + 1)
                V.scalar_tensor_tensor(xbcT[:, g, :], xbcT[:, g, :], prmT[:, N_ROWS + g:N_ROWS + g + 1], bank[7][:, 0:256],
                                       ALU.mult, ALU.add).then_inc(yz_ready, 1)
                dve.wait_ge(yz_ready, 2 * g + 1)
                V.tensor_tensor(xbcT[:, g, :], xbcT[:, g, :], siluz[:, g, :], ALU.mult).then_inc(yz_ready, 1)
                if g < 7:
                    prob_norm(g + 1)
                    seg_weight(g + 1)

            dve.wait_ge(gate_ready, 8)
            for u in range(4):
                n = U_BA + u
                dve.wait_ge(unit_done, n + 1)
                V.tensor_tensor(hT[:, 2 * u:2 * u + 2, :], bank[n % 2][:, :].rearrange("p (m l) -> p m l", m=2),
                                sig[:, KD + 2 * u:KD + 2 * u + 2, :], ALU.mult).then_inc(unit_taken, 1)
            dve.wait_ge(unit_taken, U_BS)
            dve.wait_ge(rB_ready, 1)
            for u in range(4):
                n = U_BS + u
                dve.wait_ge(unit_done, n + 1)
                s = sig[:, 2 * u:2 * u + 2, :]
                link(V.tensor_tensor(s, s, rB.unsqueeze(1).to_broadcast([P, 2, SEQ]), ALU.mult))
                V.tensor_tensor(s, s, bank[n % 2][:, :].rearrange("p (m l) -> p m l", m=2), ALU.mult).then_inc(unit_taken, 1)
                dve.wait_ge(unit_taken, n + 1)
                V.tensor_tensor(hT[:, 2 * u:2 * u + 2, :], hT[:, 2 * u:2 * u + 2, :], s, ALU.add).then_inc(mix_ready, 1)
            for u in range(4):
                n = U_O + u
                dve.wait_ge(unit_done, n + 1)
                xs = xres[:, :, u * UW:(u + 1) * UW]
                V.tensor_tensor(xs, xs, bank[n % 2][:, :].rearrange("p (t c) -> p t c", t=TT), ALU.add).then_inc(unit_taken, 1)
            dve.wait_ge(x1r_ready, 1)
            for t in range(TT):
                V.tensor_scalar(hN[:, t, :], xres[:, t, :], stat[:, 20 + t:21 + t], None, ALU.mult).then_inc(h2_ready, 1)
            scaled_T(h2T_psum, h2T_ready, R_GFFN)

            dve.wait_ge(lg_psum, 1)
            link(V.tensor_tensor(lgt, bank[6][:, 0:64].rearrange("p (t e) -> p t e", t=TT),
                                 brt_b.unsqueeze(1).to_broadcast([P, TT, NE]), ALU.add))
            for t in range(TT):
                last = V.max(top8[:, t, :], lgt[:, t, :])
            link(last)
            V.tensor_scalar(stat[:, 26:28], top8[:, :, 0:1].rearrange("p t a -> p (t a)"), -1.0, None, ALU.mult)
            for t in range(TT):
                v4 = top8[:, t, TOPK - 1:TOPK]
                V.tensor_scalar(msk[:, t, :], lgt[:, t, :], v4, None, ALU.is_gt)
                last = V.tensor_scalar(eqm[:, t, :], lgt[:, t, :], v4, None, ALU.is_equal)
            last.then_inc(lmax_ready, 1)
            dve.wait_ge(lmax_ready, 1)
            link(V.tensor_reduce(stat[:, 28:30], msk, AXX, ALU.add))
            V.tensor_scalar(stat[:, 28:30], stat[:, 28:30], -1.0, float(TOPK), ALU.mult, ALU.add)
            for t in range(TT):
                last = V.tensor_tensor_scan(eqc[:, t, :], eqm[:, t, :], eqm[:, t, :], 0.0, ALU.add, ALU.bypass)
            link(last)
            for t in range(TT):
                last = V.scalar_tensor_tensor(eqm[:, t, :], eqc[:, t, :], stat[:, 28 + t:29 + t], eqm[:, t, :], ALU.is_le, ALU.mult)
            link(last)
            V.tensor_tensor(msk, msk, eqm, ALU.add).then_inc(w_ready, 1)
            dve.wait_ge(w_ready, 1)
            dve.wait_ge(lexp_ready, 1)
            link(V.memset(wtok[:, :, NE:NE + 1], 0.0))
            link(V.tensor_tensor(wtok[:, :, 0:NE], lgt, msk, ALU.mult))
            link(V.tensor_reduce(stat[:, 32:34], wtok[:, :, 0:NE], AXX, ALU.add))
            link(V.reciprocal(stat[:, 32:34], stat[:, 32:34]))
            V.tensor_tensor(wtok[:, :, 0:NE], wtok[:, :, 0:NE], stat[:, 32:34].unsqueeze(2).to_broadcast([P, TT, NE]),
                            ALU.mult).then_inc(w_ready, 1)
            dve.wait_ge(wT_psum, 1)
            link(V.memset(rankm[:, :, :], -1.0))
            link(V.tensor_tensor(rankm[:, :, 0:NE], bank[7][:, 0:2 * NE].rearrange("p (t e) -> p t e", t=TT), msk, ALU.mult))
            link(V.tensor_scalar(rankm[:, :, 0:NE], rankm[:, :, 0:NE], -1.0, None, ALU.add))
            link(V.tensor_reduce(cnt[:, 0:1], bank[7][:, 2 * NE:3 * NE], AXX, ALU.max))
            link(V.tensor_scalar(cnt[:, 1:2], cnt[:, 0:1], float(CAP), None, ALU.is_gt))
            link(V.tensor_copy(over_i[:, :], cnt[:, 1:2]))

            def place(e, c):
                for t in range(TT):
                    rk = rankm[:, t, bass.ds(e, 1)]
                    V.tensor_scalar(slotP[:, c % 2, t, :], iota, rk, None, ALU.is_equal)
                    last = V.tensor_scalar(slotW[:, c // 2 % 2, t, c % 2, :], iota, rk, wtok[:, t, bass.ds(e, 1)], ALU.is_equal, ALU.mult)
                last.then_inc(p_ready, 1)

            def expert_in(par):
                V.tensor_tensor(xT[:, par, :, :], bank[2][:, :].rearrange("p (k s) -> p k s", k=KD),
                                prmT[:, R_GFFN:R_GFFN + KD].unsqueeze(2).to_broadcast([P, KD, CAP]), ALU.mult).then_inc(xT_ready, 1)

            for q in range(4):
                dve.wait_ge(b2_psum, q + 1)
                xs = xres[:, q // 2, (q % 2) * 512:(q % 2 + 1) * 512]
                last = V.tensor_tensor(xs, xs, bank[2 + q][:, :], ALU.add)
            last.then_inc(route_ready, 1)
            dve.wait_ge(route_ready, 1)
            place(0, 0)
            dve.wait_ge(x_psum, 1)
            expert_in(0)
            LINKS = 3 * BODY

            with dve.Fori(0, NE // BODY) as i:
                step = chain(dve, moe_dve_step, i * LINKS)
                for c in range(BODY):
                    e = i * BODY + c
                    par = c % 2
                    V_b1 = b1T[:, bass.ds(e, 1), :].rearrange("p a m -> p (a m)")
                    place(e + 1, c + 1)
                    dve.wait_ge(unit_done, e * EXP_UNITS + (N_MIX + KD))
                    V.tensor_tensor(ga.rearrange("p (m s) -> p m s", m=KD), bank[0][:, :].rearrange("p (m s) -> p m s", m=KD),
                                    V_b1[:, 0:KD].unsqueeze(2).to_broadcast([P, KD, CAP]), ALU.add)
                    step(V.tensor_tensor(ub.rearrange("p (m s) -> p m s", m=KD), bank[1][:, :].rearrange("p (m s) -> p m s", m=KD),
                                         V_b1[:, KD:2 * KD].unsqueeze(2).to_broadcast([P, KD, CAP]), ALU.add))
                    V.tensor_scalar(ga, ga, LIMIT, None, ALU.min).then_inc(ga_ready, 1)
                    step(V.tensor_scalar(ub, ub, LIMIT, -LIMIT, ALU.min, ALU.max))
                    dve.wait_ge(ga_ready, e + 1)
                    step(V.scalar_tensor_tensor(ub, ub, 1.0, ga, ALU.add, ALU.mult))
                    dve.wait_ge(sg_ready, e + 1)
                    V.tensor_tensor(actT[:, par, :, :].rearrange("p k s -> p (k s)"), ub, sg, ALU.mult).then_inc(actT_ready, 1)
                    dve.wait_ge(x_psum, e + 2)
                    expert_in((c + 1) % 2)
                    if par == 1:
                        pair = i * 2 + c // 2
                        for q in range(4):
                            dve.wait_ge(c_psum, pair * 4 + q + 1)
                            xs = xres[:, q // 2, (q % 2) * 512:(q % 2 + 1) * 512]
                            V.tensor_tensor(xs, xs, bank[6 + q % 2][:, :], ALU.add).then_inc(c_added, 1)
                assert step.count[0] == LINKS

            dve.wait_ge(fr_ready, 1)
            dve.wait_ge(gfin_in, 16)
            for t in range(TT):
                V.scalar_tensor_tensor(hN[:, t, :], xres[:, t, :], stat[:, 30 + t:31 + t], gfin, ALU.mult, ALU.mult).then_inc(fin_ready, 1)


_INS = ["x", "g_mix", "w_in", "conv_w", "conv_b", "dt_bias_f", "dt_bias_b", "a_log_f", "a_log_b", "d_skip",
        "g_ssm", "q_norm_g", "k_norm_g", "w_br_ssm", "w_br_attn", "w_out", "g_ffn", "w_router", "b_router",
        "w_mlp1", "b_mlp1", "w_mlp2", "b_mlp2", "g_final"]
_OUT = ((1, SEQ, D), "float32")


def kernel(**inputs):
    import numpy as _np
    import concourse.bacc as _bacc
    from concourse import mybir as _mybir
    from concourse.bass_utils import run_bass_kernel_spmd as _run

    nc = _bacc.Bacc("TRN2", target_bir_lowering=False, num_devices=1)
    arrays, args = {}, []
    for name in _INS:
        a = _np.ascontiguousarray(inputs[name])
        arrays[f"in_{name}_dram"] = a
        args.append(nc.dram_tensor(f"in_{name}_dram", a.shape, _mybir.dt.from_np(a.dtype), kind="ExternalInput").ap())
    c = shape_constants()
    arrays["shape_constants_dram"] = c
    args.append(nc.dram_tensor("shape_constants_dram", c.shape, _mybir.dt.from_np(c.dtype), kind="ExternalInput").ap())
    args.append(nc.dram_tensor("out_dram", _OUT[0], _mybir.dt.from_np(_np.dtype(_OUT[1])), kind="ExternalOutput").ap())
    encoder_layer(nc, *args)
    r = _run(nc, [arrays], core_ids=[0])
    return r.results[0]["out_dram"]
```

```python
import math
import concourse.bass as bass
from concourse import mybir
from contextlib import ExitStack

F32 = mybir.dt.float32
I32 = mybir.dt.int32
ALU = mybir.AluOpType
ACT = mybir.ActivationFunctionType
AXX = mybir.AxisListType.X

P = 128
D = 1024
SEQ = 256
TT = SEQ // P
KD = D // P
NH = 16
HD = 64
NST = 128
CONV = 5
PAD = (CONV - 1) // 2
XBC_TILES = (D + 2 * 2 * NST) // P
AH = 8
KVH = 2
AD = 128
XBC0 = D
DT0 = XBC0 + XBC_TILES * P
Q0 = DT0 + 2 * NH
G0 = Q0 + AH * AD + 2 * KVH * AD
NE = 32
TOPK = 4
DE = D
LIMIT = 7.0
ALPHA = 1.702
EPS = 1e-6
CAP = 64
NPASS = SEQ // CAP
NEG = -1e30

UW = 256
UNIT = KD * UW
RING_MIX = 10
RING = 8
EXP_UNITS = 12
BODY = 4
NSPLIT = 4
DIRECT = (3, 9)
SPLIT = tuple(q for q in range(EXP_UNITS) if q not in DIRECT)
SPE = len(SPLIT)
BF16 = mybir.dt.bfloat16
F32R = mybir.dt.float32r

U_XBC, U_Z, U_K, U_Q, U_V, U_G, U_BA, U_BS, U_O = 0, 6, 10, 11, 15, 16, 24, 28, 32
N_MIX = 36

R_GMIX, R_GSSM, R_GFFN, R_CB, R_CW = 0, 8, 16, 24, 36
N_ROWS = R_CW + CONV * XBC_TILES
C_ID, C_LE, C_GE, C_ONE, C_NEGF, C_ZERO, C_NEGB = (P * i for i in range(7))
C_IOTA = 7 * P
C_COS = C_IOTA + CAP
C_SIN = C_COS + TT * AD
C_SUM = C_SIN + TT * AD
N_CONST = C_SUM + CAP
SLAB = 212000


def shape_constants():
    import numpy as np
    r = np.arange(P)
    c = np.zeros((P, N_CONST), np.float32)
    c[:, C_ID:C_ID + P] = r[:, None] == r[None, :]
    c[:, C_LE:C_LE + P] = r[:, None] <= r[None, :]
    c[:, C_GE:C_GE + P] = r[:, None] >= r[None, :]
    c[:, C_ONE:C_ONE + P] = 1.0
    c[:, C_NEGF:C_NEGF + P] = np.where(r[:, None] > r[None, :], NEG, 0.0)
    c[:, C_NEGB:C_NEGB + P] = np.where(r[:, None] < r[None, :], NEG, 0.0)
    c[:, C_IOTA:C_IOTA + CAP] = np.arange(CAP)[None, :]
    c[:, C_SUM:C_SUM + CAP] = (r[:, None] % CAP) == np.arange(CAP)[None, :]
    half = AD // 4
    inv = np.float32(10000.0) ** (-np.arange(0, AD // 2, 2, dtype=np.float32) / np.float32(AD // 2))
    tok = np.arange(SEQ)
    for axis, pos in enumerate((tok // 64, tok % 64)):
        ang = (pos.astype(np.float32)[:, None] * inv).astype(np.float32)
        cos, sin = np.cos(ang).astype(np.float32), np.sin(ang).astype(np.float32)
        for t in range(TT):
            for h, sign in ((0, -1.0), (1, 1.0)):
                o = t * AD + axis * 2 * half + h * half
                c[:, C_COS + o:C_COS + o + half] = cos[t * P:(t + 1) * P]
                c[:, C_SIN + o:C_SIN + o + half] = sign * sin[t * P:(t + 1) * P]
    return c


def encoder_layer(nc, x, g_mix, w_in, conv_w, conv_b, dt_bias_f, dt_bias_b, a_log_f, a_log_b, d_skip,
                  g_ssm, q_norm_g, k_norm_g, w_br_ssm, w_br_attn, w_out, g_ffn, w_router, b_router,
                  w_mlp1, b_mlp1, w_mlp2, b_mlp2, g_final, consts, out):
    with ExitStack() as ctx:
        base = -(-nc.sbuf_base // 32) * 32
        ctx.enter_context(nc.sbuf_tensor("slab", [P, (SLAB + 32) // 4], F32))
        top = [base]
        place_of = {}

        def sb(name, shape, dt=F32, at=None):
            size = int(math.prod(shape[1:])) * mybir.dt.size(dt)
            off = top[0] if at is None else at
            place_of[name] = off
            if at is None:
                top[0] += -(-size // 32) * 32
                assert top[0] <= base + SLAB
            return nc.alloc_sbuf_tensor_at(name, shape, dt, offset=off)

        def sem(name):
            return ctx.enter_context(nc.semaphore(name))

        bank = [ctx.enter_context(nc.psum_tensor(f"bank{i}", [P, 512], F32)) for i in range(8)]

        ring = sb("ring", [P, RING_MIX, UNIT])
        over = sb("over", [P, 12288])
        split = sb("split", [P, NSPLIT, 2, UNIT], F32R, at=place_of["ring"] + RING * UNIT * 4)
        sig = over[:, 0:4096].rearrange("p (m l) -> p m l", m=16)
        roped = over[:, 0:2560].rearrange("p (t n) -> p t n", t=TT)
        xbcT = over[:, 4096:7168].rearrange("p (m l) -> p m l", m=XBC_TILES)
        siluz = over[:, 7168:9216].rearrange("p (m l) -> p m l", m=KD)
        b1raw = over[0:NE, 7168:9216]
        qk = over[:, 9216:11776].rearrange("p (t n) -> p t n", t=TT)
        kT = over[:, 11776:12288].rearrange("p (h l) -> p h l", h=KVH)

        xres = sb("xres", [P, TT, D])
        hN = sb("hN", [P, TT, D])
        hT = sb("hT", [P, KD, SEQ])
        xs = sb("xs", [P, KD, P], F32R, at=place_of["hN"])
        as_ = sb("as", [P, KD, P], F32R, at=place_of["hN"] + KD * P * 4)
        hb3 = sb("hb3", [P, TT, D], BF16, at=place_of["hT"])
        cst = sb("cst", [P, N_CONST])
        prm = sb("prm", [P, P])
        prmT = sb("prmT", [P, N_ROWS + 8])
        dskr = sb("dskr", [8, 2])
        dske = sb("dske", [8, P])
        b1T = sb("b1T", [P, NE, 16])
        wr = sb("wr", [P, KD, NE])
        wdt = sb("wdt", [P, KD, 2 * NH])
        vec = sb("vec", [P, 2 * NH + 2 * NH + NE + 2 * AD])
        dtb_b, alog_b, brt_b = vec[:, 0:32], vec[:, 32:64], vec[:, 64:96]
        kg_b, qg_b = vec[:, 96:224], vec[:, 224:352]
        stat = sb("stat", [P, 64])
        dtv = sb("dtv", [P, TT, 32])
        dta = sb("dta", [P, TT, 32])
        dtu = sb("dtu", [P, TT, 32])
        acsN = sb("acsN", [P, TT, 32])
        nacs = sb("nacs", [P, TT, 32])
        acsT = sb("acsT", [32, SEQ])

        arena = sb("arena", [P, 10000])
        vN = arena[:, 0:512].rearrange("p (t n) -> p t n", t=TT)
        qT = arena[:, 512:2560].rearrange("p (h l) -> p h l", h=AH)
        cb = arena[:, 2560:3584].rearrange("p (g i l) -> p g i l", g=2, i=TT)
        ebuf = arena[:, 3584:5120].rearrange("p (h l) -> p h l", h=2)
        gbuf = arena[:, 5120:7168].rearrange("p (b h i l) -> p b h i l", b=2, h=2, i=TT)
        prob = arena[:, 7168:7680].rearrange("p (t s) -> p t s", t=TT)
        probT = arena[:, 7680:8192].rearrange("p (i q) -> p i q", i=TT)
        ropeb = arena[:, 3584:4096].rearrange("p (t n) -> p t n", t=TT)
        xp = arena[:, 8192:9232].rearrange("p (b m l) -> p b m l", b=2, m=2)
        sqacc = arena[:, 9232:9488]
        sqb = arena[:, 9488:9744]
        rB = arena[:, 9744:10000]
        slotW = arena[:, 0:512].rearrange("p (b t s) -> p b t s", b=2, t=TT)
        x32 = arena[:, 512:1024].rearrange("p (k s) -> p k s", k=KD)
        ga = arena[:, 1024:1536]
        ub = arena[:, 1536:2048]
        act32 = ub.rearrange("p (k s) -> p k s", k=KD)
        wT = arena[0:NE, 1024:1280]
        sg = arena[:, 2048:2560]
        hs = arena[:, 2560:4608]
        ysb = arena[:, 4608:5632]
        b2s = arena[0:NE, 4608:5632]
        slotWT = arena[:, 5632:5888]
        gfin = arena[:, 5888:6912]
        msk = arena[:, 6912:6976].rearrange("p (t e) -> p t e", t=TT)
        lgt = arena[:, 6976:7040].rearrange("p (t e) -> p t e", t=TT)
        top8 = arena[:, 7040:7056].rearrange("p (t e) -> p t e", t=TT)
        eqm = arena[:, 7056:7120].rearrange("p (t e) -> p t e", t=TT)
        eqc = arena[:, 7120:7184].rearrange("p (t e) -> p t e", t=TT)
        hb1 = sb("hb1", [P, TT, D], BF16, at=place_of["arena"] + 4 * 7184)
        hb2 = sb("hb2", [P, TT, D], BF16, at=place_of["arena"] + 4 * (7184 + 1024))
        hb = (hb1, hb2, hb3)
        slotP = sb("slotP", [P, 2, TT, CAP], BF16, at=place_of["arena"] + 4 * (7184 + 2048))
        rankm = sb("rankm", [P, TT, NE + 1])
        wtok = sb("wtok", [P, TT, NE + 1])
        cnt = sb("cnt", [P, 2])
        over_i = sb("over_i", [P, 1], I32)

        ident = cst[:, C_ID:C_ID + P]
        m_le = cst[:, C_LE:C_LE + P]
        m_ge = cst[:, C_GE:C_GE + P]
        ones = cst[:, C_ONE:C_ONE + P]
        iota = cst[:, C_IOTA:C_IOTA + CAP]
        sum_id = cst[:, C_SUM:C_SUM + CAP]

        slot_full = [sem(f"slot_full{i}") for i in range(RING_MIX)]
        unit_done = sem("unit_done")
        c_in = sem("c_in"); x_in = sem("x_in"); row_in = sem("row_in"); b1_in = sem("b1_in")
        vec_in = sem("vec_in"); dsk_in = sem("dsk_in"); wdt_in = sem("wdt_in"); late_in = sem("late_in")
        gfin_in = sem("gfin_in"); out_done = sem("out_done")
        act_step = sem("act_step"); dve_step = sem("dve_step"); pool_step = sem("pool_step")
        moe_dve_step = sem("moe_dve_step")
        dsk_ready = sem("dsk_ready"); prm_ready = sem("prm_ready"); prm_taken = sem("prm_taken")
        xsq_ready = sem("xsq_ready"); xr_ready = sem("xr_ready"); h_ready = sem("h_ready")
        hT_psum = sem("hT_psum"); hT_ready = sem("hT_ready")
        unit_taken = sem("unit_taken")
        xp_ready = sem("xp_ready"); conv_done = sem("conv_done"); silu_done = sem("silu_done")
        dt_psum = sem("dt_psum"); dt_in = sem("dt_in"); dt_exp = sem("dt_exp"); a_ready = sem("a_ready")
        acs_psum = sem("acs_psum"); acsN_ready = sem("acsN_ready"); acsT_psum = sem("acsT_psum")
        acsT_ready = sem("acsT_ready")
        xN_psum = sem("xN_psum"); xN_ready = sem("xN_ready"); cb_psum = sem("cb_psum"); cb_ready = sem("cb_ready")
        qsq_ready = sem("qsq_ready"); qr_ready = sem("qr_ready"); roped_ready = sem("roped_ready")
        qT_psum = sem("qT_psum"); qT_ready = sem("qT_ready")
        seg_psum = sem("seg_psum"); seg_masked = sem("seg_masked"); seg_exp = sem("seg_exp"); g_ready = sem("g_ready")
        sc_psum = sem("sc_psum"); sc_max = sem("sc_max"); sc_exp = sem("sc_exp"); prob_ready = sem("prob_ready")
        probT_psum = sem("probT_psum"); probT_ready = sem("probT_ready")
        o_psum = sem("o_psum"); o_ready = sem("o_ready")
        y_psum = sem("y_psum"); yz_ready = sem("yz_ready"); ysq_ready = sem("ysq_ready"); ysq_added = sem("ysq_added")
        yg_ready = sem("yg_ready")
        gate_ready = sem("gate_ready")
        ssq_psum = sem("ssq_psum"); ssq_ready = sem("ssq_ready"); rB_ready = sem("rB_ready")
        mix_ready = sem("mix_ready"); x1sq_ready = sem("x1sq_ready")
        x1r_ready = sem("x1r_ready"); h2_ready = sem("h2_ready"); h2T_psum = sem("h2T_psum"); h2T_ready = sem("h2T_ready")
        lg_psum = sem("lg_psum"); lmax_ready = sem("lmax_ready"); lexp_ready = sem("lexp_ready")
        w_ready = sem("w_ready"); wT_psum = sem("wT_psum"); wT_ready = sem("wT_ready")
        b2_psum = sem("b2_psum"); route_ready = sem("route_ready")
        p_ready = sem("p_ready"); x_psum = sem("x_psum"); xs_ready = sem("xs_ready")
        ga_ready = sem("ga_ready"); sg_ready = sem("sg_ready"); actT_ready = sem("actT_ready")
        hi_ready = sem("hi_ready"); lo_ready = sem("lo_ready"); hs_ready = sem("hs_ready"); t_psum = sem("t_psum"); pw_psum = sem("pw_psum"); pw_ready = sem("pw_ready")
        hb_ready = sem("hb_ready"); res_ready = sem("res_ready"); ys_ready = sem("ys_ready"); c_psum = sem("c_psum"); c_added = sem("c_added")
        over_full = sem("over_full"); over_place = sem("over_place"); over_x = sem("over_x"); over_xr = sem("over_xr")
        over_h = sem("over_h"); over_ga = sem("over_ga"); over_sg = sem("over_sg"); over_act = sem("over_act")
        over_y = sem("over_y"); over_ys = sem("over_ys"); over_c = sem("over_c"); over_added = sem("over_added")
        over_step = sem("over_step")
        fsq_ready = sem("fsq_ready"); fr_ready = sem("fr_ready"); fin_ready = sem("fin_ready"); sum_done = sem("sum_done")

        def mix_slot(n):
            return n % RING_MIX

        def moe_slot(u):
            return (u + 6) % RING

        def mix_full(eng, n):
            eng.wait_ge(slot_full[mix_slot(n)], 16 * (n // RING_MIX + 1))

        def mix_loads(s):
            return len([n for n in range(N_MIX) if mix_slot(n) == s])

        def moe_full(eng, i, u):
            s = moe_slot(u)
            eng.wait_ge(slot_full[s], 16 * (mix_loads(s) + u // RING + 1) + i * (16 * BODY * EXP_UNITS // RING))

        def unit_used(eng, i, u):
            eng.wait_ge(unit_done, i * (BODY * EXP_UNITS) + (N_MIX + u + 1))

        def split_at(c, n):
            return c * EXP_UNITS + SPLIT[n], c * SPE + n

        def buffer_free(eng, i, c, n):
            r = c * SPE + n - NSPLIT
            c0, n0 = r // SPE, r % SPE
            unit_used(eng, i, c0 * EXP_UNITS + SPLIT[n0])

        def cols(w, c0):
            return w.rearrange("(k p) n -> p k n", p=P)[:, :, c0:c0 + UW]

        def mix_src(n):
            if n < U_Z:
                return cols(w_in[0], XBC0 + n * UW)
            if n < U_K:
                return cols(w_in[0], (n - U_Z) * UW)
            if n == U_K:
                return cols(w_in[0], Q0 + AH * AD)
            if n < U_V:
                return cols(w_in[0], Q0 + (n - U_Q) * UW)
            if n == U_V:
                return cols(w_in[0], Q0 + AH * AD + KVH * AD)
            if n < U_BA:
                return cols(w_in[0], G0 + (n - U_G) * UW)
            if n < U_BS:
                return cols(w_br_attn[0], (n - U_BA) * UW)
            if n < U_O:
                return cols(w_br_ssm[0], (n - U_BS) * UW)
            return cols(w_out[0], (n - U_O) * UW)

        w1v = w_mlp1[0].rearrange("e (k p) n -> e p k n", p=P)
        w2v = w_mlp2[0].rearrange("e (k p) n -> e p k n", p=P)

        def k_view(s):
            return ring[:, s, :].rearrange("p (k n) -> p k n", k=KD)

        def chain(eng, semaphore, base=0):
            n = [0]

            def link(ins):
                n[0] += 1
                ins.then_inc(semaphore, 1)
                eng.wait_ge(semaphore, base + n[0])
            link.count = n
            return link

        block = ctx.enter_context(nc.Block())

        @block.sync
        def _(sp):
            def load_moe(i, u):
                e = i * BODY + u // EXP_UNITS
                q = u % EXP_UNITS
                s = moe_slot(u)
                if q < KD:
                    src = w1v[bass.ds(e, 1), :, q, :].rearrange("a p n -> (a p) n")
                else:
                    k = 2 * (q - KD)
                    src = w2v[bass.ds(e, 1), :, k:k + 2, :].rearrange("a p k n -> (a p) k n")
                dst = ring[:, s, :] if q < KD else ring[:, s, :].rearrange("p (k n) -> p k n", k=2)
                sp.dma_start(dst, src).then_inc(slot_full[s], 16)

            for n in range(N_MIX):
                if n >= RING_MIX:
                    sp.wait_ge(unit_done, n - RING_MIX + 1)
                sp.dma_start(k_view(mix_slot(n)), mix_src(n)).then_inc(slot_full[mix_slot(n)], 16)
            def slot_free(i, u):
                v = u - RING
                c, q = v // EXP_UNITS, v % EXP_UNITS
                if q in DIRECT:
                    unit_used(sp, i, v)
                else:
                    sp.wait_ge(lo_ready, i * (BODY * SPE) + (c * SPE + SPLIT.index(q) + 1))

            for u in range(BODY * EXP_UNITS):
                if u < RING:
                    last_mix = max(n for n in range(N_MIX) if mix_slot(n) == moe_slot(u))
                    sp.wait_ge(unit_done, last_mix + 1)
                else:
                    slot_free(0, u)
                load_moe(0, u)
            with sp.Fori(1, NE // BODY) as i:
                for u in range(BODY * EXP_UNITS):
                    slot_free(i, u)
                    load_moe(i, u)

            sp.wait_ge(route_ready, 1)
            again = sp.value_load(over_i[0:1, 0:1], min_val=0, max_val=1)
            with sp.If(again > 0):
                with sp.Fori(0, NE) as e:
                    for r in range(NPASS - 1):
                        for q in range(EXP_UNITS):
                            if q == 0 and r == 0:
                                sp.wait_ge(over_y, e * (NPASS - 1) + 1)
                            elif q == 0:
                                sp.wait_ge(over_y, e * (NPASS - 1) + (r + 1))
                            if q == KD:
                                sp.wait_ge(over_h, e * (NPASS - 1) + (r + 1))
                            if q < KD:
                                src = w1v[bass.ds(e, 1), :, q, :].rearrange("a p n -> (a p) n")
                                dst = ring[:, q, :]
                            else:
                                k = 2 * (q - KD)
                                src = w2v[bass.ds(e, 1), :, k:k + 2, :].rearrange("a p k n -> (a p) k n")
                                dst = ring[:, q - KD, :].rearrange("p (k n) -> p k n", k=2)
                            sp.dma_start(dst, src).then_inc(over_full, 16)
            sp.wait_ge(fin_ready, 1)
            sp.dma_start(out[0, 0:P, :], hN[:, 0, :]).then_inc(out_done, 16)
            sp.wait_ge(fin_ready, 2)
            sp.dma_start(out[0, P:SEQ, :], hN[:, 1, :]).then_inc(out_done, 16)
            sp.wait_ge(out_done, 32)

        @block.tensor
        def _(pe):
            pe.wait_ge(c_in, 16)
            pe.wait_ge(row_in, 16 * 5)
            pe.wait_ge(dsk_ready, 1)
            nc.tensor.transpose(bank[6][:, 0:N_ROWS], prm[0:N_ROWS, :], ident[0:N_ROWS, 0:N_ROWS])
            nc.tensor.transpose(bank[6][:, N_ROWS:N_ROWS + 8], dske[:, :], ident[0:8, 0:8]).then_inc(prm_ready, 1)
            pe.wait_ge(b1_in, 16)
            for m in range(16):
                last = nc.tensor.transpose(bank[7][:, m * NE:(m + 1) * NE], b1raw[:, m * P:(m + 1) * P],
                                           ident[0:NE, 0:NE])
            last.then_inc(prm_ready, 1)

            def to_T(ready, psum_sem):
                pe.wait_ge(ready, 2)
                for b in range(4):
                    for kk in range(2):
                        for t in range(TT):
                            k = 2 * b + kk
                            last = nc.tensor.transpose(bank[2 + b][:, kk * 256 + t * P:kk * 256 + (t + 1) * P],
                                                       hN[:, t, k * P:(k + 1) * P], ident)
                    last.then_inc(psum_sem, 1)

            to_T(h_ready, hT_psum)

            def unit(n, rhs=None, tokens=None):
                mix_full(pe, n)
                if n >= 2:
                    pe.wait_ge(unit_taken, n - 1)
                w = k_view(mix_slot(n))
                for a in range(2):
                    for k in range(KD):
                        o = bank[n % 2][:, a * 256:(a + 1) * 256]
                        if tokens is None:
                            last = nc.tensor.matmul(o, w[:, k, a * P:(a + 1) * P], rhs[:, k, :],
                                                    start=(k == 0), stop=(k == KD - 1))
                        else:
                            last = nc.tensor.matmul(o, tokens[:, k, a * P:(a + 1) * P], w[:, k, :],
                                                    start=(k == 0), stop=(k == KD - 1))
                last.then_inc(unit_done, 1)

            pe.wait_ge(hT_ready, 4)
            for n in range(U_XBC, U_Z):
                unit(n, rhs=hT)
            pe.wait_ge(wdt_in, 16)
            pe.wait_ge(prm_taken, 2)
            for t in range(TT):
                for k in range(KD):
                    last = nc.tensor.matmul(bank[6][:, t * 32:(t + 1) * 32], hT[:, k, t * P:(t + 1) * P], wdt[:, k, :],
                                            start=(k == 0), stop=(k == KD - 1))
            last.then_inc(dt_psum, 1)
            for n in range(U_Z, U_K):
                unit(n, rhs=hT)
            pe.wait_ge(silu_done, 4)
            for b in range(4):
                t = b // 2
                for jj in range(4):
                    j = (b % 2) * 4 + jj
                    last = nc.tensor.transpose(bank[2 + b][:, jj * P:(jj + 1) * P], xbcT[:, j, t * P:(t + 1) * P], ident)
                last.then_inc(xN_psum, 1)
            pe.wait_ge(silu_done, 6)
            pe.wait_ge(dt_in, 1)
            for g in range(2):
                for i in range(TT):
                    last = nc.tensor.matmul(bank[6 + g][:, i * 256:(i + 1) * 256], xbcT[:, 8 + g, i * P:(i + 1) * P],
                                            xbcT[:, 10 + g, :], start=True, stop=True)
                last.then_inc(cb_psum, 1)

            unit(U_K, tokens=hT)
            pe.wait_ge(a_ready, 1)
            pe.wait_ge(cb_ready, 2)
            f, b_ = slice(0, NH), slice(NH, 2 * NH)
            nc.tensor.matmul(bank[7][:, 0:16], m_le, dta[:, 0, f], start=True, stop=True)
            nc.tensor.matmul(bank[7][:, 16:32], ones, dta[:, 1, b_], start=True, stop=False)
            nc.tensor.matmul(bank[7][:, 16:32], m_ge, dta[:, 0, b_], start=False, stop=True)
            nc.tensor.matmul(bank[7][:, 32:48], ones, dta[:, 0, f], start=True, stop=False)
            nc.tensor.matmul(bank[7][:, 32:48], m_le, dta[:, 1, f], start=False, stop=True)
            nc.tensor.matmul(bank[7][:, 48:64], m_ge, dta[:, 1, b_], start=True, stop=True).then_inc(acs_psum, 1)
            unit(U_Q, tokens=hT)
            pe.wait_ge(acsN_ready, 2)
            for t in range(TT):
                last = nc.tensor.transpose(bank[7][0:32, 256 + t * P:256 + (t + 1) * P], acsN[:, t, :], ident)
            last.then_inc(acsT_psum, 1)

            def qk_transposes(v):
                pe.wait_ge(roped_ready, v + 1)
                if v == 4:
                    pe.wait_ge(qT_ready, 1)
                for hh in range(2):
                    for t in range(TT):
                        last = nc.tensor.transpose(bank[2 + v % 4][:, hh * 256 + t * P:hh * 256 + (t + 1) * P],
                                                   roped[:, t, v * 256 + hh * P:v * 256 + (hh + 1) * P], ident)
                last.then_inc(qT_psum, 1)

            pe.wait_ge(xN_ready, 4)
            qk_transposes(0)
            for v in range(1, 4):
                unit(U_Q + v, tokens=hT)
                qk_transposes(v)
            unit(U_V, tokens=hT)
            qk_transposes(4)

            def seg(g):
                for hh in range(2):
                    h = 2 * g + hh
                    if h >= 2:
                        pe.wait_ge(seg_masked, h - 1)
                    for d in range(2):
                        r = d * NH + h
                        last = nc.tensor.matmul(bank[2 + hh][:, d * 256:(d + 1) * 256],
                                                ident[0:32, r:r + 1].to_broadcast([32, P]), acsT[:, :],
                                                start=True, stop=True)
                    last.then_inc(seg_psum, 1)

            def scores(h):
                if h >= 1:
                    pe.wait_ge(sc_exp, h)
                for t in range(TT):
                    last = nc.tensor.matmul(bank[4][:, t * 256:(t + 1) * 256], qT[:, h, t * P:(t + 1) * P],
                                            kT[:, h // (AH // KVH), :], start=True, stop=True)
                last.then_inc(sc_psum, 1)

            pe.wait_ge(qT_ready, 5)
            pe.wait_ge(acsT_ready, 1)
            seg(0)
            scores(0)
            for g in range(8):
                unit(U_G + g, rhs=hT)
                pe.wait_ge(prob_ready, g + 1)
                if g >= 1:
                    pe.wait_ge(probT_ready, g)
                for i in range(TT):
                    for t in range(TT):
                        last = nc.tensor.transpose(bank[5][:, i * 256 + t * P:i * 256 + (t + 1) * P],
                                                   prob[:, t, i * P:(i + 1) * P], ident)
                last.then_inc(probT_psum, 1)
                if g < 7:
                    seg(g + 1)
                    scores(g + 1)
                if g >= 1:
                    pe.wait_ge(yz_ready, 2 * g - 1)
                for hh in range(2):
                    pe.wait_ge(g_ready, 2 * g + hh + 1)
                    for i in range(TT):
                        last = nc.tensor.matmul(bank[7][hh * HD:(hh + 1) * HD, 0:256],
                                                hN[:, i, (2 * g + hh) * HD:(2 * g + hh + 1) * HD],
                                                gbuf[:, g % 2, hh, i, :], start=(i == 0), stop=(i == TT - 1))
                last.then_inc(y_psum, 1)
                pe.wait_ge(probT_ready, g + 1)
                if g >= 1:
                    pe.wait_ge(o_ready, g)
                for i in range(TT):
                    kv = g // (AH // KVH)
                    last = nc.tensor.matmul(bank[6][:, 0:256], vN[:, i, kv * AD:(kv + 1) * AD], probT[:, i, :],
                                            start=(i == 0), stop=(i == TT - 1))
                last.then_inc(o_psum, 1)

            pe.wait_ge(o_ready, 8)
            for n in range(U_BA, U_BS):
                unit(n, rhs=qT)
            pe.wait_ge(ysq_added, 8)
            nc.tensor.matmul(bank[7][:, 256:512], ones, sqacc, start=True, stop=True).then_inc(ssq_psum, 1)
            pe.wait_ge(yg_ready, 8)
            for n in range(U_BS, U_O):
                unit(n, rhs=xbcT)
            pe.wait_ge(mix_ready, 4)
            for n in range(U_O, N_MIX):
                unit(n, tokens=hT)

            to_T(h2_ready, h2T_psum)
            pe.wait_ge(h2T_ready, 4)
            pe.wait_ge(late_in, 16 * 2)
            for t in range(TT):
                for k in range(KD):
                    last = nc.tensor.matmul(bank[6][:, t * NE:(t + 1) * NE], hT[:, k, t * P:(t + 1) * P], wr[:, k, :],
                                            start=(k == 0), stop=(k == KD - 1))
            last.then_inc(lg_psum, 1)
            pe.wait_ge(w_ready, 1)
            nc.tensor.matmul(bank[7][:, 0:NE], m_le, msk[:, 0, :], start=True, stop=True)
            nc.tensor.matmul(bank[7][:, NE:2 * NE], ones, msk[:, 0, :], start=True, stop=False)
            nc.tensor.matmul(bank[7][:, NE:2 * NE], m_le, msk[:, 1, :], start=False, stop=True)
            nc.tensor.matmul(bank[7][:, 2 * NE:3 * NE], ones, msk[:, 0, :], start=True, stop=False)
            nc.tensor.matmul(bank[7][:, 2 * NE:3 * NE], ones, msk[:, 1, :], start=False, stop=True)
            pe.wait_ge(w_ready, 2)
            for t in range(TT):
                last = nc.tensor.transpose(bank[0][0:NE, t * P:(t + 1) * P], wtok[:, t, 0:NE], ident)
            last.then_inc(wT_psum, 1)
            pe.wait_ge(wT_ready, 1)
            for t in range(TT):
                for hf in range(2):
                    nc.tensor.matmul(bank[2 + 2 * t + hf][:, :], wT[:, t * P:(t + 1) * P], b2s[:, hf * 512:(hf + 1) * 512],
                                     start=True, stop=True).then_inc(b2_psum, 1)

            def gather(par):
                for k in range(KD):
                    for t in range(TT):
                        for part in (2, 1, 0):
                            last = nc.tensor.matmul(bank[6][:, k * CAP:(k + 1) * CAP], hb[part][:, t, k * P:(k + 1) * P],
                                                    slotP[:, par, t, :], start=(t == 0 and part == 2),
                                                    stop=(t == TT - 1 and part == 0))
                return last

            def slot_transposes(par):
                for t in range(TT):
                    last = nc.tensor.transpose(bank[7][:, t * P:(t + 1) * P], slotW[:, par, t, :], ident)
                return last

            def combine(q, rows):
                return nc.tensor.matmul(bank[q][:, :], slotWT[0:rows, (q // 2) * P:(q // 2 + 1) * P],
                                        ysb[0:rows, (q % 2) * 512:(q % 2 + 1) * 512], start=True, stop=True)

            def layer_unit(i, c, q, tokens, tokens32, banks, first, last_k):
                u = c * EXP_UNITS + q
                nb = len(banks)
                tiles = UNIT // (512 * nb)
                k0 = q if tiles == 1 else 2 * (q - KD)
                if q in DIRECT:
                    moe_full(pe, i, u)
                    w = ring[:, moe_slot(u), :]
                    for a in range(tiles):
                        for n, b in enumerate(banks):
                            o = (a * nb + n) * 512
                            last = nc.tensor.matmul(bank[b][0:CAP, :], tokens32[:, k0 + a, :], w[:, o:o + 512],
                                                    start=False, stop=False, skip_group_check=True)
                else:
                    _, sn = split_at(c, SPLIT.index(q))
                    for part, ready in ((0, hi_ready), (1, lo_ready)):
                        pe.wait_ge(ready, i * (BODY * SPE) + (sn + 1))
                        for a in range(tiles):
                            for n, b in enumerate(banks):
                                o = (a * nb + n) * 512
                                last = nc.tensor.matmul(
                                    bank[b][:, :], tokens[:, k0 + a, :], split[:, sn % NSPLIT, part, o:o + 512],
                                    start=(q == first and a == 0 and part == 0),
                                    stop=(q == last_k and a == tiles - 1 and part == 1), skip_group_check=True)
                last.then_inc(unit_done, 1)

            def sum_transposed(n):
                for m in range(4 * n, 4 * n + 4):
                    last = nc.tensor.matmul(bank[4 + m // 8][:, (m % 8) * CAP:(m % 8 + 1) * CAP], hs[:, m * P:(m + 1) * P],
                                            sum_id, start=True, stop=True)
                return last

            def expert(i, c, final):
                e = i * BODY + c
                pe.wait_ge(xs_ready, e + 1)
                pe.wait_ge(c_added, e * 4 + 1)
                for q in range(KD):
                    layer_unit(i, c, q, xs, x32, (0, 1, 2, 3), 0, KD - 1)
                if not final:
                    pe.wait_ge(p_ready, e + 2)
                    gather((c + 1) % 2).then_inc(x_psum, 1)
                for n in range(4):
                    pe.wait_ge(hs_ready, e * 4 + (n + 1))
                    last = sum_transposed(n)
                last.then_inc(t_psum, 1)
                pe.wait_ge(ys_ready, e + 1)
                for q in range(4):
                    last = combine(q, P)
                last.then_inc(c_psum, 1)
                slot_transposes(c % 2).then_inc(pw_psum, 1)
                pe.wait_ge(actT_ready, e + 1)
                for q in range(KD, EXP_UNITS):
                    layer_unit(i, c, q, as_, act32, (4, 5), KD, EXP_UNITS - 1)

            pe.wait_ge(p_ready, 1)
            pe.wait_ge(hb_ready, 3)
            gather(0).then_inc(x_psum, 1)
            with pe.Fori(0, NE // BODY - 1) as i:
                for c in range(BODY):
                    expert(i, c, False)
            for c in range(BODY):
                expert(NE // BODY - 1, c, c == BODY - 1)
            pe.wait_ge(ys_ready, 1 + NE)
            pe.wait_ge(pw_ready, NE)
            pe.wait_ge(c_added, 4 * NE + 1)
            for q in range(4):
                last = combine(q, P)
            last.then_inc(c_psum, 1)

            pe.wait_ge(route_ready, 1)
            again = pe.value_load(over_i[0:1, 0:1], min_val=0, max_val=1)
            with pe.If(again > 0):
                pe.wait_ge(c_added, 4 * NE + 5)
                nc.tensor.transpose(bank[7][:, 0:P], ident, ident).then_inc(over_y, 1)
                with pe.Fori(0, NE) as e:
                    for r in range(NPASS - 1):
                        n = e * (NPASS - 1) + (r + 1)
                        pe.wait_ge(over_place, n)
                        gather(0)
                        slot_transposes(0).then_inc(over_x, 1)
                        pe.wait_ge(over_xr, n)
                        pe.wait_ge(over_full, n * (16 * EXP_UNITS) - 16 * (EXP_UNITS - KD))
                        for k in range(KD):
                            for m in range(16):
                                last = nc.tensor.matmul(bank[4 + m // 8][:, (m % 8) * CAP:(m % 8 + 1) * CAP],
                                                        ring[:, k, m * P:(m + 1) * P], x32[:, k, :],
                                                        start=(k == 0 and m % 8 == 0), stop=(k == KD - 1 and m % 8 == 7),
                                                        skip_group_check=True)
                        last.then_inc(over_h, 1)
                        pe.wait_ge(over_act, n)
                        pe.wait_ge(over_full, n * (16 * EXP_UNITS))
                        for k in range(KD):
                            for hf in range(2):
                                o = (k % 2) * D + hf * 512
                                last = nc.tensor.matmul(bank[hf][0:CAP, :], act32[:, k, :], ring[:, k // 2, o:o + 512],
                                                        start=(k == 0), stop=(k == KD - 1))
                        last.then_inc(over_y, 1)
                        pe.wait_ge(over_ys, n)
                        for q in range(4):
                            last = combine(q, CAP)
                        last.then_inc(over_c, 1)

        @block.scalar
        def _(act):
            link = chain(act, act_step)
            act.dma_start(xres[:, :, :], x[0].rearrange("(t p) d -> p t d", p=P)).then_inc(x_in, 16)
            act.dma_start(cst[:, :], consts).then_inc(c_in, 16)
            for r, src in ((R_GMIX, g_mix[0].rearrange("(k p) -> k p", p=P)), (R_GSSM, g_ssm[0].rearrange("(k p) -> k p", p=P)),
                           (R_GFFN, g_ffn[0].rearrange("(k p) -> k p", p=P)), (R_CB, conv_b[0].rearrange("(k p) -> k p", p=P)),
                           (R_CW, conv_w[0].rearrange("j (k p) -> (j k) p", p=P))):
                act.dma_start(prm[r:r + src.shape[0], :], src).then_inc(row_in, 16)
            act.dma_start(dskr[:, :], d_skip[0].rearrange("(j h) -> j h", h=2)).then_inc(dsk_in, 16)
            act.dma_start(b1raw, b_mlp1[0]).then_inc(b1_in, 16)
            act.dma_start(wdt[:, :, :], w_in[0].rearrange("(k p) n -> p k n", p=P)[:, :, DT0:DT0 + 2 * NH]).then_inc(wdt_in, 16)
            at = 0
            for v in (dt_bias_f, dt_bias_b, a_log_f, a_log_b, b_router, k_norm_g, q_norm_g):
                act.dma_start(vec[:, at:at + v.shape[1]], v[0].partition_broadcast(P)).then_inc(vec_in, 16)
                at += v.shape[1]
            act.dma_start(wr[:, :, :], w_router[0].rearrange("(k p) n -> p k n", p=P)).then_inc(late_in, 16)

            act.wait_ge(x_in, 16)
            for t in range(TT):
                nc.scalar.activation(hN[:, t, :], xres[:, t, :], ACT.Square, accum_out=stat[:, t:t + 1]).then_inc(xsq_ready, 1)
            act.wait_ge(prm_ready, 1)
            nc.scalar.activation(prmT[:, :], bank[6][:, 0:N_ROWS + 8], ACT.Copy).then_inc(prm_taken, 1)
            act.wait_ge(prm_ready, 2)
            nc.scalar.activation(b1T[:, :, :], bank[7][:, :].rearrange("p (m e) -> p e m", m=16), ACT.Copy).then_inc(prm_taken, 1)

            def silu(u):
                act.wait_ge(conv_done, u + 1)
                nc.scalar.activation(xbcT[:, 2 * u:2 * u + 2, :], xbcT[:, 2 * u:2 * u + 2, :], ACT.Silu).then_inc(silu_done, 1)

            for u in range(6):
                act.wait_ge(unit_done, U_XBC + u + 1)
                if u >= 2:
                    act.wait_ge(conv_done, u - 1)
                else:
                    act.wait_ge(pool_step, 1)
                nc.scalar.activation(xp[:, u % 2, :, PAD:PAD + SEQ], bank[(U_XBC + u) % 2][:, :].rearrange("p (m l) -> p m l", m=2),
                                     ACT.Copy).then_inc(unit_taken, 1)
                if u >= 1:
                    silu(u - 1)
            silu(5)
            for u in range(4):
                act.wait_ge(unit_done, U_Z + u + 1)
                nc.scalar.activation(siluz[:, 2 * u:2 * u + 2, :], bank[(U_Z + u) % 2][:, :].rearrange("p (m l) -> p m l", m=2),
                                     ACT.Silu).then_inc(unit_taken, 1)
            for b in range(4):
                act.wait_ge(xN_psum, b + 1)
                t = b // 2
                nc.scalar.activation(hN[:, t, (b % 2) * 512:(b % 2 + 1) * 512], bank[2 + b][:, :], ACT.Copy).then_inc(xN_ready, 1)
            for g in range(2):
                act.wait_ge(cb_psum, g + 1)
                nc.scalar.activation(cb[:, g, :, :], bank[6 + g][:, :].rearrange("p (i l) -> p i l", i=TT), ACT.Copy).then_inc(cb_ready, 1)
            act.wait_ge(dt_in, 1)
            act.wait_ge(vec_in, 16 * 7)
            nc.scalar.activation(dtu[:, :, :], dta[:, :, :], ACT.Exp, scale=-1.0).then_inc(dt_exp, 1)
            nc.scalar.activation(alog_b, alog_b, ACT.Exp).then_inc(dt_exp, 1)

            def qk_square(v, n):
                act.wait_ge(unit_done, n + 1)
                nc.scalar.activation(qk[:, :, v * 256:(v + 1) * 256], bank[n % 2][:, :].rearrange("p (t c) -> p t c", t=TT),
                                     ACT.Copy).then_inc(unit_taken, 1)
                act.wait_ge(unit_taken, n + 1)
                nc.scalar.activation(roped[:, :, v * 256:(v + 1) * 256], qk[:, :, v * 256:(v + 1) * 256], ACT.Square).then_inc(qsq_ready, 1)

            def qT_copy(v):
                act.wait_ge(qT_psum, v + 1)
                dst = kT if v == 0 else qT[:, 2 * v - 2:2 * v, :]
                nc.scalar.activation(dst, bank[2 + v % 4][:, :].rearrange("p (h l) -> p h l", h=2), ACT.Copy).then_inc(qT_ready, 1)

            qk_square(0, U_K)
            qk_square(1, U_Q)
            act.wait_ge(acsT_psum, 1)
            nc.scalar.activation(acsT[:, :], bank[7][0:32, 256:512], ACT.Copy).then_inc(acsT_ready, 1)
            for v in range(2, 5):
                qk_square(v, U_Q + v - 1)
                qT_copy(v - 2)
            qT_copy(3)
            act.wait_ge(unit_done, U_V + 1)
            nc.scalar.activation(vN[:, :, :], bank[U_V % 2][:, :].rearrange("p (t c) -> p t c", t=TT), ACT.Copy).then_inc(unit_taken, 1)
            qT_copy(4)

            def seg_exps(g):
                for hh in range(2):
                    act.wait_ge(seg_masked, 2 * g + hh + 1)
                    nc.scalar.activation(ebuf[:, hh, :], ebuf[:, hh, :], ACT.Exp).then_inc(seg_exp, 1)

            def score_exps(h):
                act.wait_ge(sc_max, h + 1)
                if h >= 1:
                    act.wait_ge(probT_psum, h)
                for t in range(TT):
                    last = nc.scalar.activation(prob[:, t, :], bank[4][:, t * 256:(t + 1) * 256], ACT.Exp,
                                                bias=stat[:, 12 + t:13 + t], scale=float(AD) ** -0.5,
                                                accum_out=stat[:, 14 + t:15 + t])
                last.then_inc(sc_exp, 1)

            score_exps(0)
            seg_exps(0)
            for g in range(8):
                act.wait_ge(unit_done, U_G + g + 1)
                nc.scalar.activation(sig[:, 2 * g:2 * g + 2, :], bank[(U_G + g) % 2][:, :].rearrange("p (m l) -> p m l", m=2),
                                     ACT.Exp, scale=-1.0).then_inc(unit_taken, 1)
                act.wait_ge(probT_psum, g + 1)
                if g >= 1:
                    act.wait_ge(o_psum, g)
                nc.scalar.activation(probT[:, :, :], bank[5][:, :].rearrange("p (i q) -> p i q", i=TT), ACT.Copy).then_inc(probT_ready, 1)
                if g < 7:
                    score_exps(g + 1)
                    seg_exps(g + 1)
                act.wait_ge(o_psum, g + 1)
                nc.scalar.activation(qT[:, g, :], bank[6][:, 0:256], ACT.Copy).then_inc(o_ready, 1)
                act.wait_ge(yz_ready, 2 * g + 2)
                if g >= 1:
                    act.wait_ge(ysq_added, g)
                nc.scalar.activation(sqb, xbcT[:, g, :], ACT.Square).then_inc(ysq_ready, 1)
                nc.scalar.activation(xbcT[:, g, :], xbcT[:, g, :], ACT.Copy, scale=prmT[:, R_GSSM + g:R_GSSM + g + 1]).then_inc(yg_ready, 1)
            act.dma_start(b2s, b_mlp2[0]).then_inc(late_in, 16)
            act.wait_ge(ssq_psum, 1)
            nc.scalar.activation(rB, bank[7][:, 256:512], ACT.Copy, bias=EPS, scale=1.0 / D).then_inc(ssq_ready, 1)
            def hi_split(i, c, n):
                u, sn = split_at(c, n)
                moe_full(act, i, u)
                nc.scalar.activation(split[:, sn % NSPLIT, 0, :], ring[:, moe_slot(u), :], ACT.Copy).then_inc(hi_ready, 1)

            act.wait_ge(unit_done, U_O)
            act.wait_ge(mix_ready, 4)
            for n in range(NSPLIT):
                hi_split(0, 0, n)
            act.wait_ge(unit_taken, N_MIX)
            for t in range(TT):
                nc.scalar.activation(hN[:, t, :], xres[:, t, :], ACT.Square, accum_out=stat[:, 20 + t:21 + t]).then_inc(x1sq_ready, 1)
            act.wait_ge(h2_ready, 2)
            nc.scalar.activation(hb1[:, :, :], hN[:, :, :], ACT.Copy).then_inc(hb_ready, 1)
            act.wait_ge(res_ready, 1)
            nc.scalar.activation(hb2[:, :, :], hs, ACT.Copy).then_inc(hb_ready, 1)
            act.wait_ge(lmax_ready, 1)
            for t in range(TT):
                last = nc.scalar.activation(lgt[:, t, :], lgt[:, t, :], ACT.Exp, bias=stat[:, 26 + t:27 + t])
            last.then_inc(lexp_ready, 1)
            act.wait_ge(res_ready, 2)
            act.wait_ge(wT_psum, 1)
            nc.scalar.activation(wT[:, :], bank[0][0:NE, 0:SEQ], ACT.Copy).then_inc(wT_ready, 1)
            act.wait_ge(wT_ready, 1)
            act.dma_start(gfin, g_final.partition_broadcast(P)).then_inc(gfin_in, 16)

            act.wait_ge(b2_psum, 4)
            nc.scalar.activation(hb3[:, :, :], hs, ACT.Copy).then_inc(hb_ready, 1)

            def expert(i, c, final):
                e = i * BODY + c
                for n in range(NSPLIT, SPE):
                    buffer_free(act, i, c, n)
                    hi_split(i, c, n)
                unit_used(act, i, c * EXP_UNITS + KD - 1)
                for n in range(4):
                    nc.scalar.activation(hs[:, n * 512:(n + 1) * 512], bank[n][:, :], ACT.Copy).then_inc(hs_ready, 1)
                if not final:
                    buffer_free(act, i, c + 1, 0)
                    hi_split(i, c + 1, 0)
                act.wait_ge(ga_ready, e + 1)
                nc.scalar.activation(sg, ga, ACT.Sigmoid, scale=ALPHA).then_inc(sg_ready, 1)
                act.wait_ge(pw_psum, e + 1)
                nc.scalar.activation(slotWT, bank[7][:, 0:256], ACT.Copy).then_inc(pw_ready, 1)
                if not final:
                    for n in (1, 2):
                        buffer_free(act, i, c + 1, n)
                        hi_split(i, c + 1, n)
                unit_used(act, i, c * EXP_UNITS + EXP_UNITS - 1)
                nc.scalar.activation(ysb[:, 0:512], bank[4][:, :], ACT.Copy)
                nc.scalar.activation(ysb[:, 512:1024], bank[5][:, :], ACT.Copy).then_inc(ys_ready, 1)
                if not final:
                    buffer_free(act, i, c + 1, 3)
                    hi_split(i, c + 1, 3)

            with act.Fori(0, NE // BODY - 1) as i:
                for c in range(BODY):
                    expert(i, c, False)
            for c in range(BODY):
                expert(NE // BODY - 1, c, c == BODY - 1)

            act.wait_ge(route_ready, 1)
            again = act.value_load(over_i[0:1, 0:1], min_val=0, max_val=1)
            with act.If(again > 0):
                with act.Fori(0, NE) as e:
                    for r in range(NPASS - 1):
                        n = e * (NPASS - 1) + (r + 1)
                        act.wait_ge(over_x, n)
                        nc.scalar.activation(slotWT, bank[7][:, 0:256], ACT.Copy)
                        act.wait_ge(over_ga, n)
                        nc.scalar.activation(sg, ga, ACT.Sigmoid, scale=ALPHA).then_inc(over_sg, 1)
                        act.wait_ge(over_y, n + 1)
                        nc.scalar.activation(ysb[0:CAP, 0:512], bank[0][0:CAP, :], ACT.Copy)
                        nc.scalar.activation(ysb[0:CAP, 512:1024], bank[1][0:CAP, :], ACT.Copy).then_inc(over_ys, 1)

            act.wait_ge(sum_done, 1)
            for t in range(TT):
                nc.scalar.activation(hN[:, t, :], xres[:, t, :], ACT.Square, accum_out=stat[:, 30 + t:31 + t]).then_inc(fsq_ready, 1)

        @block.gpsimd
        def _(pool):
            link = chain(pool, pool_step)
            link(nc.gpsimd.memset(xp, 0.0))
            nc.gpsimd.memset(stat[:, 40:64], -0.5).then_inc(pool_step, 1)
            nc.gpsimd.memset(sqacc, 0.0).then_inc(pool_step, 1)
            pool.wait_ge(pool_step, 3)
            link.count[0] = 3

            def rsqrt_mean(o, n, count):
                link(nc.gpsimd.tensor_scalar(stat[:, o:o + n], stat[:, o:o + n], 1.0 / count, EPS, ALU.mult, ALU.add))
                return nc.gpsimd.tensor_tensor(stat[:, o:o + n], stat[:, o:o + n], stat[:, 40:40 + n], ALU.pow)

            pool.wait_ge(xsq_ready, 2)
            rsqrt_mean(0, TT, D).then_inc(xr_ready, 1)
            for v in range(5):
                pool.wait_ge(qr_ready, 2 * v + 1)
                rsqrt_mean(4, 4, AD).then_inc(qr_ready, 1)
            for g in range(8):
                pool.wait_ge(ysq_ready, g + 1)
                nc.gpsimd.tensor_tensor(sqacc, sqacc, sqb, ALU.add).then_inc(ysq_added, 1)
                pool.wait_ge(ysq_added, g + 1)
            pool.wait_ge(ssq_ready, 1)
            nc.gpsimd.tensor_tensor(rB, rB, stat[:, 40:41].to_broadcast([P, 256]), ALU.pow).then_inc(rB_ready, 1)
            pool.wait_ge(x1sq_ready, 2)
            rsqrt_mean(20, TT, D).then_inc(x1r_ready, 1)
            pool.wait_ge(fsq_ready, 2)
            rsqrt_mean(30, TT, D).then_inc(fr_ready, 1)

        @block.vector
        def _(dve):
            link = chain(dve, dve_step)
            V = nc.vector
            dve.wait_ge(dsk_in, 16)
            V.tensor_copy(dske[:, :].rearrange("j (h p) -> j h p", h=2),
                          dskr[:, :].unsqueeze(2).to_broadcast([8, 2, HD])).then_inc(dsk_ready, 1)
            dve.wait_ge(xr_ready, 1)
            for t in range(TT):
                V.tensor_scalar(hN[:, t, :], xres[:, t, :], stat[:, t:t + 1], None, ALU.mult).then_inc(h_ready, 1)
            dve.wait_ge(prm_taken, 1)

            def scaled_T(psum_sem, ready, row):
                for b in range(4):
                    dve.wait_ge(psum_sem, b + 1)
                    V.tensor_tensor(hT[:, 2 * b:2 * b + 2, :], bank[2 + b][:, :].rearrange("p (k l) -> p k l", k=2),
                                    prmT[:, row + 2 * b:row + 2 * b + 2].unsqueeze(2).to_broadcast([P, 2, SEQ]), ALU.mult).then_inc(ready, 1)

            scaled_T(hT_psum, hT_ready, R_GMIX)
            for u in range(6):
                dve.wait_ge(unit_taken, U_XBC + u + 1)
                for j in range(CONV):
                    for mm in range(2):
                        m = 2 * u + mm
                        wcol = prmT[:, R_CW + j * XBC_TILES + m:R_CW + j * XBC_TILES + m + 1]
                        src = xp[:, u % 2, mm, j:j + SEQ]
                        if j == 0:
                            last = V.tensor_scalar(xbcT[:, m, :], src, wcol, prmT[:, R_CB + m:R_CB + m + 1], ALU.mult, ALU.add)
                        else:
                            last = V.scalar_tensor_tensor(xbcT[:, m, :], src, wcol, xbcT[:, m, :], ALU.mult, ALU.add)
                    if j < CONV - 1:
                        link(last)
                last.then_inc(conv_done, 1)
            dve.wait_ge(dt_psum, 1)
            dve.wait_ge(vec_in, 16 * 7)
            link(V.tensor_tensor(dtv[:, :, :], bank[6][:, 0:64].rearrange("p (t c) -> p t c", t=TT),
                                 dtb_b.unsqueeze(1).to_broadcast([P, TT, 32]), ALU.add))
            V.scalar_tensor_tensor(dta[:, :, :], dtv[:, :, :], -1.0, dtv[:, :, :], ALU.mult, ALU.max).then_inc(dt_in, 1)
            dve.wait_ge(dt_exp, 2)
            link(V.tensor_scalar(dta[:, :, :], dtu[:, :, :], 2.0, None, ALU.add))
            link(V.reciprocal(dta[:, :, :], dta[:, :, :]))
            link(V.tensor_tensor(dtu[:, :, :], dtu[:, :, :], dta[:, :, :], ALU.mult))
            link(V.tensor_tensor(acsN[:, :, :], dtu[:, :, :], dtu[:, :, :], ALU.mult))
            link(V.tensor_scalar(dta[:, :, :], acsN[:, :, :], 1.0 / 19, None, ALU.mult))
            for k in range(17, 1, -2):
                link(V.scalar_tensor_tensor(dta[:, :, :], dta[:, :, :], 1.0 / k, acsN[:, :, :], ALU.add, ALU.mult))
            link(V.scalar_tensor_tensor(dta[:, :, :], dta[:, :, :], 1.0, dtu[:, :, :], ALU.add, ALU.mult))
            link(V.tensor_scalar(dtv[:, :, :], dtv[:, :, :], 0.0, None, ALU.max))
            link(V.scalar_tensor_tensor(dtv[:, :, :], dta[:, :, :], 2.0, dtv[:, :, :], ALU.mult, ALU.add))
            V.scalar_tensor_tensor(dta[:, :, :], dtv[:, :, :], -1.0, alog_b.unsqueeze(1).to_broadcast([P, TT, 32]),
                                   ALU.mult, ALU.mult).then_inc(a_ready, 1)

            def rope(v):
                raw = qk[:, :, v * 256:(v + 1) * 256].rearrange("p t (h d) -> p t h d", h=2)
                new = roped[:, :, v * 256:(v + 1) * 256].rearrange("p t (h d) -> p t h d", h=2)
                tmp = ropeb[:, :, :].rearrange("p t (h d) -> p t h d", h=2)
                ss = stat[:, 4:8].rearrange("p (t h) -> p t h", t=TT)
                dve.wait_ge(qsq_ready, v + 1)
                V.tensor_reduce(ss, new, AXX, ALU.add).then_inc(qr_ready, 1)
                dve.wait_ge(qr_ready, 2 * v + 2)
                link(V.tensor_tensor(raw, raw, ss.unsqueeze(3).to_broadcast([P, TT, 2, AD]), ALU.mult))
                gb = (kg_b if v == 0 else qg_b).unsqueeze(1).unsqueeze(1).to_broadcast([P, TT, 2, AD])
                link(V.tensor_tensor(raw, raw, gb, ALU.mult))
                for t in range(TT):
                    cosv = cst[:, C_COS + t * AD:C_COS + (t + 1) * AD].unsqueeze(1).to_broadcast([P, 2, AD])
                    V.tensor_tensor(new[:, t], raw[:, t], cosv, ALU.mult)
                    for hf in range(2):
                        o = hf * 32
                        sn = cst[:, C_SIN + t * AD:C_SIN + (t + 1) * AD].rearrange("p (a c) -> p a c", a=2)[:, :, o:o + 32]
                        last = V.tensor_tensor(tmp[:, t].rearrange("p h (a c) -> p h a c", a=2)[:, :, :, o:o + 32],
                                               raw[:, t].rearrange("p h (a c) -> p h a c", a=2)[:, :, :, 32 - o:64 - o],
                                               sn.unsqueeze(1).to_broadcast([P, 2, 2, 32]), ALU.mult)
                link(last)
                V.tensor_tensor(new, new, tmp, ALU.add).then_inc(roped_ready, 1)

            rope(0)
            dve.wait_ge(acs_psum, 1)
            V.tensor_copy(acsN[:, :, :], bank[7][:, 0:64].rearrange("p (t c) -> p t c", t=TT)).then_inc(acsN_ready, 1)
            V.tensor_scalar(nacs[:, :, :], bank[7][:, 0:64].rearrange("p (t c) -> p t c", t=TT), -1.0, None, ALU.mult).then_inc(acsN_ready, 1)
            for v in range(1, 5):
                rope(v)

            def seg_mask(g):
                for hh in range(2):
                    h = 2 * g + hh
                    dve.wait_ge(seg_psum, h + 1)
                    e, b = ebuf[:, hh, :], bank[2 + hh]
                    f0, b0 = nacs[:, 0, h:h + 1], nacs[:, 0, NH + h:NH + h + 1]
                    f1, b1 = nacs[:, 1, h:h + 1], nacs[:, 1, NH + h:NH + h + 1]
                    V.scalar_tensor_tensor(e[:, 0:256], b[:, 0:256], f0, cst[:, C_NEGF:C_NEGF + 256], ALU.add, ALU.add)
                    V.scalar_tensor_tensor(e[:, 256:384], b[:, 256:384], b0, cst[:, C_NEGB:C_NEGB + P], ALU.add, ALU.add)
                    V.scalar_tensor_tensor(e[:, 384:512], b[:, 128:256], f1, cst[:, C_NEGF:C_NEGF + P], ALU.add, ALU.add)
                    V.scalar_tensor_tensor(e[:, 512:768], b[:, 256:512], b1, cst[:, C_ZERO:C_ZERO + 256], ALU.add, ALU.add).then_inc(seg_masked, 1)

            def seg_weight(g):
                if g >= 2:
                    dve.wait_ge(y_psum, g - 1)
                for hh in range(2):
                    h = 2 * g + hh
                    dve.wait_ge(seg_exp, h + 1)
                    e, o = ebuf[:, hh, :], gbuf[:, g % 2, hh, :, :]
                    f0, b0 = dtv[:, 0, h:h + 1], dtv[:, 0, NH + h:NH + h + 1]
                    f1, b1 = dtv[:, 1, h:h + 1], dtv[:, 1, NH + h:NH + h + 1]
                    V.tensor_scalar(o[:, 0, :], e[:, 0:256], f0, None, ALU.mult)
                    link(V.tensor_scalar(o[:, 1, :], e[:, 512:768], b1, None, ALU.mult))
                    V.scalar_tensor_tensor(o[:, 0, 0:P], e[:, 256:384], b0, o[:, 0, 0:P], ALU.mult, ALU.add)
                    link(V.scalar_tensor_tensor(o[:, 1, P:256], e[:, 384:512], f1, o[:, 1, P:256], ALU.mult, ALU.add))
                    V.tensor_tensor(o, o, cb[:, h // 8, :, :], ALU.mult).then_inc(g_ready, 1)

            def score_max(h):
                dve.wait_ge(sc_psum, h + 1)
                link(V.tensor_reduce(stat[:, 12:14], bank[4][:, :].rearrange("p (t s) -> p t s", t=TT), AXX, ALU.max))
                V.tensor_scalar(stat[:, 12:14], stat[:, 12:14], -(float(AD) ** -0.5), None, ALU.mult).then_inc(sc_max, 1)

            def prob_norm(h):
                dve.wait_ge(sc_exp, h + 1)
                link(V.reciprocal(stat[:, 16:18], stat[:, 14:16]))
                for t in range(TT):
                    last = V.tensor_scalar(prob[:, t, :], prob[:, t, :], stat[:, 16 + t:17 + t], None, ALU.mult)
                last.then_inc(prob_ready, 1)

            dve.wait_ge(qT_psum, 5)
            dve.wait_ge(acsN_ready, 2)
            dve.wait_ge(cb_ready, 2)
            score_max(0)
            seg_mask(0)
            prob_norm(0)
            seg_weight(0)
            for g in range(8):
                dve.wait_ge(unit_taken, U_G + g + 1)
                link(V.tensor_scalar(sig[:, 2 * g:2 * g + 2, :], sig[:, 2 * g:2 * g + 2, :], 1.0, None, ALU.add))
                V.reciprocal(sig[:, 2 * g:2 * g + 2, :], sig[:, 2 * g:2 * g + 2, :]).then_inc(gate_ready, 1)
                if g < 7:
                    seg_mask(g + 1)
                    score_max(g + 1)
                dve.wait_ge(y_psum, g + 1)
                V.scalar_tensor_tensor(xbcT[:, g, :], xbcT[:, g, :], prmT[:, N_ROWS + g:N_ROWS + g + 1], bank[7][:, 0:256],
                                       ALU.mult, ALU.add).then_inc(yz_ready, 1)
                dve.wait_ge(yz_ready, 2 * g + 1)
                V.tensor_tensor(xbcT[:, g, :], xbcT[:, g, :], siluz[:, g, :], ALU.mult).then_inc(yz_ready, 1)
                if g < 7:
                    prob_norm(g + 1)
                    seg_weight(g + 1)

            dve.wait_ge(gate_ready, 8)
            for u in range(4):
                n = U_BA + u
                dve.wait_ge(unit_done, n + 1)
                V.tensor_tensor(hT[:, 2 * u:2 * u + 2, :], bank[n % 2][:, :].rearrange("p (m l) -> p m l", m=2),
                                sig[:, KD + 2 * u:KD + 2 * u + 2, :], ALU.mult).then_inc(unit_taken, 1)
            dve.wait_ge(unit_taken, U_BS)
            dve.wait_ge(rB_ready, 1)
            for u in range(4):
                n = U_BS + u
                dve.wait_ge(unit_done, n + 1)
                s = sig[:, 2 * u:2 * u + 2, :]
                link(V.tensor_tensor(s, s, rB.unsqueeze(1).to_broadcast([P, 2, SEQ]), ALU.mult))
                V.tensor_tensor(s, s, bank[n % 2][:, :].rearrange("p (m l) -> p m l", m=2), ALU.mult).then_inc(unit_taken, 1)
                dve.wait_ge(unit_taken, n + 1)
                V.tensor_tensor(hT[:, 2 * u:2 * u + 2, :], hT[:, 2 * u:2 * u + 2, :], s, ALU.add).then_inc(mix_ready, 1)
            def lo_split(i, c, n):
                u, sn = split_at(c, n)
                dve.wait_ge(hi_ready, i * (BODY * SPE) + (sn + 1))
                V.tensor_tensor(split[:, sn % NSPLIT, 1, :], ring[:, moe_slot(u), :],
                                split[:, sn % NSPLIT, 0, :].bitcast(F32), ALU.subtract).then_inc(lo_ready, 1)

            for u in range(4):
                n = U_O + u
                dve.wait_ge(unit_done, n + 1)
                x_ = xres[:, :, u * UW:(u + 1) * UW]
                V.tensor_tensor(x_, x_, bank[n % 2][:, :].rearrange("p (t c) -> p t c", t=TT), ALU.add).then_inc(unit_taken, 1)
                lo_split(0, 0, u)
            dve.wait_ge(x1r_ready, 1)
            for t in range(TT):
                V.tensor_scalar(hN[:, t, :], xres[:, t, :], stat[:, 20 + t:21 + t], None, ALU.mult).then_inc(h2_ready, 1)
            scaled_T(h2T_psum, h2T_ready, R_GFFN)
            hs3 = hs.rearrange("p (t d) -> p t d", t=TT)
            dve.wait_ge(hb_ready, 1)
            V.tensor_tensor(hs3, hN[:, :, :], hb1[:, :, :], ALU.subtract).then_inc(res_ready, 1)

            dve.wait_ge(lg_psum, 1)
            link(V.tensor_tensor(lgt, bank[6][:, 0:64].rearrange("p (t e) -> p t e", t=TT),
                                 brt_b.unsqueeze(1).to_broadcast([P, TT, NE]), ALU.add))
            for t in range(TT):
                last = V.max(top8[:, t, :], lgt[:, t, :])
            link(last)
            V.tensor_scalar(stat[:, 26:28], top8[:, :, 0:1].rearrange("p t a -> p (t a)"), -1.0, None, ALU.mult)
            for t in range(TT):
                v4 = top8[:, t, TOPK - 1:TOPK]
                V.tensor_scalar(msk[:, t, :], lgt[:, t, :], v4, None, ALU.is_gt)
                last = V.tensor_scalar(eqm[:, t, :], lgt[:, t, :], v4, None, ALU.is_equal)
            last.then_inc(lmax_ready, 1)
            dve.wait_ge(lmax_ready, 1)
            dve.wait_ge(hb_ready, 2)
            V.tensor_tensor(hs3, hs3, hb2[:, :, :], ALU.subtract).then_inc(res_ready, 1)
            link(V.tensor_reduce(stat[:, 28:30], msk, AXX, ALU.add))
            V.tensor_scalar(stat[:, 28:30], stat[:, 28:30], -1.0, float(TOPK), ALU.mult, ALU.add)
            for t in range(TT):
                last = V.tensor_tensor_scan(eqc[:, t, :], eqm[:, t, :], eqm[:, t, :], 0.0, ALU.add, ALU.bypass)
            link(last)
            for t in range(TT):
                last = V.scalar_tensor_tensor(eqm[:, t, :], eqc[:, t, :], stat[:, 28 + t:29 + t], eqm[:, t, :], ALU.is_le, ALU.mult)
            link(last)
            V.tensor_tensor(msk, msk, eqm, ALU.add).then_inc(w_ready, 1)
            dve.wait_ge(w_ready, 1)
            dve.wait_ge(lexp_ready, 1)
            link(V.memset(wtok[:, :, NE:NE + 1], 0.0))
            link(V.tensor_tensor(wtok[:, :, 0:NE], lgt, msk, ALU.mult))
            link(V.tensor_reduce(stat[:, 32:34], wtok[:, :, 0:NE], AXX, ALU.add))
            link(V.reciprocal(stat[:, 32:34], stat[:, 32:34]))
            V.tensor_tensor(wtok[:, :, 0:NE], wtok[:, :, 0:NE], stat[:, 32:34].unsqueeze(2).to_broadcast([P, TT, NE]),
                            ALU.mult).then_inc(w_ready, 1)
            dve.wait_ge(wT_psum, 1)
            link(V.memset(rankm[:, :, :], -1.0))
            link(V.tensor_tensor(rankm[:, :, 0:NE], bank[7][:, 0:2 * NE].rearrange("p (t e) -> p t e", t=TT), msk, ALU.mult))
            link(V.tensor_scalar(rankm[:, :, 0:NE], rankm[:, :, 0:NE], -1.0, None, ALU.add))
            link(V.tensor_reduce(cnt[:, 0:1], bank[7][:, 2 * NE:3 * NE], AXX, ALU.max))
            link(V.tensor_scalar(cnt[:, 1:2], cnt[:, 0:1], float(CAP), None, ALU.is_gt))
            V.tensor_copy(over_i[:, :], cnt[:, 1:2]).then_inc(route_ready, 1)

            V.memset(slotWT, 0.0)

            def place(e, c, shift=0):
                for t in range(TT):
                    rk = rankm[:, t, bass.ds(e, 1)]
                    wk = wtok[:, t, bass.ds(e, 1)]
                    if shift:
                        link2(V.tensor_scalar(eqc[:, t, 0:1], rk, -float(shift), None, ALU.add))
                        rk = eqc[:, t, 0:1]
                    V.tensor_scalar(slotP[:, c % 2, t, :], iota, rk, None, ALU.is_equal)
                    V.tensor_scalar(slotW[:, c % 2, t, 0:CAP], iota, rk, wk, ALU.is_equal, ALU.mult)
                    last = V.tensor_scalar(slotW[:, c % 2, t, CAP:P], iota, rk, wk, ALU.is_equal, ALU.mult)
                return last

            def tokens_in():
                return V.tensor_tensor(x32, bank[6][:, :].rearrange("p (k s) -> p k s", k=KD),
                                       prmT[:, R_GFFN:R_GFFN + KD].unsqueeze(2).to_broadcast([P, KD, CAP]), ALU.mult)

            def hi_lo(step, src, dst):
                step(V.tensor_copy(dst[:, :, 0:CAP], src))
                return V.tensor_tensor(dst[:, :, CAP:P], src, dst[:, :, 0:CAP].bitcast(F32), ALU.subtract)

            def gate_up(step, e, ga_sem):
                bias = b1T[:, bass.ds(e, 1), :].rearrange("p a m -> p (a m)")
                V.tensor_tensor(ga.rearrange("p (m s) -> p m s", m=KD), bank[4][:, :].rearrange("p (m s) -> p m s", m=KD),
                                bias[:, 0:KD].unsqueeze(2).to_broadcast([P, KD, CAP]), ALU.add)
                step(V.tensor_tensor(ub.rearrange("p (m s) -> p m s", m=KD), bank[5][:, :].rearrange("p (m s) -> p m s", m=KD),
                                     bias[:, KD:2 * KD].unsqueeze(2).to_broadcast([P, KD, CAP]), ALU.add))
                V.tensor_scalar(ga, ga, LIMIT, None, ALU.min).then_inc(ga_sem, 1)
                step(V.tensor_scalar(ub, ub, LIMIT, -LIMIT, ALU.min, ALU.max))
                step(V.scalar_tensor_tensor(ub, ub, 1.0, ga, ALU.add, ALU.mult))

            for q in range(4):
                dve.wait_ge(b2_psum, q + 1)
                x_ = xres[:, q // 2, (q % 2) * 512:(q % 2 + 1) * 512]
                last = V.tensor_tensor(x_, x_, bank[2 + q][:, :], ALU.add)
            last.then_inc(c_added, 1)
            dve.wait_ge(c_added, 1)
            V.memset(ysb, 0.0).then_inc(ys_ready, 1)
            place(0, 0).then_inc(p_ready, 1)
            dve.wait_ge(x_psum, 1)
            link(tokens_in())
            hi_lo(link, x32, xs).then_inc(xs_ready, 1)

            def expert(i, c, final):
                e = i * BODY + c
                step = chain(dve, moe_dve_step, e * LINKS - (2 if final else 0))
                if not final:
                    place(e + 1, c + 1).then_inc(p_ready, 1)
                for n in range(NSPLIT, SPE):
                    lo_split(i, c, n)
                if not final:
                    dve.wait_ge(x_psum, e + 2)
                    step(tokens_in())
                    hi_lo(step, x32, xs).then_inc(xs_ready, 1)
                else:
                    step.count[0] = 2
                dve.wait_ge(t_psum, e + 1)
                gate_up(step, e, ga_ready)
                dve.wait_ge(sg_ready, e + 1)
                step(V.tensor_tensor(ub, ub, sg, ALU.mult))
                hi_lo(step, act32, as_).then_inc(actT_ready, 1)
                if not final:
                    lo_split(i, c + 1, 0)
                dve.wait_ge(c_psum, e + 1)
                add_sums(c_added)
                if not final:
                    for n in range(1, NSPLIT):
                        lo_split(i, c + 1, n)
                assert step.count[0] == LINKS

            def add_sums(added):
                for q in range(4):
                    x_ = xres[:, q // 2, (q % 2) * 512:(q % 2 + 1) * 512]
                    V.tensor_tensor(x_, x_, bank[q][:, :], ALU.add).then_inc(added, 1)

            LINKS = 7
            with dve.Fori(0, NE // BODY - 1) as i:
                for c in range(BODY):
                    expert(i, c, False)
            for c in range(BODY - 1):
                expert(NE // BODY - 1, c, False)
            expert(NE // BODY - 1, BODY - 1, True)
            dve.wait_ge(c_psum, NE + 1)
            add_sums(c_added)
            dve.wait_ge(c_added, 4 * NE + 5)

            OSTEPS = TT + 3
            dve.wait_ge(route_ready, 1)
            again = dve.value_load(over_i[0:1, 0:1], min_val=0, max_val=1)
            with dve.If(again > 0):
                with dve.Fori(0, NE) as e:
                    for r in range(NPASS - 1):
                        n = e * (NPASS - 1) + (r + 1)
                        link2 = chain(dve, over_step, e * (OSTEPS * (NPASS - 1)) + r * OSTEPS)
                        place(e, 0, (r + 1) * CAP).then_inc(over_place, 1)
                        dve.wait_ge(over_x, n)
                        tokens_in().then_inc(over_xr, 1)
                        dve.wait_ge(over_h, n)
                        gate_up(link2, e, over_ga)
                        dve.wait_ge(over_sg, n)
                        V.tensor_tensor(ub, ub, sg, ALU.mult).then_inc(over_act, 1)
                        dve.wait_ge(over_c, n)
                        add_sums(over_added)
                        dve.wait_ge(over_added, n * 4)
                        assert link2.count[0] == OSTEPS
            V.tensor_copy(cnt[:, 0:1], cnt[:, 0:1]).then_inc(sum_done, 1)
            dve.wait_ge(fr_ready, 1)
            dve.wait_ge(gfin_in, 16)
            for t in range(TT):
                V.scalar_tensor_tensor(hN[:, t, :], xres[:, t, :], stat[:, 30 + t:31 + t], gfin, ALU.mult, ALU.mult).then_inc(fin_ready, 1)


_INS = ["x", "g_mix", "w_in", "conv_w", "conv_b", "dt_bias_f", "dt_bias_b", "a_log_f", "a_log_b", "d_skip",
        "g_ssm", "q_norm_g", "k_norm_g", "w_br_ssm", "w_br_attn", "w_out", "g_ffn", "w_router", "b_router",
        "w_mlp1", "b_mlp1", "w_mlp2", "b_mlp2", "g_final"]
_OUT = ((1, SEQ, D), "float32")


def kernel(**inputs):
    import numpy as _np
    import concourse.bacc as _bacc
    from concourse import mybir as _mybir
    from concourse.bass_utils import run_bass_kernel_spmd as _run

    nc = _bacc.Bacc("TRN2", target_bir_lowering=False, num_devices=1)
    arrays, args = {}, []
    for name in _INS:
        a = _np.ascontiguousarray(inputs[name])
        arrays[f"in_{name}_dram"] = a
        args.append(nc.dram_tensor(f"in_{name}_dram", a.shape, _mybir.dt.from_np(a.dtype), kind="ExternalInput").ap())
    c = shape_constants()
    arrays["shape_constants_dram"] = c
    args.append(nc.dram_tensor("shape_constants_dram", c.shape, _mybir.dt.from_np(c.dtype), kind="ExternalInput").ap())
    args.append(nc.dram_tensor("out_dram", _OUT[0], _mybir.dt.from_np(_np.dtype(_OUT[1])), kind="ExternalOutput").ap())
    encoder_layer(nc, *args)
    r = _run(nc, [arrays], core_ids=[0])
    return r.results[0]["out_dram"]
```

```python
import math
import concourse.bass as bass
from concourse import mybir
from contextlib import ExitStack

F32 = mybir.dt.float32
I32 = mybir.dt.int32
ALU = mybir.AluOpType
ACT = mybir.ActivationFunctionType
AXX = mybir.AxisListType.X

P = 128
D = 1024
SEQ = 256
TT = SEQ // P
KD = D // P
NH = 16
HD = 64
NST = 128
CONV = 5
PAD = (CONV - 1) // 2
XBC_TILES = (D + 2 * 2 * NST) // P
AH = 8
KVH = 2
AD = 128
XBC0 = D
DT0 = XBC0 + XBC_TILES * P
Q0 = DT0 + 2 * NH
G0 = Q0 + AH * AD + 2 * KVH * AD
NE = 32
TOPK = 4
DE = D
LIMIT = 7.0
ALPHA = 1.702
EPS = 1e-6
CAP = 64
NPASS = SEQ // CAP
NEG = -1e30

UW = 256
UNIT = KD * UW
RING_MIX = 10
SUMS = 4
BLOCKS = (0, 2, 1, 3)
RING = 8
EXP_UNITS = 12
BODY = 4
NSPLIT = 4
DIRECT = (3, 9)
SPLIT = tuple(q for q in range(EXP_UNITS) if q not in DIRECT)
SPE = len(SPLIT)
PRE = 9
BF16 = mybir.dt.bfloat16
F32R = mybir.dt.float32r

U_XBC, U_Z, U_K, U_Q, U_V, U_G, U_BA, U_BS, U_O = 0, 6, 10, 11, 15, 16, 24, 28, 32
N_MIX = 36

R_GMIX, R_GSSM, R_GFFN, R_CB, R_CW = 0, 8, 16, 24, 36
N_ROWS = R_CW + CONV * XBC_TILES
C_ID, C_LE, C_GE, C_ONE, C_NEGF, C_ZERO, C_NEGB = (P * i for i in range(7))
C_IOTA = 7 * P
C_COS = C_IOTA + CAP
C_SIN = C_COS + TT * AD
N_CONST = C_SIN + TT * AD
SLAB = 212000


def shape_constants():
    import numpy as np
    r = np.arange(P)
    c = np.zeros((P, N_CONST), np.float32)
    c[:, C_ID:C_ID + P] = r[:, None] == r[None, :]
    c[:, C_LE:C_LE + P] = r[:, None] <= r[None, :]
    c[:, C_GE:C_GE + P] = r[:, None] >= r[None, :]
    c[:, C_ONE:C_ONE + P] = 1.0
    c[:, C_NEGF:C_NEGF + P] = np.where(r[:, None] > r[None, :], NEG, 0.0)
    c[:, C_NEGB:C_NEGB + P] = np.where(r[:, None] < r[None, :], NEG, 0.0)
    c[:, C_IOTA:C_IOTA + CAP] = np.arange(CAP)[None, :]
    half = AD // 4
    inv = np.float32(10000.0) ** (-np.arange(0, AD // 2, 2, dtype=np.float32) / np.float32(AD // 2))
    tok = np.arange(SEQ)
    for axis, pos in enumerate((tok // 64, tok % 64)):
        ang = (pos.astype(np.float32)[:, None] * inv).astype(np.float32)
        cos, sin = np.cos(ang).astype(np.float32), np.sin(ang).astype(np.float32)
        for t in range(TT):
            for h, sign in ((0, -1.0), (1, 1.0)):
                o = t * AD + axis * 2 * half + h * half
                c[:, C_COS + o:C_COS + o + half] = cos[t * P:(t + 1) * P]
                c[:, C_SIN + o:C_SIN + o + half] = sign * sin[t * P:(t + 1) * P]
    return c


def encoder_layer(nc, x, g_mix, w_in, conv_w, conv_b, dt_bias_f, dt_bias_b, a_log_f, a_log_b, d_skip,
                  g_ssm, q_norm_g, k_norm_g, w_br_ssm, w_br_attn, w_out, g_ffn, w_router, b_router,
                  w_mlp1, b_mlp1, w_mlp2, b_mlp2, g_final, consts, out):
    with ExitStack() as ctx:
        base = -(-nc.sbuf_base // 32) * 32
        ctx.enter_context(nc.sbuf_tensor("slab", [P, (SLAB + 32) // 4], F32))
        top = [base]
        place_of = {}

        def sb(name, shape, dt=F32, at=None):
            size = int(math.prod(shape[1:])) * mybir.dt.size(dt)
            off = top[0] if at is None else at
            place_of[name] = off
            if at is None:
                top[0] += -(-size // 32) * 32
                assert top[0] <= base + SLAB
            return nc.alloc_sbuf_tensor_at(name, shape, dt, offset=off)

        def sem(name):
            return ctx.enter_context(nc.semaphore(name))

        bank = [ctx.enter_context(nc.psum_tensor(f"bank{i}", [P, 512], F32)) for i in range(8)]

        ring = sb("ring", [P, RING_MIX, UNIT])
        over = sb("over", [P, 12288])
        split = sb("split", [P, NSPLIT, 2, UNIT], F32R, at=place_of["ring"] + RING * UNIT * 4)
        sig = over[:, 0:4096].rearrange("p (m l) -> p m l", m=16)
        roped = over[:, 0:2560].rearrange("p (t n) -> p t n", t=TT)
        xbcT = over[:, 4096:7168].rearrange("p (m l) -> p m l", m=XBC_TILES)
        siluz = over[:, 7168:9216].rearrange("p (m l) -> p m l", m=KD)
        b1raw = over[0:NE, 7168:9216]
        qk = over[:, 9216:11776].rearrange("p (t n) -> p t n", t=TT)
        kT = over[:, 11776:12288].rearrange("p (h l) -> p h l", h=KVH)

        xres = sb("xres", [P, TT, D])
        hN = sb("hN", [P, TT, D])
        hT = sb("hT", [P, KD, SEQ])
        xs = sb("xs", [P, KD, P], F32R, at=place_of["hN"])
        as_ = sb("as", [P, KD, P], F32R, at=place_of["hN"] + KD * P * 4)
        hb3 = sb("hb3", [P, TT, D], BF16, at=place_of["hT"])
        cst = sb("cst", [P, N_CONST])
        prm = sb("prm", [P, P])
        prmT = sb("prmT", [P, N_ROWS + 8])
        dskr = sb("dskr", [8, 2])
        dske = sb("dske", [8, P])
        b1T = sb("b1T", [P, NE, 16])
        wr = sb("wr", [P, KD, NE])
        wdt = sb("wdt", [P, KD, 2 * NH])
        vec = sb("vec", [P, 2 * NH + 2 * NH + NE + 2 * AD])
        dtb_b, alog_b, brt_b = vec[:, 0:32], vec[:, 32:64], vec[:, 64:96]
        kg_b, qg_b = vec[:, 96:224], vec[:, 224:352]
        stat = sb("stat", [P, 64])
        dtv = sb("dtv", [P, TT, 32])
        dta = sb("dta", [P, TT, 32])
        dtu = sb("dtu", [P, TT, 32])
        acsN = sb("acsN", [P, TT, 32])
        nacs = sb("nacs", [P, TT, 32])
        acsT = sb("acsT", [32, SEQ])

        arena = sb("arena", [P, 10000])
        vN = arena[:, 0:512].rearrange("p (t n) -> p t n", t=TT)
        qT = arena[:, 512:2560].rearrange("p (h l) -> p h l", h=AH)
        cb = arena[:, 2560:3584].rearrange("p (g i l) -> p g i l", g=2, i=TT)
        ebuf = arena[:, 3584:5120].rearrange("p (h l) -> p h l", h=2)
        gbuf = arena[:, 5120:7168].rearrange("p (b h i l) -> p b h i l", b=2, h=2, i=TT)
        prob = arena[:, 7168:7680].rearrange("p (t s) -> p t s", t=TT)
        probT = arena[:, 7680:8192].rearrange("p (i q) -> p i q", i=TT)
        ropeb = arena[:, 3584:4096].rearrange("p (t n) -> p t n", t=TT)
        xp = arena[:, 8192:9232].rearrange("p (b m l) -> p b m l", b=2, m=2)
        sqacc = arena[:, 9232:9488]
        sqb = arena[:, 9488:9744]
        rB = arena[:, 9744:10000]
        slotW = arena[:, 0:512].rearrange("p (b t s) -> p b t s", b=2, t=TT)
        x32 = arena[:, 512:1024].rearrange("p (k s) -> p k s", k=KD)
        ga = arena[:, 1024:1536]
        ub = arena[:, 1536:2048]
        act32 = ub.rearrange("p (k s) -> p k s", k=KD)
        wT = arena[0:NE, 1024:1280]
        sg = arena[:, 2048:2560]
        hs = arena[:, 2560:4608]
        ysb = arena[:, 4608:5632]
        b2s = arena[0:NE, 4608:5632]
        slotWT = arena[:, 5632:5888]
        gfin = arena[:, 5888:6912]
        msk = arena[:, 6912:6976].rearrange("p (t e) -> p t e", t=TT)
        lgt = arena[:, 6976:7040].rearrange("p (t e) -> p t e", t=TT)
        top8 = arena[:, 7040:7056].rearrange("p (t e) -> p t e", t=TT)
        eqm = arena[:, 7056:7120].rearrange("p (t e) -> p t e", t=TT)
        eqc = arena[:, 7120:7184].rearrange("p (t e) -> p t e", t=TT)
        hb1 = sb("hb1", [P, TT, D], BF16, at=place_of["arena"] + 4 * 7184)
        hb2 = sb("hb2", [P, TT, D], BF16, at=place_of["arena"] + 4 * (7184 + 1024))
        hb = (hb1, hb2, hb3)
        slotP = sb("slotP", [P, 2, TT, CAP], BF16, at=place_of["arena"] + 4 * (7184 + 2048))
        rankm = sb("rankm", [P, TT, NE + 1])
        wtok = sb("wtok", [P, TT, NE + 1])
        cnt = sb("cnt", [P, 2])
        over_i = sb("over_i", [P, 1], I32)

        ident = cst[:, C_ID:C_ID + P]
        m_le = cst[:, C_LE:C_LE + P]
        m_ge = cst[:, C_GE:C_GE + P]
        ones = cst[:, C_ONE:C_ONE + P]
        iota = cst[:, C_IOTA:C_IOTA + CAP]
        
        slot_full = [sem(f"slot_full{i}") for i in range(RING_MIX)]
        unit_done = sem("unit_done")
        c_in = sem("c_in"); x_in = sem("x_in"); row_in = sem("row_in"); b1_in = sem("b1_in")
        vec_in = sem("vec_in"); dsk_in = sem("dsk_in"); wdt_in = sem("wdt_in"); late_in = sem("late_in")
        gfin_in = sem("gfin_in"); out_done = sem("out_done")
        act_step = sem("act_step"); dve_step = sem("dve_step"); pool_step = sem("pool_step")
        moe_dve_step = sem("moe_dve_step")
        dsk_ready = sem("dsk_ready"); prm_ready = sem("prm_ready"); prm_taken = sem("prm_taken")
        xsq_ready = sem("xsq_ready"); xr_ready = sem("xr_ready"); h_ready = sem("h_ready")
        hT_psum = sem("hT_psum"); hT_ready = sem("hT_ready")
        unit_taken = sem("unit_taken")
        conv_done = sem("conv_done"); silu_done = sem("silu_done")
        dt_psum = sem("dt_psum"); dt_in = sem("dt_in"); dt_exp = sem("dt_exp"); a_ready = sem("a_ready")
        acs_psum = sem("acs_psum"); acsN_ready = sem("acsN_ready"); acsT_psum = sem("acsT_psum")
        acsT_ready = sem("acsT_ready")
        xN_psum = sem("xN_psum"); xN_ready = sem("xN_ready"); cb_psum = sem("cb_psum"); cb_ready = sem("cb_ready")
        qsq_ready = sem("qsq_ready"); qr_ready = sem("qr_ready"); roped_ready = sem("roped_ready")
        qT_psum = sem("qT_psum"); qT_ready = sem("qT_ready")
        seg_psum = sem("seg_psum"); seg_masked = sem("seg_masked"); seg_exp = sem("seg_exp"); g_ready = sem("g_ready")
        sc_psum = sem("sc_psum"); sc_max = sem("sc_max"); sc_exp = sem("sc_exp"); prob_ready = sem("prob_ready")
        probT_psum = sem("probT_psum"); probT_ready = sem("probT_ready")
        o_psum = sem("o_psum"); o_ready = sem("o_ready")
        y_psum = sem("y_psum"); yz_ready = sem("yz_ready"); ysq_ready = sem("ysq_ready"); ysq_added = sem("ysq_added")
        yg_ready = sem("yg_ready")
        gate_ready = sem("gate_ready")
        yr_ready = sem("yr_ready"); diag_ready = sem("diag_ready"); rB_psum = sem("rB_psum")
        ssq_psum = sem("ssq_psum"); ssq_ready = sem("ssq_ready"); rB_ready = sem("rB_ready")
        mix_ready = sem("mix_ready"); x1sq_ready = sem("x1sq_ready")
        x1r_ready = sem("x1r_ready"); h2_ready = sem("h2_ready"); h2T_psum = sem("h2T_psum"); h2T_ready = sem("h2T_ready")
        lg_psum = sem("lg_psum"); lmax_ready = sem("lmax_ready"); lexp_ready = sem("lexp_ready")
        w_ready = sem("w_ready"); wT_psum = sem("wT_psum"); wT_ready = sem("wT_ready")
        b2_psum = sem("b2_psum"); route_ready = sem("route_ready")
        p_ready = sem("p_ready"); x_psum = sem("x_psum"); xs_ready = sem("xs_ready")
        ga_ready = sem("ga_ready"); sg_ready = sem("sg_ready"); actT_ready = sem("actT_ready")
        hi_ready = sem("hi_ready"); lo_ready = sem("lo_ready"); hs_ready = sem("hs_ready"); t_psum = sem("t_psum")
        pw_psum = sem("pw_psum"); pw_ready = sem("pw_ready")
        hb_ready = sem("hb_ready"); res_ready = sem("res_ready"); ys_ready = sem("ys_ready"); h_psum = sem("h_psum"); y_half = sem("y_half"); c_psum = sem("c_psum"); c_added = sem("c_added")
        over_full = sem("over_full"); over_place = sem("over_place"); over_x = sem("over_x"); over_xr = sem("over_xr")
        over_h = sem("over_h"); over_ga = sem("over_ga"); over_sg = sem("over_sg"); over_act = sem("over_act")
        over_y = sem("over_y"); over_ys = sem("over_ys"); over_c = sem("over_c"); over_added = sem("over_added")
        over_step = sem("over_step")
        fsq_ready = sem("fsq_ready"); fr_ready = sem("fr_ready"); fin_ready = sem("fin_ready"); sum_done = sem("sum_done")

        def mix_slot(n):
            return n % RING_MIX

        def moe_slot(u):
            return (u + 6) % RING

        def mix_full(eng, n):
            eng.wait_ge(slot_full[mix_slot(n)], 16 * (n // RING_MIX + 1))

        def mix_loads(s):
            return len([n for n in range(N_MIX) if mix_slot(n) == s])

        def moe_full(eng, i, u):
            s = moe_slot(u)
            eng.wait_ge(slot_full[s], 16 * (mix_loads(s) + u // RING + 1) + i * (16 * BODY * EXP_UNITS // RING))

        def unit_used(eng, i, u):
            eng.wait_ge(unit_done, i * (BODY * EXP_UNITS) + (N_MIX + u + 1))

        def split_at(c, n):
            return c * EXP_UNITS + SPLIT[n], c * SPE + n

        def buffer_free(eng, i, c, n):
            r = c * SPE + n - NSPLIT
            c0, n0 = r // SPE, r % SPE
            unit_used(eng, i, c0 * EXP_UNITS + SPLIT[n0])

        def cols(w, c0):
            return w.rearrange("(k p) n -> p k n", p=P)[:, :, c0:c0 + UW]

        def mix_src(n):
            if n < U_Z:
                return cols(w_in[0], XBC0 + n * UW)
            if n < U_K:
                return cols(w_in[0], (n - U_Z) * UW)
            if n == U_K:
                return cols(w_in[0], Q0 + AH * AD)
            if n < U_V:
                return cols(w_in[0], Q0 + (n - U_Q) * UW)
            if n == U_V:
                return cols(w_in[0], Q0 + AH * AD + KVH * AD)
            if n < U_BA:
                return cols(w_in[0], G0 + (n - U_G) * UW)
            if n < U_BS:
                return cols(w_br_attn[0], (n - U_BA) * UW)
            if n < U_O:
                return cols(w_br_ssm[0], (n - U_BS) * UW)
            return cols(w_out[0], (n - U_O) * UW)

        w1v = w_mlp1[0].rearrange("e (k p) n -> e p k n", p=P)
        w2v = w_mlp2[0].rearrange("e (k p) n -> e p k n", p=P)

        def k_view(s):
            return ring[:, s, :].rearrange("p (k n) -> p k n", k=KD)

        def chain(eng, semaphore, base=0):
            n = [0]

            def link(ins):
                n[0] += 1
                ins.then_inc(semaphore, 1)
                eng.wait_ge(semaphore, base + n[0])

            def post(ins):
                n[0] += 1
                ins.then_inc(semaphore, 1)
            link.count, link.post = n, post
            return link

        block = ctx.enter_context(nc.Block())

        @block.sync
        def _(sp):
            def load_moe(i, u):
                e = i * BODY + u // EXP_UNITS
                q = u % EXP_UNITS
                s = moe_slot(u)
                if q < KD:
                    src = w1v[bass.ds(e, 1), :, q, :].rearrange("a p n -> (a p) n")
                else:
                    k = 2 * (q - KD)
                    src = w2v[bass.ds(e, 1), :, k:k + 2, :].rearrange("a p k n -> (a p) k n")
                dst = ring[:, s, :] if q < KD else ring[:, s, :].rearrange("p (k n) -> p k n", k=2)
                sp.dma_start(dst, src).then_inc(slot_full[s], 16)

            sp.wait_ge(x_in, 16)
            sp.wait_ge(row_in, 16 * 5)
            sp.wait_ge(b1_in, 16)
            for n in range(N_MIX):
                if n >= RING_MIX:
                    sp.wait_ge(unit_done, n - RING_MIX + 1)
                sp.dma_start(k_view(mix_slot(n)), mix_src(n)).then_inc(slot_full[mix_slot(n)], 16)
            def slot_free(i, u):
                v = u - RING
                c, q = v // EXP_UNITS, v % EXP_UNITS
                if q in DIRECT:
                    unit_used(sp, i, v)
                else:
                    sp.wait_ge(lo_ready, i * (BODY * SPE) + (c * SPE + SPLIT.index(q) + 1))

            for u in range(BODY * EXP_UNITS):
                if u < RING:
                    last_mix = max(n for n in range(N_MIX) if mix_slot(n) == moe_slot(u))
                    sp.wait_ge(unit_done, last_mix + 1)
                else:
                    slot_free(0, u)
                load_moe(0, u)
            with sp.Fori(1, NE // BODY) as i:
                for u in range(BODY * EXP_UNITS):
                    slot_free(i, u)
                    load_moe(i, u)

            sp.wait_ge(route_ready, 1)
            again = sp.value_load(over_i[0:1, 0:1], min_val=0, max_val=1)
            with sp.If(again > 0):
                with sp.Fori(0, NE) as e:
                    for r in range(NPASS - 1):
                        for q in range(EXP_UNITS):
                            if q == 0 and r == 0:
                                sp.wait_ge(over_y, e * (NPASS - 1) + 1)
                            elif q == 0:
                                sp.wait_ge(over_y, e * (NPASS - 1) + (r + 1))
                            if q == KD:
                                sp.wait_ge(over_h, e * (NPASS - 1) + (r + 1))
                            if q < KD:
                                src = w1v[bass.ds(e, 1), :, q, :].rearrange("a p n -> (a p) n")
                                dst = ring[:, q, :]
                            else:
                                k = 2 * (q - KD)
                                src = w2v[bass.ds(e, 1), :, k:k + 2, :].rearrange("a p k n -> (a p) k n")
                                dst = ring[:, q - KD, :].rearrange("p (k n) -> p k n", k=2)
                            sp.dma_start(dst, src).then_inc(over_full, 16)
            sp.wait_ge(fin_ready, 1)
            sp.dma_start(out[0, 0:P, :], hN[:, 0, :]).then_inc(out_done, 16)
            sp.wait_ge(fin_ready, 2)
            sp.dma_start(out[0, P:SEQ, :], hN[:, 1, :]).then_inc(out_done, 16)
            sp.wait_ge(out_done, 32)

        @block.tensor
        def _(pe):
            pe.wait_ge(c_in, 16)
            pe.wait_ge(row_in, 16 * 5)
            pe.wait_ge(dsk_ready, 1)
            nc.tensor.transpose(bank[6][:, 0:N_ROWS], prm[0:N_ROWS, :], ident[0:N_ROWS, 0:N_ROWS])
            nc.tensor.transpose(bank[6][:, N_ROWS:N_ROWS + 8], dske[:, :], ident[0:8, 0:8]).then_inc(prm_ready, 1)
            pe.wait_ge(b1_in, 16)
            for m in range(16):
                last = nc.tensor.transpose(bank[7][:, m * NE:(m + 1) * NE], b1raw[:, m * P:(m + 1) * P],
                                           ident[0:NE, 0:NE])
            last.then_inc(prm_ready, 1)

            def to_T(ready, psum_sem):
                pe.wait_ge(ready, 2)
                for b in range(4):
                    for kk in range(2):
                        for t in range(TT):
                            k = 2 * b + kk
                            last = nc.tensor.transpose(bank[2 + b][:, kk * 256 + t * P:kk * 256 + (t + 1) * P],
                                                       hN[:, t, k * P:(k + 1) * P], ident)
                    last.then_inc(psum_sem, 1)

            to_T(h_ready, hT_psum)

            def unit(n, rhs=None, tokens=None):
                mix_full(pe, n)
                if n >= 2:
                    pe.wait_ge(unit_taken, n - 1)
                w = k_view(mix_slot(n))
                for a in range(2):
                    for k in range(KD):
                        o = bank[n % 2][:, a * 256:(a + 1) * 256]
                        if tokens is None:
                            last = nc.tensor.matmul(o, w[:, k, a * P:(a + 1) * P], rhs[:, k, :],
                                                    start=(k == 0), stop=(k == KD - 1))
                        else:
                            last = nc.tensor.matmul(o, tokens[:, k, a * P:(a + 1) * P], w[:, k, :],
                                                    start=(k == 0), stop=(k == KD - 1))
                last.then_inc(unit_done, 1)

            pe.wait_ge(hT_ready, 4)
            for n in range(U_XBC, U_Z):
                unit(n, rhs=hT)
            pe.wait_ge(wdt_in, 16)
            pe.wait_ge(prm_taken, 2)
            for t in range(TT):
                for k in range(KD):
                    last = nc.tensor.matmul(bank[6][:, t * 32:(t + 1) * 32], hT[:, k, t * P:(t + 1) * P], wdt[:, k, :],
                                            start=(k == 0), stop=(k == KD - 1))
            last.then_inc(dt_psum, 1)
            for n in range(U_Z, U_K):
                unit(n, rhs=hT)
            pe.wait_ge(silu_done, 4)
            for b in range(4):
                t = b // 2
                for jj in range(4):
                    j = (b % 2) * 4 + jj
                    last = nc.tensor.transpose(bank[2 + b][:, jj * P:(jj + 1) * P], xbcT[:, j, t * P:(t + 1) * P], ident)
                last.then_inc(xN_psum, 1)
            pe.wait_ge(silu_done, 6)
            pe.wait_ge(dt_in, 1)
            for g in range(2):
                for i in range(TT):
                    last = nc.tensor.matmul(bank[6 + g][:, i * 256:(i + 1) * 256], xbcT[:, 8 + g, i * P:(i + 1) * P],
                                            xbcT[:, 10 + g, :], start=True, stop=True)
                last.then_inc(cb_psum, 1)

            unit(U_K, tokens=hT)
            pe.wait_ge(a_ready, 1)
            pe.wait_ge(cb_ready, 2)
            f, b_ = slice(0, NH), slice(NH, 2 * NH)
            nc.tensor.matmul(bank[7][:, 0:16], m_le, dta[:, 0, f], start=True, stop=True)
            nc.tensor.matmul(bank[7][:, 16:32], ones, dta[:, 1, b_], start=True, stop=False)
            nc.tensor.matmul(bank[7][:, 16:32], m_ge, dta[:, 0, b_], start=False, stop=True)
            nc.tensor.matmul(bank[7][:, 32:48], ones, dta[:, 0, f], start=True, stop=False)
            nc.tensor.matmul(bank[7][:, 32:48], m_le, dta[:, 1, f], start=False, stop=True)
            nc.tensor.matmul(bank[7][:, 48:64], m_ge, dta[:, 1, b_], start=True, stop=True).then_inc(acs_psum, 1)
            unit(U_Q, tokens=hT)
            pe.wait_ge(acsN_ready, 2)
            for t in range(TT):
                last = nc.tensor.transpose(bank[7][0:32, 256 + t * P:256 + (t + 1) * P], acsN[:, t, :], ident)
            last.then_inc(acsT_psum, 1)

            def qk_transposes(v):
                pe.wait_ge(roped_ready, v + 1)
                if v == 4:
                    pe.wait_ge(qT_ready, 1)
                for hh in range(2):
                    for t in range(TT):
                        last = nc.tensor.transpose(bank[2 + v % 4][:, hh * 256 + t * P:hh * 256 + (t + 1) * P],
                                                   roped[:, t, v * 256 + hh * P:v * 256 + (hh + 1) * P], ident)
                last.then_inc(qT_psum, 1)

            pe.wait_ge(xN_ready, 4)
            qk_transposes(0)
            for v in range(1, 4):
                unit(U_Q + v, tokens=hT)
                qk_transposes(v)
            unit(U_V, tokens=hT)
            qk_transposes(4)

            def seg(g):
                for hh in range(2):
                    h = 2 * g + hh
                    if h >= 2:
                        pe.wait_ge(seg_masked, h - 1)
                    for d in range(2):
                        r = d * NH + h
                        last = nc.tensor.matmul(bank[2 + hh][:, d * 256:(d + 1) * 256],
                                                ident[0:32, r:r + 1].to_broadcast([32, P]), acsT[:, :],
                                                start=True, stop=True)
                    last.then_inc(seg_psum, 1)

            def scores(h):
                if h >= 1:
                    pe.wait_ge(sc_exp, h)
                for t in range(TT):
                    last = nc.tensor.matmul(bank[4][:, t * 256:(t + 1) * 256], qT[:, h, t * P:(t + 1) * P],
                                            kT[:, h // (AH // KVH), :], start=True, stop=True)
                last.then_inc(sc_psum, 1)

            pe.wait_ge(qT_ready, 5)
            pe.wait_ge(acsT_ready, 1)
            seg(0)
            scores(0)
            for g in range(8):
                unit(U_G + g, rhs=hT)
                pe.wait_ge(prob_ready, g + 1)
                if g >= 1:
                    pe.wait_ge(probT_ready, g)
                for i in range(TT):
                    for t in range(TT):
                        last = nc.tensor.transpose(bank[5][:, i * 256 + t * P:i * 256 + (t + 1) * P],
                                                   prob[:, t, i * P:(i + 1) * P], ident)
                last.then_inc(probT_psum, 1)
                if g < 7:
                    seg(g + 1)
                    scores(g + 1)
                if g >= 1:
                    pe.wait_ge(yz_ready, 2 * g - 1)
                for hh in range(2):
                    pe.wait_ge(g_ready, 2 * g + hh + 1)
                    for i in range(TT):
                        last = nc.tensor.matmul(bank[7][hh * HD:(hh + 1) * HD, 0:256],
                                                hN[:, i, (2 * g + hh) * HD:(2 * g + hh + 1) * HD],
                                                gbuf[:, g % 2, hh, i, :], start=(i == 0), stop=(i == TT - 1))
                last.then_inc(y_psum, 1)
                pe.wait_ge(probT_ready, g + 1)
                if g >= 1:
                    pe.wait_ge(o_ready, g)
                for i in range(TT):
                    kv = g // (AH // KVH)
                    last = nc.tensor.matmul(bank[6][:, 0:256], vN[:, i, kv * AD:(kv + 1) * AD], probT[:, i, :],
                                            start=(i == 0), stop=(i == TT - 1))
                last.then_inc(o_psum, 1)

            pe.wait_ge(o_ready, 8)
            unit(U_BA, rhs=qT)
            pe.wait_ge(ysq_added, 8)
            for t in range(TT):
                last = nc.tensor.matmul(bank[7][:, 256 + t * 16:272 + t * 16], sqacc[:, t * P:(t + 1) * P], ones[:, 0:16],
                                        start=True, stop=True)
            last.then_inc(ssq_psum, 1)
            unit(U_BA + 1, rhs=qT)
            unit(U_BA + 2, rhs=qT)
            pe.wait_ge(diag_ready, 1)
            nc.tensor.matmul(bank[7][:, 256:512], ones, sqb, start=True, stop=True).then_inc(rB_psum, 1)
            unit(U_BA + 3, rhs=qT)
            pe.wait_ge(yg_ready, 8)
            for n in range(U_BS, U_O):
                unit(n, rhs=xbcT)
            pe.wait_ge(mix_ready, 4)
            for n in range(U_O, N_MIX):
                unit(n, tokens=hT)

            to_T(h2_ready, h2T_psum)
            pe.wait_ge(h2T_ready, 4)
            pe.wait_ge(late_in, 16 * 2)
            for t in range(TT):
                for k in range(KD):
                    last = nc.tensor.matmul(bank[6][:, t * NE:(t + 1) * NE], hT[:, k, t * P:(t + 1) * P], wr[:, k, :],
                                            start=(k == 0), stop=(k == KD - 1))
            last.then_inc(lg_psum, 1)
            pe.wait_ge(w_ready, 1)
            nc.tensor.matmul(bank[7][:, 0:NE], m_le, msk[:, 0, :], start=True, stop=True)
            nc.tensor.matmul(bank[7][:, NE:2 * NE], ones, msk[:, 0, :], start=True, stop=False)
            nc.tensor.matmul(bank[7][:, NE:2 * NE], m_le, msk[:, 1, :], start=False, stop=True)
            nc.tensor.matmul(bank[7][:, 2 * NE:3 * NE], ones, msk[:, 0, :], start=True, stop=False)
            nc.tensor.matmul(bank[7][:, 2 * NE:3 * NE], ones, msk[:, 1, :], start=False, stop=True)
            pe.wait_ge(w_ready, 2)
            for t in range(TT):
                last = nc.tensor.transpose(bank[0][0:NE, t * P:(t + 1) * P], wtok[:, t, 0:NE], ident)
            last.then_inc(wT_psum, 1)
            def gather(par, b):
                for k in range(KD):
                    for t in range(TT):
                        for part in (2, 1, 0):
                            last = nc.tensor.matmul(bank[b][:, k * CAP:(k + 1) * CAP], hb[part][:, t, k * P:(k + 1) * P],
                                                    slotP[:, par, t, :], start=(t == 0 and part == 2),
                                                    stop=(t == TT - 1 and part == 0))
                return last

            def slot_transposes(par, b):
                for t in range(TT):
                    last = nc.tensor.transpose(bank[b][:, t * P:(t + 1) * P], slotW[:, par, t, :], ident)
                return last

            def combine(q, rows, b0=SUMS, start=False, stop=False):
                return nc.tensor.matmul(bank[b0 + q][:, :], slotWT[0:rows, (q // 2) * P:(q // 2 + 1) * P],
                                        ysb[0:rows, (q % 2) * 512:(q % 2 + 1) * 512], start=start, stop=stop,
                                        skip_group_check=True)

            def layer_unit(i, c, q, tokens, tokens32, blocks, first, last_k, bank_sem=None, wait_bank=None):
                u = c * EXP_UNITS + q
                nb = len(blocks)
                tiles = UNIT // (512 * nb)
                k0 = q if tiles == 1 else 2 * (q - KD)
                if q in DIRECT:
                    moe_full(pe, i, u)
                    w = ring[:, moe_slot(u), :]
                    for a in range(tiles):
                        for n, b in blocks:
                            o = (a * nb + n) * 512
                            last = nc.tensor.matmul(bank[b][0:CAP, :], tokens32[:, k0 + a, :], w[:, o:o + 512],
                                                    start=False, stop=False, skip_group_check=True)
                    last.then_inc(unit_done, 1)
                    return
                _, sn = split_at(c, SPLIT.index(q))

                def product(part, a, n, b):
                    o = (a * nb + n) * 512
                    return nc.tensor.matmul(bank[b][:, :], tokens[:, k0 + a, :], split[:, sn % NSPLIT, part, o:o + 512],
                                            start=(q == first and a == 0 and part == 0),
                                            stop=(q == last_k and a == tiles - 1 and part == 1), skip_group_check=True)

                pe.wait_ge(hi_ready, i * (BODY * SPE) + (sn + 1))
                if q == last_k:
                    pe.wait_ge(lo_ready, i * (BODY * SPE) + (sn + 1))
                    for n, b in blocks:
                        for part in range(2):
                            for a in range(tiles):
                                last = product(part, a, n, b)
                        if b != blocks[-1][1]:
                            last.then_inc(bank_sem, 1)
                else:
                    for part in range(2):
                        if part == 1:
                            pe.wait_ge(lo_ready, i * (BODY * SPE) + (sn + 1))
                        for a in range(tiles):
                            for n, b in blocks:
                                if wait_bank and part == 0 and b == wait_bank[0]:
                                    pe.wait_ge(*wait_bank[1:])
                                last = product(part, a, n, b)
                last.then_inc(unit_done, 1)

            def transposes(n):
                for m in range(4 * n, 4 * n + 4):
                    last = nc.tensor.transpose(bank[n][:, (m % 4) * P:(m % 4 + 1) * P], hs[:, m * P:(m + 1) * P], ident)
                return last

            def expert(i, c, final):
                e = i * BODY + c
                pe.wait_ge(xs_ready, e + 1)
                pe.wait_ge(pw_ready, e + 1)
                for q in range(KD):
                    order = (1, 3, 0, 2) if q == 0 else (0, 2, 1, 3)
                    layer_unit(i, c, q, xs, x32, [(n, n) for n in order], 0, KD - 1, bank_sem=h_psum,
                               wait_bank=(0, ys_ready, e + 1) if q == 0 else None)
                for n in range(4):
                    pe.wait_ge(hs_ready, e * 4 + (n + 1))
                    transposes(BLOCKS[n]).then_inc(t_psum, 1)
                for q in range(4):
                    combine(q, P)
                for q in range(KD, EXP_UNITS):
                    if q == KD:
                        pe.wait_ge(actT_ready, 2 * e + 1)
                    elif q == KD + 2:
                        pe.wait_ge(actT_ready, 2 * e + 2)
                        slot_transposes(c % 2, 3).then_inc(pw_psum, 1)
                        if not final:
                            pe.wait_ge(p_ready, e + 2)
                            gather((c + 1) % 2, 1).then_inc(x_psum, 1)
                    layer_unit(i, c, q, as_, act32, ((0, 0), (1, 2)), KD, EXP_UNITS - 1, bank_sem=y_half)

            pe.wait_ge(p_ready, 1)
            pe.wait_ge(hb_ready, 3)
            gather(0, 1).then_inc(x_psum, 1)
            pe.wait_ge(wT_ready, 1)
            for t in range(TT):
                for hf in range(2):
                    if t == 1 and hf == 1:
                        pe.wait_ge(route_ready, 1)
                    nc.tensor.matmul(bank[SUMS + 2 * t + hf][:, :], wT[:, t * P:(t + 1) * P],
                                     b2s[:, hf * 512:(hf + 1) * 512],
                                     start=True, stop=False, skip_group_check=True).then_inc(b2_psum, 1)
            with pe.Fori(0, NE // BODY - 1) as i:
                for c in range(BODY):
                    expert(i, c, False)
            for c in range(BODY):
                expert(NE // BODY - 1, c, c == BODY - 1)
            pe.wait_ge(ys_ready, 1 + NE)
            pe.wait_ge(pw_ready, NE + 1)
            for q in range(4):
                combine(q, P, stop=True).then_inc(c_psum, 1)

            pe.wait_ge(route_ready, 1)
            again = pe.value_load(over_i[0:1, 0:1], min_val=0, max_val=1)
            with pe.If(again > 0):
                pe.wait_ge(c_added, 4)
                nc.tensor.transpose(bank[7][:, 0:P], ident, ident).then_inc(over_y, 1)
                with pe.Fori(0, NE) as e:
                    for r in range(NPASS - 1):
                        n = e * (NPASS - 1) + (r + 1)
                        pe.wait_ge(over_place, n)
                        gather(0, 6)
                        slot_transposes(0, 7).then_inc(over_x, 1)
                        pe.wait_ge(over_xr, n)
                        pe.wait_ge(over_full, n * (16 * EXP_UNITS) - 16 * (EXP_UNITS - KD))
                        for k in range(KD):
                            for m in range(16):
                                last = nc.tensor.matmul(bank[4 + m // 8][:, (m % 8) * CAP:(m % 8 + 1) * CAP],
                                                        ring[:, k, m * P:(m + 1) * P], x32[:, k, :],
                                                        start=(k == 0 and m % 8 == 0), stop=(k == KD - 1 and m % 8 == 7),
                                                        skip_group_check=True)
                        last.then_inc(over_h, 1)
                        pe.wait_ge(over_act, n)
                        pe.wait_ge(over_full, n * (16 * EXP_UNITS))
                        for k in range(KD):
                            for hf in range(2):
                                o = (k % 2) * D + hf * 512
                                last = nc.tensor.matmul(bank[hf][0:CAP, :], act32[:, k, :], ring[:, k // 2, o:o + 512],
                                                        start=(k == 0), stop=(k == KD - 1))
                        last.then_inc(over_y, 1)
                        pe.wait_ge(over_ys, n)
                        for q in range(4):
                            last = combine(q, CAP, b0=0, start=True, stop=True)
                        last.then_inc(over_c, 1)

        @block.scalar
        def _(act):
            link = chain(act, act_step)
            act.dma_start(xres[:, :, :], x[0].rearrange("(t p) d -> p t d", p=P)).then_inc(x_in, 16)
            act.dma_start(cst[:, :], consts).then_inc(c_in, 16)
            for r, src in ((R_GMIX, g_mix[0].rearrange("(k p) -> k p", p=P)), (R_GSSM, g_ssm[0].rearrange("(k p) -> k p", p=P)),
                           (R_GFFN, g_ffn[0].rearrange("(k p) -> k p", p=P)), (R_CB, conv_b[0].rearrange("(k p) -> k p", p=P)),
                           (R_CW, conv_w[0].rearrange("j (k p) -> (j k) p", p=P))):
                act.dma_start(prm[r:r + src.shape[0], :], src).then_inc(row_in, 16)
            act.dma_start(dskr[:, :], d_skip[0].rearrange("(j h) -> j h", h=2)).then_inc(dsk_in, 16)
            act.dma_start(b1raw, b_mlp1[0]).then_inc(b1_in, 16)
            act.dma_start(wdt[:, :, :], w_in[0].rearrange("(k p) n -> p k n", p=P)[:, :, DT0:DT0 + 2 * NH]).then_inc(wdt_in, 16)
            at = 0
            for v in (dt_bias_f, dt_bias_b, a_log_f, a_log_b, b_router, k_norm_g, q_norm_g):
                act.dma_start(vec[:, at:at + v.shape[1]], v[0].partition_broadcast(P)).then_inc(vec_in, 16)
                at += v.shape[1]
            act.dma_start(wr[:, :, :], w_router[0].rearrange("(k p) n -> p k n", p=P)).then_inc(late_in, 16)

            act.wait_ge(x_in, 16)
            for t in range(TT):
                nc.scalar.activation(hN[:, t, :], xres[:, t, :], ACT.Square, accum_out=stat[:, t:t + 1]).then_inc(xsq_ready, 1)
            act.wait_ge(prm_ready, 1)
            nc.scalar.activation(prmT[:, :], bank[6][:, 0:N_ROWS + 8], ACT.Copy).then_inc(prm_taken, 1)
            act.wait_ge(prm_ready, 2)
            nc.scalar.activation(b1T[:, :, :], bank[7][:, :].rearrange("p (m e) -> p e m", m=16), ACT.Copy).then_inc(prm_taken, 1)

            def silu(u):
                act.wait_ge(conv_done, u + 1)
                nc.scalar.activation(xbcT[:, 2 * u:2 * u + 2, :], xbcT[:, 2 * u:2 * u + 2, :], ACT.Silu).then_inc(silu_done, 1)

            for u in range(6):
                act.wait_ge(unit_done, U_XBC + u + 1)
                if u >= 2:
                    act.wait_ge(conv_done, u - 1)
                else:
                    act.wait_ge(pool_step, 1)
                nc.scalar.activation(xp[:, u % 2, :, PAD:PAD + SEQ], bank[(U_XBC + u) % 2][:, :].rearrange("p (m l) -> p m l", m=2),
                                     ACT.Copy).then_inc(unit_taken, 1)
                if u >= 1:
                    silu(u - 1)
            silu(5)
            for u in range(4):
                act.wait_ge(unit_done, U_Z + u + 1)
                nc.scalar.activation(siluz[:, 2 * u:2 * u + 2, :], bank[(U_Z + u) % 2][:, :].rearrange("p (m l) -> p m l", m=2),
                                     ACT.Silu).then_inc(unit_taken, 1)
            for b in range(4):
                act.wait_ge(xN_psum, b + 1)
                t = b // 2
                nc.scalar.activation(hN[:, t, (b % 2) * 512:(b % 2 + 1) * 512], bank[2 + b][:, :], ACT.Copy).then_inc(xN_ready, 1)
            for g in range(2):
                act.wait_ge(cb_psum, g + 1)
                nc.scalar.activation(cb[:, g, :, :], bank[6 + g][:, :].rearrange("p (i l) -> p i l", i=TT), ACT.Copy).then_inc(cb_ready, 1)
            act.wait_ge(dt_in, 1)
            act.wait_ge(vec_in, 16 * 7)
            nc.scalar.activation(dtu[:, :, :], dta[:, :, :], ACT.Exp, scale=-1.0).then_inc(dt_exp, 1)
            nc.scalar.activation(alog_b, alog_b, ACT.Exp).then_inc(dt_exp, 1)

            def qk_square(v, n):
                act.wait_ge(unit_done, n + 1)
                nc.scalar.activation(qk[:, :, v * 256:(v + 1) * 256], bank[n % 2][:, :].rearrange("p (t c) -> p t c", t=TT),
                                     ACT.Copy).then_inc(unit_taken, 1)
                act.wait_ge(unit_taken, n + 1)
                nc.scalar.activation(roped[:, :, v * 256:(v + 1) * 256], qk[:, :, v * 256:(v + 1) * 256], ACT.Square).then_inc(qsq_ready, 1)

            def qT_copy(v):
                act.wait_ge(qT_psum, v + 1)
                dst = kT if v == 0 else qT[:, 2 * v - 2:2 * v, :]
                nc.scalar.activation(dst, bank[2 + v % 4][:, :].rearrange("p (h l) -> p h l", h=2), ACT.Copy).then_inc(qT_ready, 1)

            qk_square(0, U_K)
            qk_square(1, U_Q)
            act.wait_ge(acsT_psum, 1)
            nc.scalar.activation(acsT[:, :], bank[7][0:32, 256:512], ACT.Copy).then_inc(acsT_ready, 1)
            for v in range(2, 5):
                qk_square(v, U_Q + v - 1)
                qT_copy(v - 2)
            qT_copy(3)
            act.wait_ge(unit_done, U_V + 1)
            nc.scalar.activation(vN[:, :, :], bank[U_V % 2][:, :].rearrange("p (t c) -> p t c", t=TT), ACT.Copy).then_inc(unit_taken, 1)
            qT_copy(4)

            def seg_exps(g):
                for hh in range(2):
                    act.wait_ge(seg_masked, 2 * g + hh + 1)
                    nc.scalar.activation(ebuf[:, hh, :], ebuf[:, hh, :], ACT.Exp).then_inc(seg_exp, 1)

            def score_exps(h):
                act.wait_ge(sc_max, h + 1)
                if h >= 1:
                    act.wait_ge(probT_psum, h)
                for t in range(TT):
                    last = nc.scalar.activation(prob[:, t, :], bank[4][:, t * 256:(t + 1) * 256], ACT.Exp,
                                                bias=stat[:, 12 + t:13 + t], scale=float(AD) ** -0.5,
                                                accum_out=stat[:, 14 + t:15 + t])
                last.then_inc(sc_exp, 1)

            score_exps(0)
            seg_exps(0)
            for g in range(8):
                act.wait_ge(unit_done, U_G + g + 1)
                nc.scalar.activation(sig[:, 2 * g:2 * g + 2, :], bank[(U_G + g) % 2][:, :].rearrange("p (m l) -> p m l", m=2),
                                     ACT.Exp, scale=-1.0).then_inc(unit_taken, 1)
                act.wait_ge(probT_psum, g + 1)
                if g >= 1:
                    act.wait_ge(o_psum, g)
                nc.scalar.activation(probT[:, :, :], bank[5][:, :].rearrange("p (i q) -> p i q", i=TT), ACT.Copy).then_inc(probT_ready, 1)
                if g < 7:
                    score_exps(g + 1)
                    seg_exps(g + 1)
                act.wait_ge(o_psum, g + 1)
                nc.scalar.activation(qT[:, g, :], bank[6][:, 0:256], ACT.Copy).then_inc(o_ready, 1)
                act.wait_ge(yz_ready, 2 * g + 2)
                if g >= 1:
                    act.wait_ge(ysq_added, g)
                nc.scalar.activation(sqb, xbcT[:, g, :], ACT.Square).then_inc(ysq_ready, 1)
                nc.scalar.activation(xbcT[:, g, :], xbcT[:, g, :], ACT.Copy, scale=prmT[:, R_GSSM + g:R_GSSM + g + 1]).then_inc(yg_ready, 1)
            act.dma_start(b2s, b_mlp2[0]).then_inc(late_in, 16)
            act.wait_ge(ssq_psum, 1)
            nc.scalar.activation(stat[:, 34:36], bank[7][:, 256:288].rearrange("p (t a) -> p a t", t=TT)[:, 0, :],
                                 ACT.Copy, bias=EPS, scale=1.0 / D).then_inc(ssq_ready, 1)
            act.wait_ge(rB_psum, 1)
            nc.scalar.activation(rB, bank[7][:, 256:512], ACT.Copy).then_inc(rB_ready, 1)

            def hi_split(i, c, n):
                u, sn = split_at(c, n)
                moe_full(act, i, u)
                nc.scalar.activation(split[:, sn % NSPLIT, 0, :], ring[:, moe_slot(u), :], ACT.Copy).then_inc(hi_ready, 1)

            act.wait_ge(unit_done, U_O)
            act.wait_ge(mix_ready, 4)
            for n in range(NSPLIT):
                hi_split(0, 0, n)
            act.wait_ge(unit_taken, N_MIX)
            for t in range(TT):
                nc.scalar.activation(hN[:, t, :], xres[:, t, :], ACT.Square, accum_out=stat[:, 20 + t:21 + t]).then_inc(x1sq_ready, 1)
            act.wait_ge(h2_ready, 2)
            nc.scalar.activation(hb1[:, :, :], hN[:, :, :], ACT.Copy).then_inc(hb_ready, 1)
            act.wait_ge(res_ready, 1)
            nc.scalar.activation(hb2[:, :, :], hs, ACT.Copy).then_inc(hb_ready, 1)
            act.wait_ge(lmax_ready, 1)
            for t in range(TT):
                last = nc.scalar.activation(lgt[:, t, :], lgt[:, t, :], ACT.Exp, bias=stat[:, 26 + t:27 + t])
            last.then_inc(lexp_ready, 1)
            act.wait_ge(res_ready, 2)
            nc.scalar.activation(hb3[:, :, :], hs, ACT.Copy).then_inc(hb_ready, 1)
            act.wait_ge(wT_psum, 1)
            nc.scalar.activation(wT[:, :], bank[0][0:NE, 0:SEQ], ACT.Copy).then_inc(wT_ready, 1)
            act.wait_ge(wT_ready, 1)
            act.dma_start(gfin, g_final.partition_broadcast(P)).then_inc(gfin_in, 16)


            def expert(i, c, final):
                e = i * BODY + c
                for n in range(NSPLIT, PRE):
                    buffer_free(act, i, c, n)
                    hi_split(i, c, n)
                for n in range(4):
                    if n < 3:
                        act.wait_ge(h_psum, e * 3 + (n + 1))
                    else:
                        unit_used(act, i, c * EXP_UNITS + KD - 1)
                    m = BLOCKS[n]
                    nc.scalar.activation(hs[:, m * 512:(m + 1) * 512], bank[m][:, :], ACT.Copy).then_inc(hs_ready, 1)
                for n in range(PRE, SPE):
                    buffer_free(act, i, c, n)
                    hi_split(i, c, n)
                for h in range(2):
                    act.wait_ge(ga_ready, 2 * e + (h + 1))
                    nc.scalar.activation(sg[:, h * 256:(h + 1) * 256], ga[:, h * 256:(h + 1) * 256], ACT.Sigmoid,
                                         scale=ALPHA).then_inc(sg_ready, 1)
                if not final:
                    buffer_free(act, i, c + 1, 0)
                    hi_split(i, c + 1, 0)
                act.wait_ge(pw_psum, e + 1)
                nc.scalar.activation(slotWT, bank[3][:, 0:256], ACT.Copy).then_inc(pw_ready, 1)
                if not final:
                    for n in (1, 2):
                        buffer_free(act, i, c + 1, n)
                        hi_split(i, c + 1, n)
                act.wait_ge(y_half, e + 1)
                nc.scalar.activation(ysb[:, 0:512], bank[0][:, :], ACT.Copy)
                unit_used(act, i, c * EXP_UNITS + EXP_UNITS - 1)
                nc.scalar.activation(ysb[:, 512:1024], bank[2][:, :], ACT.Copy).then_inc(ys_ready, 1)
                if not final:
                    buffer_free(act, i, c + 1, 3)
                    hi_split(i, c + 1, 3)

            with act.Fori(0, NE // BODY - 1) as i:
                for c in range(BODY):
                    expert(i, c, False)
            for c in range(BODY):
                expert(NE // BODY - 1, c, c == BODY - 1)

            act.wait_ge(route_ready, 1)
            again = act.value_load(over_i[0:1, 0:1], min_val=0, max_val=1)
            with act.If(again > 0):
                with act.Fori(0, NE) as e:
                    for r in range(NPASS - 1):
                        n = e * (NPASS - 1) + (r + 1)
                        act.wait_ge(over_x, n)
                        nc.scalar.activation(slotWT, bank[7][:, 0:256], ACT.Copy)
                        act.wait_ge(over_ga, n)
                        nc.scalar.activation(sg, ga, ACT.Sigmoid, scale=ALPHA).then_inc(over_sg, 1)
                        act.wait_ge(over_y, n + 1)
                        nc.scalar.activation(ysb[0:CAP, 0:512], bank[0][0:CAP, :], ACT.Copy)
                        nc.scalar.activation(ysb[0:CAP, 512:1024], bank[1][0:CAP, :], ACT.Copy).then_inc(over_ys, 1)

            act.wait_ge(sum_done, 1)
            for t in range(TT):
                nc.scalar.activation(hN[:, t, :], xres[:, t, :], ACT.Square, accum_out=stat[:, 30 + t:31 + t]).then_inc(fsq_ready, 1)

        @block.gpsimd
        def _(pool):
            link = chain(pool, pool_step)
            link(nc.gpsimd.memset(xp, 0.0))
            nc.gpsimd.memset(stat[:, 40:64], -0.5).then_inc(pool_step, 1)
            nc.gpsimd.memset(sqacc, 0.0).then_inc(pool_step, 1)
            pool.wait_ge(pool_step, 3)
            link.count[0] = 3

            def rsqrt_mean(o, n, count):
                link(nc.gpsimd.tensor_scalar(stat[:, o:o + n], stat[:, o:o + n], 1.0 / count, EPS, ALU.mult, ALU.add))
                return nc.gpsimd.tensor_tensor(stat[:, o:o + n], stat[:, o:o + n], stat[:, 40:40 + n], ALU.pow)

            pool.wait_ge(xsq_ready, 2)
            rsqrt_mean(0, TT, D).then_inc(xr_ready, 1)
            for v in range(5):
                pool.wait_ge(qr_ready, 2 * v + 1)
                rsqrt_mean(4, 4, AD).then_inc(qr_ready, 1)
            for g in range(8):
                pool.wait_ge(ysq_ready, g + 1)
                nc.gpsimd.tensor_tensor(sqacc, sqacc, sqb, ALU.add).then_inc(ysq_added, 1)
                pool.wait_ge(ysq_added, g + 1)
            pool.wait_ge(ssq_ready, 1)
            nc.gpsimd.tensor_tensor(stat[:, 34:36], stat[:, 34:36], stat[:, 40:42], ALU.pow).then_inc(yr_ready, 1)
            pool.wait_ge(x1sq_ready, 2)
            rsqrt_mean(20, TT, D).then_inc(x1r_ready, 1)
            pool.wait_ge(fsq_ready, 2)
            rsqrt_mean(30, TT, D).then_inc(fr_ready, 1)

        @block.vector
        def _(dve):
            link = chain(dve, dve_step)
            V = nc.vector
            dve.wait_ge(dsk_in, 16)
            V.tensor_copy(dske[:, :].rearrange("j (h p) -> j h p", h=2),
                          dskr[:, :].unsqueeze(2).to_broadcast([8, 2, HD])).then_inc(dsk_ready, 1)
            dve.wait_ge(xr_ready, 1)
            for t in range(TT):
                V.tensor_scalar(hN[:, t, :], xres[:, t, :], stat[:, t:t + 1], None, ALU.mult).then_inc(h_ready, 1)
            dve.wait_ge(prm_taken, 1)

            def scaled_T(psum_sem, ready, row):
                for b in range(4):
                    dve.wait_ge(psum_sem, b + 1)
                    V.tensor_tensor(hT[:, 2 * b:2 * b + 2, :], bank[2 + b][:, :].rearrange("p (k l) -> p k l", k=2),
                                    prmT[:, row + 2 * b:row + 2 * b + 2].unsqueeze(2).to_broadcast([P, 2, SEQ]), ALU.mult).then_inc(ready, 1)

            scaled_T(hT_psum, hT_ready, R_GMIX)
            for u in range(6):
                dve.wait_ge(unit_taken, U_XBC + u + 1)
                for j in range(CONV):
                    for mm in range(2):
                        m = 2 * u + mm
                        wcol = prmT[:, R_CW + j * XBC_TILES + m:R_CW + j * XBC_TILES + m + 1]
                        src = xp[:, u % 2, mm, j:j + SEQ]
                        if j == 0:
                            last = V.tensor_scalar(xbcT[:, m, :], src, wcol, prmT[:, R_CB + m:R_CB + m + 1], ALU.mult, ALU.add)
                        else:
                            last = V.scalar_tensor_tensor(xbcT[:, m, :], src, wcol, xbcT[:, m, :], ALU.mult, ALU.add)
                    if j < CONV - 1:
                        link(last)
                last.then_inc(conv_done, 1)
            dve.wait_ge(dt_psum, 1)
            dve.wait_ge(vec_in, 16 * 7)
            link(V.tensor_tensor(dtv[:, :, :], bank[6][:, 0:64].rearrange("p (t c) -> p t c", t=TT),
                                 dtb_b.unsqueeze(1).to_broadcast([P, TT, 32]), ALU.add))
            V.scalar_tensor_tensor(dta[:, :, :], dtv[:, :, :], -1.0, dtv[:, :, :], ALU.mult, ALU.max).then_inc(dt_in, 1)
            dve.wait_ge(dt_exp, 2)
            link(V.tensor_scalar(dta[:, :, :], dtu[:, :, :], 2.0, None, ALU.add))
            link(V.reciprocal(dta[:, :, :], dta[:, :, :]))
            link(V.tensor_tensor(dtu[:, :, :], dtu[:, :, :], dta[:, :, :], ALU.mult))
            link(V.tensor_tensor(acsN[:, :, :], dtu[:, :, :], dtu[:, :, :], ALU.mult))
            link(V.tensor_scalar(dta[:, :, :], acsN[:, :, :], 1.0 / 19, None, ALU.mult))
            for k in range(17, 1, -2):
                link(V.scalar_tensor_tensor(dta[:, :, :], dta[:, :, :], 1.0 / k, acsN[:, :, :], ALU.add, ALU.mult))
            link(V.scalar_tensor_tensor(dta[:, :, :], dta[:, :, :], 1.0, dtu[:, :, :], ALU.add, ALU.mult))
            link(V.tensor_scalar(dtv[:, :, :], dtv[:, :, :], 0.0, None, ALU.max))
            link(V.scalar_tensor_tensor(dtv[:, :, :], dta[:, :, :], 2.0, dtv[:, :, :], ALU.mult, ALU.add))
            V.scalar_tensor_tensor(dta[:, :, :], dtv[:, :, :], -1.0, alog_b.unsqueeze(1).to_broadcast([P, TT, 32]),
                                   ALU.mult, ALU.mult).then_inc(a_ready, 1)

            def rope(v):
                raw = qk[:, :, v * 256:(v + 1) * 256].rearrange("p t (h d) -> p t h d", h=2)
                new = roped[:, :, v * 256:(v + 1) * 256].rearrange("p t (h d) -> p t h d", h=2)
                tmp = ropeb[:, :, :].rearrange("p t (h d) -> p t h d", h=2)
                ss = stat[:, 4:8].rearrange("p (t h) -> p t h", t=TT)
                dve.wait_ge(qsq_ready, v + 1)
                V.tensor_reduce(ss, new, AXX, ALU.add).then_inc(qr_ready, 1)
                dve.wait_ge(qr_ready, 2 * v + 2)
                link(V.tensor_tensor(raw, raw, ss.unsqueeze(3).to_broadcast([P, TT, 2, AD]), ALU.mult))
                gb = (kg_b if v == 0 else qg_b).unsqueeze(1).unsqueeze(1).to_broadcast([P, TT, 2, AD])
                link(V.tensor_tensor(raw, raw, gb, ALU.mult))
                for t in range(TT):
                    cosv = cst[:, C_COS + t * AD:C_COS + (t + 1) * AD].unsqueeze(1).to_broadcast([P, 2, AD])
                    V.tensor_tensor(new[:, t], raw[:, t], cosv, ALU.mult)
                    for hf in range(2):
                        o = hf * 32
                        sn = cst[:, C_SIN + t * AD:C_SIN + (t + 1) * AD].rearrange("p (a c) -> p a c", a=2)[:, :, o:o + 32]
                        last = V.tensor_tensor(tmp[:, t].rearrange("p h (a c) -> p h a c", a=2)[:, :, :, o:o + 32],
                                               raw[:, t].rearrange("p h (a c) -> p h a c", a=2)[:, :, :, 32 - o:64 - o],
                                               sn.unsqueeze(1).to_broadcast([P, 2, 2, 32]), ALU.mult)
                link(last)
                V.tensor_tensor(new, new, tmp, ALU.add).then_inc(roped_ready, 1)

            rope(0)
            dve.wait_ge(acs_psum, 1)
            V.tensor_copy(acsN[:, :, :], bank[7][:, 0:64].rearrange("p (t c) -> p t c", t=TT)).then_inc(acsN_ready, 1)
            V.tensor_scalar(nacs[:, :, :], bank[7][:, 0:64].rearrange("p (t c) -> p t c", t=TT), -1.0, None, ALU.mult).then_inc(acsN_ready, 1)
            for v in range(1, 5):
                rope(v)

            def seg_mask(g):
                for hh in range(2):
                    h = 2 * g + hh
                    dve.wait_ge(seg_psum, h + 1)
                    e, b = ebuf[:, hh, :], bank[2 + hh]
                    f0, b0 = nacs[:, 0, h:h + 1], nacs[:, 0, NH + h:NH + h + 1]
                    f1, b1 = nacs[:, 1, h:h + 1], nacs[:, 1, NH + h:NH + h + 1]
                    V.scalar_tensor_tensor(e[:, 0:256], b[:, 0:256], f0, cst[:, C_NEGF:C_NEGF + 256], ALU.add, ALU.add)
                    V.scalar_tensor_tensor(e[:, 256:384], b[:, 256:384], b0, cst[:, C_NEGB:C_NEGB + P], ALU.add, ALU.add)
                    V.scalar_tensor_tensor(e[:, 384:512], b[:, 128:256], f1, cst[:, C_NEGF:C_NEGF + P], ALU.add, ALU.add)
                    V.scalar_tensor_tensor(e[:, 512:768], b[:, 256:512], b1, cst[:, C_ZERO:C_ZERO + 256], ALU.add, ALU.add).then_inc(seg_masked, 1)

            def seg_weight(g):
                if g >= 2:
                    dve.wait_ge(y_psum, g - 1)
                for hh in range(2):
                    h = 2 * g + hh
                    dve.wait_ge(seg_exp, h + 1)
                    e, o = ebuf[:, hh, :], gbuf[:, g % 2, hh, :, :]
                    f0, b0 = dtv[:, 0, h:h + 1], dtv[:, 0, NH + h:NH + h + 1]
                    f1, b1 = dtv[:, 1, h:h + 1], dtv[:, 1, NH + h:NH + h + 1]
                    V.tensor_scalar(o[:, 0, :], e[:, 0:256], f0, None, ALU.mult)
                    link(V.tensor_scalar(o[:, 1, :], e[:, 512:768], b1, None, ALU.mult))
                    V.scalar_tensor_tensor(o[:, 0, 0:P], e[:, 256:384], b0, o[:, 0, 0:P], ALU.mult, ALU.add)
                    link(V.scalar_tensor_tensor(o[:, 1, P:256], e[:, 384:512], f1, o[:, 1, P:256], ALU.mult, ALU.add))
                    V.tensor_tensor(o, o, cb[:, h // 8, :, :], ALU.mult).then_inc(g_ready, 1)

            def score_max(h):
                dve.wait_ge(sc_psum, h + 1)
                link(V.tensor_reduce(stat[:, 12:14], bank[4][:, :].rearrange("p (t s) -> p t s", t=TT), AXX, ALU.max))
                V.tensor_scalar(stat[:, 12:14], stat[:, 12:14], -(float(AD) ** -0.5), None, ALU.mult).then_inc(sc_max, 1)

            def prob_norm(h):
                dve.wait_ge(sc_exp, h + 1)
                link(V.reciprocal(stat[:, 16:18], stat[:, 14:16]))
                for t in range(TT):
                    last = V.tensor_scalar(prob[:, t, :], prob[:, t, :], stat[:, 16 + t:17 + t], None, ALU.mult)
                last.then_inc(prob_ready, 1)

            dve.wait_ge(qT_psum, 5)
            dve.wait_ge(acsN_ready, 2)
            dve.wait_ge(cb_ready, 2)
            score_max(0)
            seg_mask(0)
            prob_norm(0)
            seg_weight(0)
            for g in range(8):
                dve.wait_ge(unit_taken, U_G + g + 1)
                link(V.tensor_scalar(sig[:, 2 * g:2 * g + 2, :], sig[:, 2 * g:2 * g + 2, :], 1.0, None, ALU.add))
                V.reciprocal(sig[:, 2 * g:2 * g + 2, :], sig[:, 2 * g:2 * g + 2, :]).then_inc(gate_ready, 1)
                if g < 7:
                    seg_mask(g + 1)
                    score_max(g + 1)
                dve.wait_ge(y_psum, g + 1)
                V.scalar_tensor_tensor(xbcT[:, g, :], xbcT[:, g, :], prmT[:, N_ROWS + g:N_ROWS + g + 1], bank[7][:, 0:256],
                                       ALU.mult, ALU.add).then_inc(yz_ready, 1)
                dve.wait_ge(yz_ready, 2 * g + 1)
                V.tensor_tensor(xbcT[:, g, :], xbcT[:, g, :], siluz[:, g, :], ALU.mult).then_inc(yz_ready, 1)
                if g < 7:
                    prob_norm(g + 1)
                    seg_weight(g + 1)

            dve.wait_ge(gate_ready, 8)
            for u in range(4):
                n = U_BA + u
                dve.wait_ge(unit_done, n + 1)
                V.tensor_tensor(hT[:, 2 * u:2 * u + 2, :], bank[n % 2][:, :].rearrange("p (m l) -> p m l", m=2),
                                sig[:, KD + 2 * u:KD + 2 * u + 2, :], ALU.mult).then_inc(unit_taken, 1)
                if u == 1:
                    dve.wait_ge(yr_ready, 1)
                    for t in range(TT):
                        last = V.tensor_scalar(sqb[:, t * P:(t + 1) * P], ident, stat[:, 34 + t:35 + t], None, ALU.mult)
                    last.then_inc(diag_ready, 1)
            dve.wait_ge(unit_taken, U_BS)
            dve.wait_ge(rB_ready, 1)
            for u in range(4):
                n = U_BS + u
                dve.wait_ge(unit_done, n + 1)
                s = sig[:, 2 * u:2 * u + 2, :]
                link(V.tensor_tensor(s, s, rB.unsqueeze(1).to_broadcast([P, 2, SEQ]), ALU.mult))
                V.tensor_tensor(s, s, bank[n % 2][:, :].rearrange("p (m l) -> p m l", m=2), ALU.mult).then_inc(unit_taken, 1)
                dve.wait_ge(unit_taken, n + 1)
                V.tensor_tensor(hT[:, 2 * u:2 * u + 2, :], hT[:, 2 * u:2 * u + 2, :], s, ALU.add).then_inc(mix_ready, 1)

            def lo_split(i, c, n):
                u, sn = split_at(c, n)
                dve.wait_ge(hi_ready, i * (BODY * SPE) + (sn + 1))
                V.tensor_tensor(split[:, sn % NSPLIT, 1, :], ring[:, moe_slot(u), :],
                                split[:, sn % NSPLIT, 0, :].bitcast(F32), ALU.subtract).then_inc(lo_ready, 1)

            for u in range(4):
                n = U_O + u
                dve.wait_ge(unit_done, n + 1)
                x_ = xres[:, :, u * UW:(u + 1) * UW]
                V.tensor_tensor(x_, x_, bank[n % 2][:, :].rearrange("p (t c) -> p t c", t=TT), ALU.add).then_inc(unit_taken, 1)
                lo_split(0, 0, u)
            dve.wait_ge(x1r_ready, 1)
            for t in range(TT):
                V.tensor_scalar(hN[:, t, :], xres[:, t, :], stat[:, 20 + t:21 + t], None, ALU.mult).then_inc(h2_ready, 1)
            scaled_T(h2T_psum, h2T_ready, R_GFFN)
            hs3 = hs.rearrange("p (t d) -> p t d", t=TT)
            dve.wait_ge(hb_ready, 1)
            V.tensor_tensor(hs3, hN[:, :, :], hb1[:, :, :], ALU.subtract).then_inc(res_ready, 1)

            dve.wait_ge(lg_psum, 1)
            link(V.tensor_tensor(lgt, bank[6][:, 0:64].rearrange("p (t e) -> p t e", t=TT),
                                 brt_b.unsqueeze(1).to_broadcast([P, TT, NE]), ALU.add))
            for t in range(TT):
                last = V.max(top8[:, t, :], lgt[:, t, :])
            link(last)
            V.tensor_scalar(stat[:, 26:28], top8[:, :, 0:1].rearrange("p t a -> p (t a)"), -1.0, None, ALU.mult)
            for t in range(TT):
                v4 = top8[:, t, TOPK - 1:TOPK]
                V.tensor_scalar(msk[:, t, :], lgt[:, t, :], v4, None, ALU.is_gt)
                last = V.tensor_scalar(eqm[:, t, :], lgt[:, t, :], v4, None, ALU.is_equal)
            last.then_inc(lmax_ready, 1)
            dve.wait_ge(lmax_ready, 1)
            link(V.tensor_reduce(stat[:, 28:30], msk, AXX, ALU.add))
            V.tensor_scalar(stat[:, 28:30], stat[:, 28:30], -1.0, float(TOPK), ALU.mult, ALU.add)
            for t in range(TT):
                last = V.tensor_tensor_scan(eqc[:, t, :], eqm[:, t, :], eqm[:, t, :], 0.0, ALU.add, ALU.bypass)
            link(last)
            for t in range(TT):
                last = V.scalar_tensor_tensor(eqm[:, t, :], eqc[:, t, :], stat[:, 28 + t:29 + t], eqm[:, t, :], ALU.is_le, ALU.mult)
            link(last)
            V.tensor_tensor(msk, msk, eqm, ALU.add).then_inc(w_ready, 1)
            dve.wait_ge(w_ready, 1)
            dve.wait_ge(lexp_ready, 1)
            link(V.memset(wtok[:, :, NE:NE + 1], 0.0))
            link(V.tensor_tensor(wtok[:, :, 0:NE], lgt, msk, ALU.mult))
            link(V.tensor_reduce(stat[:, 32:34], wtok[:, :, 0:NE], AXX, ALU.add))
            link(V.reciprocal(stat[:, 32:34], stat[:, 32:34]))
            V.tensor_tensor(wtok[:, :, 0:NE], wtok[:, :, 0:NE], stat[:, 32:34].unsqueeze(2).to_broadcast([P, TT, NE]),
                            ALU.mult).then_inc(w_ready, 1)
            dve.wait_ge(hb_ready, 2)
            V.tensor_tensor(hs3, hs3, hb2[:, :, :], ALU.subtract).then_inc(res_ready, 1)
            dve.wait_ge(wT_psum, 1)
            link(V.memset(rankm[:, :, :], -1.0))
            link(V.tensor_tensor(rankm[:, :, 0:NE], bank[7][:, 0:2 * NE].rearrange("p (t e) -> p t e", t=TT), msk, ALU.mult))
            link(V.tensor_scalar(rankm[:, :, 0:NE], rankm[:, :, 0:NE], -1.0, None, ALU.add))
            link(V.tensor_reduce(cnt[:, 0:1], bank[7][:, 2 * NE:3 * NE], AXX, ALU.max))
            link(V.tensor_scalar(cnt[:, 1:2], cnt[:, 0:1], float(CAP), None, ALU.is_gt))
            V.tensor_copy(over_i[:, :], cnt[:, 1:2]).then_inc(route_ready, 1)

            V.memset(slotWT, 0.0).then_inc(pw_ready, 1)

            def place(e, c, shift=0):
                for t in range(TT):
                    rk = rankm[:, t, bass.ds(e, 1)]
                    wk = wtok[:, t, bass.ds(e, 1)]
                    if shift:
                        link2(V.tensor_scalar(eqc[:, t, 0:1], rk, -float(shift), None, ALU.add))
                        rk = eqc[:, t, 0:1]
                    V.tensor_scalar(slotP[:, c % 2, t, :], iota, rk, None, ALU.is_equal)
                    V.tensor_scalar(slotW[:, c % 2, t, 0:CAP], iota, rk, wk, ALU.is_equal, ALU.mult)
                    last = V.tensor_scalar(slotW[:, c % 2, t, CAP:P], iota, rk, wk, ALU.is_equal, ALU.mult)
                return last

            def tokens_in(b):
                return V.tensor_tensor(x32, bank[b][:, :].rearrange("p (k s) -> p k s", k=KD),
                                       prmT[:, R_GFFN:R_GFFN + KD].unsqueeze(2).to_broadcast([P, KD, CAP]), ALU.mult)

            def hi_lo(step, src, dst):
                step(V.tensor_copy(dst[:, :, 0:CAP], src))
                return V.tensor_tensor(dst[:, :, CAP:P], src, dst[:, :, 0:CAP].bitcast(F32), ALU.subtract)

            def activations(step, e, h):
                bias = b1T[:, bass.ds(e, 1), :].rearrange("p a m -> p (a m)")
                half = slice(4 * h * CAP, 4 * (h + 1) * CAP)
                g_, u_, s_ = ga[:, half], ub[:, half], sg[:, half]
                for part in range(2):
                    for o, b, m0 in ((g_, h, 4 * h), (u_, 2 + h, KD + 4 * h)):
                        o3 = o.rearrange("p (m s) -> p m s", m=4)
                        src = bank[b][:, :].rearrange("p (m a s) -> p m a s", m=4, a=2)[:, :, part, :]
                        other = o3 if part else bias[:, m0:m0 + 4].unsqueeze(2).to_broadcast([P, 4, CAP])
                        if b == h:
                            step.post(V.tensor_tensor(o3, src, other, ALU.add))
                        else:
                            step(V.tensor_tensor(o3, src, other, ALU.add))
                V.tensor_scalar(g_, g_, LIMIT, None, ALU.min).then_inc(ga_ready, 1)
                dve.wait_ge(ga_ready, 2 * e + (h + 1))
                step(V.tensor_scalar(u_, u_, LIMIT, -LIMIT, ALU.min, ALU.max))
                step(V.scalar_tensor_tensor(u_, u_, 1.0, g_, ALU.add, ALU.mult))
                dve.wait_ge(sg_ready, 2 * e + (h + 1))
                step(V.tensor_tensor(u_, u_, s_, ALU.mult))
                hi_lo(step, act32[:, 4 * h:4 * h + 4, :], as_[:, 4 * h:4 * h + 4, :]).then_inc(actT_ready, 1)

            def gate_up(step, e, ga_sem):
                bias = b1T[:, bass.ds(e, 1), :].rearrange("p a m -> p (a m)")
                V.tensor_tensor(ga.rearrange("p (m s) -> p m s", m=KD), bank[4][:, :].rearrange("p (m s) -> p m s", m=KD),
                                bias[:, 0:KD].unsqueeze(2).to_broadcast([P, KD, CAP]), ALU.add)
                step(V.tensor_tensor(ub.rearrange("p (m s) -> p m s", m=KD), bank[5][:, :].rearrange("p (m s) -> p m s", m=KD),
                                     bias[:, KD:2 * KD].unsqueeze(2).to_broadcast([P, KD, CAP]), ALU.add))
                V.tensor_scalar(ga, ga, LIMIT, None, ALU.min).then_inc(ga_sem, 1)
                step(V.tensor_scalar(ub, ub, LIMIT, -LIMIT, ALU.min, ALU.max))
                step(V.scalar_tensor_tensor(ub, ub, 1.0, ga, ALU.add, ALU.mult))

            place(0, 0).then_inc(p_ready, 1)
            dve.wait_ge(x_psum, 1)
            link(tokens_in(1))
            hi_lo(link, x32, xs).then_inc(xs_ready, 1)
            dve.wait_ge(b2_psum, 4)
            V.memset(ysb, 0.0).then_inc(ys_ready, 1)

            def expert(i, c, final):
                e = i * BODY + c
                step = chain(dve, moe_dve_step, e * LINKS)
                if not final:
                    place(e + 1, c + 1).then_inc(p_ready, 1)
                for n in range(NSPLIT, PRE):
                    lo_split(i, c, n)
                for h in range(2):
                    dve.wait_ge(t_psum, 4 * e + 2 * (h + 1))
                    activations(step, e, h)
                for n in range(PRE, SPE):
                    lo_split(i, c, n)
                if not final:
                    lo_split(i, c + 1, 0)
                    lo_split(i, c + 1, 1)
                    dve.wait_ge(x_psum, e + 2)
                    step(tokens_in(1))
                    hi_lo(step, x32, xs).then_inc(xs_ready, 1)
                    for n in range(2, NSPLIT):
                        lo_split(i, c + 1, n)
                    assert step.count[0] == LINKS

            def add_sums(added, b0):
                for q in range(4):
                    x_ = xres[:, q // 2, (q % 2) * 512:(q % 2 + 1) * 512]
                    V.tensor_tensor(x_, x_, bank[b0 + q][:, :], ALU.add).then_inc(added, 1)

            LINKS = 2 * 8 + 2
            with dve.Fori(0, NE // BODY - 1) as i:
                for c in range(BODY):
                    expert(i, c, False)
            for c in range(BODY - 1):
                expert(NE // BODY - 1, c, False)
            expert(NE // BODY - 1, BODY - 1, True)
            dve.wait_ge(c_psum, 4)
            add_sums(c_added, SUMS)
            dve.wait_ge(c_added, 4)

            OSTEPS = TT + 3
            dve.wait_ge(route_ready, 1)
            again = dve.value_load(over_i[0:1, 0:1], min_val=0, max_val=1)
            with dve.If(again > 0):
                with dve.Fori(0, NE) as e:
                    for r in range(NPASS - 1):
                        n = e * (NPASS - 1) + (r + 1)
                        link2 = chain(dve, over_step, e * (OSTEPS * (NPASS - 1)) + r * OSTEPS)
                        place(e, 0, (r + 1) * CAP).then_inc(over_place, 1)
                        dve.wait_ge(over_x, n)
                        tokens_in(6).then_inc(over_xr, 1)
                        dve.wait_ge(over_h, n)
                        gate_up(link2, e, over_ga)
                        dve.wait_ge(over_sg, n)
                        V.tensor_tensor(ub, ub, sg, ALU.mult).then_inc(over_act, 1)
                        dve.wait_ge(over_c, n)
                        add_sums(over_added, 0)
                        dve.wait_ge(over_added, n * 4)
                        assert link2.count[0] == OSTEPS
            V.tensor_copy(cnt[:, 0:1], cnt[:, 0:1]).then_inc(sum_done, 1)
            dve.wait_ge(fr_ready, 1)
            dve.wait_ge(gfin_in, 16)
            for t in range(TT):
                V.scalar_tensor_tensor(hN[:, t, :], xres[:, t, :], stat[:, 30 + t:31 + t], gfin, ALU.mult, ALU.mult).then_inc(fin_ready, 1)


_INS = ["x", "g_mix", "w_in", "conv_w", "conv_b", "dt_bias_f", "dt_bias_b", "a_log_f", "a_log_b", "d_skip",
        "g_ssm", "q_norm_g", "k_norm_g", "w_br_ssm", "w_br_attn", "w_out", "g_ffn", "w_router", "b_router",
        "w_mlp1", "b_mlp1", "w_mlp2", "b_mlp2", "g_final"]
_OUT = ((1, SEQ, D), "float32")


def kernel(**inputs):
    import numpy as _np
    import concourse.bacc as _bacc
    from concourse import mybir as _mybir
    from concourse.bass_utils import run_bass_kernel_spmd as _run

    nc = _bacc.Bacc("TRN2", target_bir_lowering=False, num_devices=1)
    arrays, args = {}, []
    for name in _INS:
        a = _np.ascontiguousarray(inputs[name])
        arrays[f"in_{name}_dram"] = a
        args.append(nc.dram_tensor(f"in_{name}_dram", a.shape, _mybir.dt.from_np(a.dtype), kind="ExternalInput").ap())
    c = shape_constants()
    arrays["shape_constants_dram"] = c
    args.append(nc.dram_tensor("shape_constants_dram", c.shape, _mybir.dt.from_np(c.dtype), kind="ExternalInput").ap())
    args.append(nc.dram_tensor("out_dram", _OUT[0], _mybir.dt.from_np(_np.dtype(_OUT[1])), kind="ExternalOutput").ap())
    encoder_layer(nc, *args)
    r = _run(nc, [arrays], core_ids=[0])
    return r.results[0]["out_dram"]
```
